# Optimizing a Trainium2 kernel written in Bass

```python
import math
import jax, jax.numpy as jnp
from jax import lax
import numpy as np

D_MODEL = 1024
BATCH = 1
SEQ = 256
DEPTH = 2

GRID_W = 64
CTX_LEN = 256
EPS = 1e-6
ROPE_BASE = 10000.0
ATTN_BLOCK = 128

A_HEADS = 4
A_DK = 128
A_DV = 128
A_WIDTH = A_HEADS * A_DK
HGRN_CHUNK = 16
B_HEADS = 4
B_HALF = 64
B_DV = 2 * B_HALF
B_WIDTH = B_HEADS * B_DV
EVEN_IN = 5 * A_WIDTH + 3 * B_WIDTH
C_HEADS = 16
C_KV_HEADS = 4
C_HEAD_DIM = 64
C_WINDOW = 128
ODD_IN = (C_HEADS + 2 * C_KV_HEADS) * C_HEAD_DIM
N_EXPERTS = 16
N_GROUPS = 4
EXPERTS_PER_GROUP = N_EXPERTS // N_GROUPS
TOP_K = 2
D_EXPERT = 1024
MOE_BLOCK = 128

N_EVEN = (DEPTH + 1) // 2
N_ODD = DEPTH // 2


F32 = jnp.float32

def rms_norm(x, g):
    xf = x.astype(F32)
    y = xf * lax.rsqrt(jnp.mean(xf * xf, axis=-1, keepdims=True) + EPS)
    return (y * g.astype(F32)).astype(x.dtype)

def axial_rope_tables(n_tokens, dim):
    n_rows = n_tokens // GRID_W
    row = jnp.repeat(jnp.arange(n_rows), GRID_W).astype(F32)
    col = jnp.tile(jnp.arange(GRID_W), n_rows).astype(F32)
    half = dim // 2
    inv = 1.0 / (ROPE_BASE ** (jnp.arange(0, half, 2, dtype=F32) / half))
    ar = row[:, None] * inv
    ac = col[:, None] * inv
    ang = jnp.concatenate([ar, ar, ac, ac], axis=-1)
    return jnp.cos(ang), jnp.sin(ang)

def _rotate_half(x):
    x1, x2 = jnp.split(x, 2, axis=-1)
    return jnp.concatenate([-x2, x1], axis=-1)

def apply_axial_rope(x, cos, sin):
    xr, xc = jnp.split(x, 2, axis=-1)
    xrot = jnp.concatenate([_rotate_half(xr), _rotate_half(xc)], axis=-1)
    return (x * cos[None, :, None, :] + xrot * sin[None, :, None, :]).astype(x.dtype)

def hgrn2_scan(q, k, v, logf, s0):
    b_, t_, h_, _ = q.shape
    dv = v.shape[-1]
    n = t_ // HGRN_CHUNK

    def chunks(a):
        return a.astype(F32).reshape(b_, n, HGRN_CHUNK, h_, a.shape[-1])

    qc, kc, vc, lf = chunks(q), chunks(k), chunks(v), chunks(logf)
    cum = jnp.cumsum(lf, axis=2)
    total = cum[:, :, -1]
    tri = jnp.tril(jnp.ones((HGRN_CHUNK, HGRN_CHUNK), dtype=bool))
    diff = cum[:, :, :, None] - cum[:, :, None, :]
    decay = jnp.exp(jnp.where(tri[:, :, None, None], diff, -jnp.inf))
    scores = jnp.einsum('bnthk,bntshk,bnshk->bnhts', qc, decay, kc)
    o_intra = jnp.einsum('bnhts,bnshv->bnthv', scores, vc)
    q_in = qc * jnp.exp(cum)
    k_out = kc * jnp.exp(total[:, :, None] - cum)

    def step(state, inp):
        q_n, k_n, v_n, tot_n = inp
        o_n = jnp.einsum('bthk,bhkv->bthv', q_n, state)
        state = state * jnp.exp(tot_n)[..., None] + jnp.einsum('bshk,bshv->bhkv', k_n, v_n)
        return state, o_n

    xs = (jnp.moveaxis(q_in, 1, 0), jnp.moveaxis(k_out, 1, 0), jnp.moveaxis(vc, 1, 0), jnp.moveaxis(total, 1, 0))
    s_final, o_inter = lax.scan(step, s0, xs)
    o = o_intra + jnp.moveaxis(o_inter, 0, 1)
    return o.reshape(b_, t_, h_, dv), s_final

def hgrn2_mixer(p, pc, lb, onorm_g):
    b_ = p.shape[0]

    def heads(a):
        return a.reshape(a.shape[0], a.shape[1], A_HEADS, -1)

    def split(a):
        q, ff, fb, i, g = jnp.split(a, 5, axis=-1)
        q = heads(jax.nn.silu(q.astype(F32)) * (A_DK ** -0.5))
        return q, heads(ff), heads(fb), heads(i), heads(g)

    ql, ffl, fbl, il, gl = split(p)
    qc, ffc, fbc, ic, gc = split(pc)
    lb = lb.astype(F32).reshape(2, A_HEADS, A_DK)

    def gates(f_raw, lb_d):
        f = lb_d + (1.0 - lb_d) * jax.nn.sigmoid(f_raw.astype(F32))
        return 1.0 - f, jnp.log(f)

    def direction(d, reverse, f_lat, f_ctx):
        fl = (lambda a: jnp.flip(a, axis=1)) if reverse else (lambda a: a)
        k_c, lf_c = gates(f_ctx, lb[d])
        k_l, lf_l = gates(f_lat, lb[d])
        s0 = jnp.zeros((b_, A_HEADS, A_DK, A_DV), F32)
        o_c, s_c = hgrn2_scan(fl(qc), fl(k_c), fl(ic), fl(lf_c), s0)
        o_l, _ = hgrn2_scan(fl(ql), fl(k_l), fl(il), fl(lf_l), s_c)
        return fl(o_c), fl(o_l)

    oc_f, ol_f = direction(0, False, ffl, ffc)
    oc_b, ol_b = direction(1, True, fbl, fbc)

    def finish(o, g):
        y = rms_norm(o, onorm_g) * jax.nn.silu(g.astype(F32))
        return y.reshape(y.shape[0], y.shape[1], A_WIDTH)

    return finish(ol_f + ol_b, gl), finish(oc_f + oc_b, gc)

def diff_attention_mixer(p, pc, lam_p, subln_g, lambda_init, rope, need_ctx):
    b_, t_, _ = p.shape

    def split_qkv(a):
        bb, tt = a.shape[0], a.shape[1]
        q, k, v = jnp.split(a, 3, axis=-1)
        return (q.reshape(bb, tt, B_HEADS, 2, B_HALF), k.reshape(bb, tt, B_HEADS, 2, B_HALF),
                v.reshape(bb, tt, B_HEADS, B_DV))

    q, k, v = split_qkv(p)
    qc, kc, vc = split_qkv(pc)
    cos, sin = rope
    q = apply_axial_rope(q.reshape(b_, t_, 2 * B_HEADS, B_HALF), cos, sin).reshape(b_, t_, B_HEADS, 2, B_HALF)
    k = apply_axial_rope(k.reshape(b_, t_, 2 * B_HEADS, B_HALF), cos, sin).reshape(b_, t_, B_HEADS, 2, B_HALF)
    lam_p = lam_p.astype(F32)
    lam = jnp.exp(jnp.sum(lam_p[0] * lam_p[1])) - jnp.exp(jnp.sum(lam_p[2] * lam_p[3])) + lambda_init
    scale = B_HALF ** -0.5

    def attend(qb, keys, vals):
        s = jnp.einsum('bqhmd,bkhmd->bhmqk', qb, keys).astype(F32) * scale
        pm = jax.nn.softmax(s, axis=-1)
        a = pm[:, :, 0] - lam * pm[:, :, 1]
        return jnp.einsum('bhqk,bkhv->bqhv', a, vals)

    keys = jnp.concatenate([kc, k], axis=1)
    vals = jnp.concatenate([vc, v], axis=1)
    nb = t_ // ATTN_BLOCK
    qb = jnp.moveaxis(q.reshape(b_, nb, ATTN_BLOCK, B_HEADS, 2, B_HALF), 1, 0)
    o = lax.map(lambda blk: attend(blk, keys, vals), qb)
    o = jnp.moveaxis(o, 0, 1).reshape(b_, t_, B_HEADS, B_DV)

    def finish(o):
        y = rms_norm(o, subln_g) * (1.0 - lambda_init)
        return y.reshape(y.shape[0], y.shape[1], B_WIDTH)

    y = finish(o)
    yc = finish(attend(qc, kc, vc)) if need_ctx else None
    return y, yc

def even_layer_mixer(h, hc, w_in, w_out, lb, onorm_g, lam_p, subln_g, lambda_init, rope, need_ctx):
    p = h @ w_in
    pc = hc @ w_in
    ya, yac = hgrn2_mixer(p[..., :5 * A_WIDTH], pc[..., :5 * A_WIDTH], lb, onorm_g)
    yb, ybc = diff_attention_mixer(p[..., 5 * A_WIDTH:], pc[..., 5 * A_WIDTH:], lam_p, subln_g, lambda_init, rope, need_ctx)
    y = jnp.concatenate([ya, yb], axis=-1) @ w_out
    yc = (jnp.concatenate([yac, ybc], axis=-1) @ w_out) if need_ctx else None
    return y, yc

def _sink_attend(qb, parts, sink_logit):
    scale = C_HEAD_DIM ** -0.5
    logits = []
    for kk, _, valid in parts:
        s = jnp.einsum('bqkgd,bskd->bkgqs', qb, kk).astype(F32) * scale
        if valid is not None:
            s = jnp.where(valid, s, -jnp.inf)
        logits.append(s)
    b_, nq = qb.shape[0], qb.shape[1]
    sink_col = jnp.broadcast_to(sink_logit[None, :, :, None, None], (b_, C_KV_HEADS, C_HEADS // C_KV_HEADS, nq, 1))
    pr = jax.nn.softmax(jnp.concatenate([sink_col] + logits, axis=-1), axis=-1)
    out = 0.0
    off = 1
    for (_, vv, _), s in zip(parts, logits):
        n = s.shape[-1]
        out = out + jnp.einsum('bkgqs,bskd->bqkgd', pr[..., off:off + n], vv)
        off += n
    return out

def odd_layer_mixer(h, hc, w_qkv, w_out, sink, rope, need_ctx):
    b_, t_, d_ = h.shape
    n_ctx = hc.shape[1]
    grp = C_HEADS // C_KV_HEADS
    q_cols = C_HEADS * C_HEAD_DIM
    p = h @ w_qkv
    q = p[..., :q_cols].reshape(b_, t_, C_HEADS, C_HEAD_DIM)
    k, v = jnp.split(p[..., q_cols:], 2, axis=-1)
    k = k.reshape(b_, t_, C_KV_HEADS, C_HEAD_DIM)
    v = v.reshape(b_, t_, C_KV_HEADS, C_HEAD_DIM)
    if need_ctx:
        pc = hc @ w_qkv
        qc = pc[..., :q_cols].reshape(b_, n_ctx, C_KV_HEADS, grp, C_HEAD_DIM)
        kvc = pc[..., q_cols:]
    else:
        kvc = hc @ w_qkv[:, q_cols:]
    kc, vc = jnp.split(kvc, 2, axis=-1)
    kc = kc.reshape(b_, n_ctx, C_KV_HEADS, C_HEAD_DIM)
    vc = vc.reshape(b_, n_ctx, C_KV_HEADS, C_HEAD_DIM)
    cos, sin = rope
    q = apply_axial_rope(q, cos, sin).reshape(b_, t_, C_KV_HEADS, grp, C_HEAD_DIM)
    k = apply_axial_rope(k, cos, sin)
    sink_logit = sink.astype(F32).reshape(C_KV_HEADS, grp)
    pad = ((0, 0), (C_WINDOW, C_WINDOW), (0, 0), (0, 0))
    kp = jnp.pad(k, pad)
    vp = jnp.pad(v, pad)
    span = ATTN_BLOCK + 2 * C_WINDOW
    nb = t_ // ATTN_BLOCK

    def block(n):
        start = n * ATTN_BLOCK
        qb = lax.dynamic_slice_in_dim(q, start, ATTN_BLOCK, axis=1)
        kb = lax.dynamic_slice_in_dim(kp, start, span, axis=1)
        vb = lax.dynamic_slice_in_dim(vp, start, span, axis=1)
        qpos = start + jnp.arange(ATTN_BLOCK)
        kpos = start - C_WINDOW + jnp.arange(span)
        valid = (jnp.abs(qpos[:, None] - kpos[None, :]) <= C_WINDOW) & (kpos[None, :] >= 0) & (kpos[None, :] < t_)
        return _sink_attend(qb, [(kc, vc, None), (kb, vb, valid)], sink_logit)

    o = lax.map(block, jnp.arange(nb))
    y = jnp.moveaxis(o, 0, 1).reshape(b_, t_, d_) @ w_out
    yc = None
    if need_ctx:
        yc = _sink_attend(qc, [(kc, vc, None)], sink_logit).reshape(b_, n_ctx, d_) @ w_out
    return y, yc

def routed_moe(h2d, router_w, router_b, w_gate, w_up, w_down):
    n_tok, d_ = h2d.shape
    aff = jax.nn.sigmoid(jnp.dot(h2d, router_w).astype(F32))
    sel = (aff + router_b.astype(F32)).reshape(n_tok, N_GROUPS, EXPERTS_PER_GROUP)
    group_score = jnp.sum(lax.top_k(sel, TOP_K)[0], axis=-1)
    grp = jnp.argmax(group_score, axis=-1)
    in_group = jnp.take_along_axis(sel, grp[:, None, None], axis=1)[:, 0]
    _, local = lax.top_k(in_group, TOP_K)
    expert = (grp[:, None] * EXPERTS_PER_GROUP + local).astype(jnp.int32)
    wts = jnp.take_along_axis(aff, expert, axis=1)
    wts = wts / jnp.sum(wts, axis=-1, keepdims=True)
    n_assign = n_tok * TOP_K
    n_blocks = -(-n_assign // MOE_BLOCK) + N_EXPERTS
    n_rows = n_blocks * MOE_BLOCK
    flat_e = expert.reshape(-1)
    flat_t = jnp.repeat(jnp.arange(n_tok, dtype=jnp.int32), TOP_K)
    flat_w = wts.reshape(-1)
    order = jnp.argsort(flat_e)
    e_sorted = flat_e[order]
    counts = jnp.bincount(flat_e, length=N_EXPERTS)
    padded = (counts + MOE_BLOCK - 1) // MOE_BLOCK * MOE_BLOCK
    pad_end = jnp.cumsum(padded)
    pad_start = pad_end - padded
    start = jnp.cumsum(counts) - counts
    dest = pad_start[e_sorted] + jnp.arange(n_assign) - start[e_sorted]
    row_tok = jnp.full((n_rows,), n_tok, jnp.int32).at[dest].set(flat_t[order])
    row_w = jnp.zeros((n_rows,), F32).at[dest].set(flat_w[order])
    block_start = jnp.arange(n_blocks) * MOE_BLOCK
    block_e = jnp.minimum(jnp.sum(pad_end[None, :] <= block_start[:, None], axis=1), N_EXPERTS - 1)
    x_pad = jnp.concatenate([h2d, jnp.zeros((1, d_), h2d.dtype)], axis=0)
    xb = x_pad[row_tok].reshape(n_blocks, MOE_BLOCK, d_)

    def expert_block(args):
        xblk, e = args
        hid = jax.nn.silu(xblk @ w_gate[e]) * (xblk @ w_up[e])
        return hid @ w_down[e]

    yb = lax.map(expert_block, (xb, block_e)).reshape(n_rows, d_)
    out = jnp.zeros((n_tok + 1, d_), F32).at[row_tok].add(yb * row_w[:, None])
    return out[:n_tok]

def first_inputs(seed: int = 0) -> dict:
    key = jax.random.key(seed)
    ks = jax.random.split(key, 24)
    d = D_MODEL
    nrm = jax.random.normal
    return {
        'x': nrm(ks[0], (BATCH, SEQ, d), F32),
        'c': nrm(ks[1], (BATCH, d), F32),
        'ctx': nrm(ks[2], (BATCH, CTX_LEN, d), F32),
        'c_ctx': nrm(ks[3], (d,), F32),
        'ada_w': nrm(ks[4], (DEPTH, d, 6 * d), F32) * (0.5 * d ** -0.5),
        'ada_b': nrm(ks[5], (DEPTH, 6 * d), F32) * 0.02,
        'norm_mix_g': 1.0 + 0.02 * nrm(ks[6], (DEPTH, d), F32),
        'norm_ffn_g': 1.0 + 0.02 * nrm(ks[7], (DEPTH, d), F32),
        'even_w_in': nrm(ks[8], (N_EVEN, d, EVEN_IN), F32) * d ** -0.5,
        'even_w_out': nrm(ks[9], (N_EVEN, A_WIDTH + B_WIDTH, d), F32) * (A_WIDTH + B_WIDTH) ** -0.5,
        'hgrn_lb_logits': 0.1 * nrm(ks[10], (DEPTH + 1, 2, A_WIDTH), F32),
        'hgrn_onorm_g': 1.0 + 0.02 * nrm(ks[11], (N_EVEN, A_DV), F32),
        'diff_lambda': 0.1 * nrm(ks[12], (N_EVEN, 4, B_HALF), F32),
        'diff_subln_g': 1.0 + 0.02 * nrm(ks[13], (N_EVEN, B_DV), F32),
        'odd_w_qkv': nrm(ks[14], (N_ODD, d, ODD_IN), F32) * d ** -0.5,
        'odd_w_out': nrm(ks[15], (N_ODD, C_HEADS * C_HEAD_DIM, d), F32) * (C_HEADS * C_HEAD_DIM) ** -0.5,
        'swa_sink': 0.5 * nrm(ks[16], (N_ODD, C_HEADS), F32),
        'router_w': nrm(ks[17], (d, N_EXPERTS), F32) * d ** -0.5,
        'router_b': 0.01 * nrm(ks[18], (N_EXPERTS,), F32),
        'moe_w_gate': nrm(ks[19], (DEPTH, N_EXPERTS, d, D_EXPERT), F32) * d ** -0.5,
        'moe_w_up': nrm(ks[20], (DEPTH, N_EXPERTS, d, D_EXPERT), F32) * d ** -0.5,
        'moe_w_down': nrm(ks[21], (DEPTH, N_EXPERTS, D_EXPERT, d), F32) * D_EXPERT ** -0.5,
        'final_norm_g': 1.0 + 0.02 * nrm(ks[22], (d,), F32),
    }

def first_block(x, c, ctx, c_ctx, ada_w, ada_b, norm_mix_g, norm_ffn_g, even_w_in, even_w_out,
              hgrn_lb_logits, hgrn_onorm_g, diff_lambda, diff_subln_g, odd_w_qkv, odd_w_out, swa_sink,
              router_w, router_b, moe_w_gate, moe_w_up, moe_w_down, final_norm_g):
    b_, t_, d_ = x.shape
    n_ctx = ctx.shape[1]
    rope_b = axial_rope_tables(t_, B_HALF)
    rope_c = axial_rope_tables(t_, C_HEAD_DIM)
    lower_bounds = jnp.cumsum(jax.nn.softmax(hgrn_lb_logits.astype(F32), axis=0), axis=0)
    xc = ctx
    for layer in range(DEPTH):
        last = layer == DEPTH - 1
        w_ada, b_ada = ada_w[layer], ada_b[layer]
        mod = (jax.nn.silu(c) @ w_ada + b_ada)[:, None, :]
        mod_c = (jax.nn.silu(c_ctx) @ w_ada + b_ada)[None, None, :]
        sh1, sc1, g1, sh2, sc2, g2 = jnp.split(mod, 6, axis=-1)
        csh1, csc1, cg1, csh2, csc2, cg2 = jnp.split(mod_c, 6, axis=-1)
        h = rms_norm(x, norm_mix_g[layer]) * (1.0 + sc1) + sh1
        hc = rms_norm(xc, norm_mix_g[layer]) * (1.0 + csc1) + csh1
        if layer % 2 == 0:
            j = layer // 2
            lambda_init = 0.8 - 0.6 * math.exp(-0.3 * layer)
            y, yc = even_layer_mixer(h, hc, even_w_in[j], even_w_out[j], lower_bounds[layer], hgrn_onorm_g[j],
                                     diff_lambda[j], diff_subln_g[j], lambda_init, rope_b, not last)
        else:
            j = layer // 2
            y, yc = odd_layer_mixer(h, hc, odd_w_qkv[j], odd_w_out[j], swa_sink[j], rope_c, not last)
        x = x + g1 * y
        h2 = rms_norm(x, norm_ffn_g[layer]) * (1.0 + sc2) + sh2
        if last:
            f = routed_moe(h2.reshape(-1, d_), router_w, router_b,
                           moe_w_gate[layer], moe_w_up[layer], moe_w_down[layer])
            x = x + g2 * f.reshape(b_, t_, d_)
        else:
            xc = xc + cg1 * yc
            hc2 = rms_norm(xc, norm_ffn_g[layer]) * (1.0 + csc2) + csh2
            tokens = jnp.concatenate([h2.reshape(-1, d_), hc2.reshape(-1, d_)], axis=0)
            f = routed_moe(tokens, router_w, router_b, moe_w_gate[layer], moe_w_up[layer], moe_w_down[layer])
            x = x + g2 * f[:b_ * t_].reshape(b_, t_, d_)
            xc = xc + cg2 * f[b_ * t_:].reshape(b_, n_ctx, d_)
    return rms_norm(x, final_norm_g)


DEPTH_2 = 1


F_GROUP_W = 128
F_WIDTH = D_MODEL // 2
F_GROUPS = F_WIDTH // F_GROUP_W

D_INNER = (3 * D_MODEL) // 2
SSD_HEAD_DIM = 64
SSD_HEADS = D_INNER // SSD_HEAD_DIM
SSD_GROUPS = 4
D_STATE = 128
CONV_W = 3
CHUNK = 128
CONV_CH = D_INNER + 2 * SSD_GROUPS * D_STATE

N_BRANCH = 2
P_IN = F_WIDTH + D_INNER + CONV_CH + 2 * SSD_HEADS + N_BRANCH * D_MODEL

EC_FACTOR = 2
EXPERT_FF = D_MODEL

N_MOD = 6
RMS_EPS = 1e-6


def rms_norm_2(x, w):
    xf = x.astype(jnp.float32)
    y = xf * lax.rsqrt(jnp.mean(xf * xf, axis=-1, keepdims=True) + RMS_EPS)
    return (y * w.astype(jnp.float32)).astype(x.dtype)

def modulate(x, gain, shift, scale):
    return rms_norm_2(x, gain) * (1 + scale) + shift

def centred_dwconv(u, w, b, n_rows):
    bn, length, ch = u.shape
    row_len = length // n_rows
    r = u.reshape(bn, n_rows, row_len, ch)
    pad = CONV_W // 2
    rp = jnp.pad(r, ((0, 0), (0, 0), (pad, pad), (0, 0)))
    out = sum(rp[:, :, k:k + row_len] * w[k] for k in range(CONV_W)) + b
    return out.reshape(bn, length, ch)

def ssd_chunked(xh, dt, a, bm, cm, h0):
    bn, length, nh, hp = xh.shape
    g, n = bm.shape[2], bm.shape[3]
    hg = nh // g
    nc = length // CHUNK
    x = xh.reshape(bn, nc, CHUNK, g, hg, hp)
    dtc = dt.reshape(bn, nc, CHUNK, g, hg)
    bc = bm.reshape(bn, nc, CHUNK, g, n)
    cc = cm.reshape(bn, nc, CHUNK, g, n)
    acum = jnp.cumsum(dtc * a.reshape(g, hg), axis=2)
    xdt = x * dtc[..., None]
    seg = acum[:, :, :, None] - acum[:, :, None, :]
    lower = jnp.tril(jnp.ones((CHUNK, CHUNK), dtype=bool))[:, :, None, None]
    decay = jnp.where(lower, jnp.exp(jnp.where(lower, seg, 0.0)), 0.0)
    cb = jnp.einsum('bctgn,bcsgn->bctsg', cc, bc)
    y_diag = jnp.einsum('bctsg,bctsgh,bcsghp->bctghp', cb, decay, xdt)
    decay_end = jnp.exp(acum[:, :, -1:] - acum)
    states = jnp.einsum('bcsgn,bcsgh,bcsghp->bcghpn', bc, decay_end, xdt)
    chunk_decay = jnp.exp(acum[:, :, -1])

    def step(h, inp):
        dec, st = inp
        return dec[..., None, None] * h + st, h

    h_final, h_prev = lax.scan(step, h0, (jnp.moveaxis(chunk_decay, 1, 0), jnp.moveaxis(states, 1, 0)))
    h_prev = jnp.moveaxis(h_prev, 0, 1)
    y_off = jnp.einsum('bctgn,bctgh,bcghpn->bctghp', cc, jnp.exp(acum), h_prev)
    y = (y_diag + y_off).reshape(bn, length, nh, hp)
    return y, h_final

def bidir_ssd(xh, dt_raw, bm, cm, dt_bias, a_log, h0_f, h0_b):
    dt_f = jax.nn.softplus(dt_raw[:, :, 0] + dt_bias[0])
    dt_b = jax.nn.softplus(dt_raw[:, :, 1] + dt_bias[1])
    a_f = -jnp.exp(a_log[0].astype(jnp.float32))
    a_b = -jnp.exp(a_log[1].astype(jnp.float32))
    y_f, h_f = ssd_chunked(xh, dt_f, a_f, bm, cm, h0_f)
    flip = lambda t: jnp.flip(t, axis=1)
    y_b, h_b = ssd_chunked(flip(xh), flip(dt_b), a_b, flip(bm), flip(cm), h0_b)
    return y_f + flip(y_b), h_f, h_b

def token_mixer(h, n_rows, h0_f, h0_b, w_in, conv_w, conv_b, dt_bias, a_log, d_skip, ssd_norm,
                w_fourier, w_ssd_out, b_gate, w_out):
    bn, length, _ = h.shape
    proj = h @ w_in
    i1 = F_WIDTH
    i2 = i1 + D_INNER
    i3 = i2 + CONV_CH
    i4 = i3 + 2 * SSD_HEADS
    u_f, z, xbc, dt_raw, gate_logits = jnp.split(proj, [i1, i2, i3, i4], axis=-1)
    uf = u_f.reshape(bn, length, F_GROUPS, F_GROUP_W).astype(jnp.float32)
    f = jnp.fft.fft2(uf, axes=(1, 3), norm='ortho').real.astype(h.dtype).reshape(bn, length, F_WIDTH)
    f_branch = f @ w_fourier
    xbc = jax.nn.silu(centred_dwconv(xbc, conv_w, conv_b, n_rows))
    xs, bm, cm = jnp.split(xbc, [D_INNER, D_INNER + SSD_GROUPS * D_STATE], axis=-1)
    xh = xs.reshape(bn, length, SSD_HEADS, SSD_HEAD_DIM).astype(jnp.float32)
    bm = bm.reshape(bn, length, SSD_GROUPS, D_STATE).astype(jnp.float32)
    cm = cm.reshape(bn, length, SSD_GROUPS, D_STATE).astype(jnp.float32)
    dt_raw = dt_raw.reshape(bn, length, 2, SSD_HEADS).astype(jnp.float32)
    y, h_f, h_b = bidir_ssd(xh, dt_raw, bm, cm, dt_bias, a_log, h0_f, h0_b)
    y = y + d_skip[:, None].astype(jnp.float32) * xh
    y = y.reshape(bn, length, D_INNER).astype(h.dtype)
    y = rms_norm_2(y * jax.nn.silu(z), ssd_norm)
    s_branch = y @ w_ssd_out
    g = jax.nn.sigmoid(gate_logits.reshape(bn, length, N_BRANCH, D_MODEL) + b_gate)
    merged = g[:, :, 0] * f_branch + g[:, :, 1] * s_branch
    return merged @ w_out, h_f, h_b

def expert_choice_ffn(h, w_router, w_e_gate, w_e_up, w_e_down):
    bn, length, d = h.shape
    cap = EC_FACTOR * length // N_EXPERTS
    aff = jax.nn.softmax((h @ w_router).astype(jnp.float32), axis=-1)
    top_aff, top_idx = lax.top_k(jnp.swapaxes(aff, 1, 2), cap)
    xe = jax.vmap(lambda hb, ib: hb[ib])(h, top_idx)
    hid = jax.nn.silu(jnp.einsum('becd,edf->becf', xe, w_e_gate)) * jnp.einsum('becd,edf->becf', xe, w_e_up)
    ye = jnp.einsum('becf,efd->becd', hid, w_e_down) * top_aff[..., None].astype(h.dtype)
    return jax.vmap(lambda ib, yb: jnp.zeros((length, d), yb.dtype).at[ib.reshape(-1)].add(yb.reshape(-1, d)))(top_idx, ye)

def second_inputs(seed: int = 0) -> dict:
    key = jax.random.key(seed)
    ks = jax.random.split(key, 32)
    nrm = lambda k, shape, s: jax.random.normal(k, shape, jnp.float32) * s
    L = DEPTH_2
    dt0 = jnp.exp(jax.random.uniform(ks[12], (L, 2, SSD_HEADS), jnp.float32, np.log(1e-3), np.log(1e-1)))
    return {
        'x': nrm(ks[0], (BATCH, SEQ, D_MODEL), 1.0),
        'c': nrm(ks[1], (BATCH, D_MODEL), 1.0),
        'ctx': nrm(ks[2], (BATCH, CTX_LEN, D_MODEL), 1.0),
        'c_ctx': nrm(ks[3], (D_MODEL,), 1.0),
        'w_mod': nrm(ks[4], (L, D_MODEL, N_MOD * D_MODEL), 0.5 * D_MODEL ** -0.5),
        'b_mod': nrm(ks[5], (L, N_MOD * D_MODEL), 0.02),
        'norm_mix_pre': 1.0 + nrm(ks[6], (L, D_MODEL), 0.05),
        'norm_mix_post': 1.0 + nrm(ks[7], (L, D_MODEL), 0.05),
        'norm_ffn_pre': 1.0 + nrm(ks[8], (L, D_MODEL), 0.05),
        'norm_ffn_post': 1.0 + nrm(ks[9], (L, D_MODEL), 0.05),
        'w_in': nrm(ks[10], (L, D_MODEL, P_IN), D_MODEL ** -0.5),
        'conv_w': nrm(ks[11], (L, CONV_W, CONV_CH), CONV_W ** -0.5),
        'conv_b': nrm(ks[13], (L, CONV_CH), 0.02),
        'dt_bias': dt0 + jnp.log(-jnp.expm1(-dt0)),
        'a_log': jnp.log(jax.random.uniform(ks[14], (L, 2, SSD_HEADS), jnp.float32, 1.0, 16.0)),
        'd_skip': 1.0 + nrm(ks[15], (L, SSD_HEADS), 0.1),
        'ssd_norm': 1.0 + nrm(ks[16], (L, D_INNER), 0.05),
        'w_fourier': nrm(ks[17], (L, F_WIDTH, D_MODEL), F_WIDTH ** -0.5),
        'w_ssd_out': nrm(ks[18], (L, D_INNER, D_MODEL), D_INNER ** -0.5),
        'b_gate': nrm(ks[19], (L, N_BRANCH, D_MODEL), 0.1),
        'w_out': nrm(ks[20], (L, D_MODEL, D_MODEL), D_MODEL ** -0.5),
        'w_router': nrm(ks[21], (L, D_MODEL, N_EXPERTS), D_MODEL ** -0.5),
        'w_e_gate': nrm(ks[22], (L, N_EXPERTS, D_MODEL, EXPERT_FF), D_MODEL ** -0.5),
        'w_e_up': nrm(ks[23], (L, N_EXPERTS, D_MODEL, EXPERT_FF), D_MODEL ** -0.5),
        'w_e_down': nrm(ks[24], (L, N_EXPERTS, EXPERT_FF, D_MODEL), EXPERT_FF ** -0.5),
    }

def second_block(x, c, ctx, c_ctx, w_mod, b_mod, norm_mix_pre, norm_mix_post, norm_ffn_pre, norm_ffn_post,
              w_in, conv_w, conv_b, dt_bias, a_log, d_skip, ssd_norm, w_fourier, w_ssd_out, b_gate, w_out,
              w_router, w_e_gate, w_e_up, w_e_down):
    bn, length, d = x.shape
    rows = length // GRID_W
    hx, hc = x, ctx
    for l in range(DEPTH_2):
        mod_x = (jax.nn.silu(c) @ w_mod[l] + b_mod[l]).reshape(bn, N_MOD, 1, d)
        mod_c = (jax.nn.silu(c_ctx) @ w_mod[l] + b_mod[l]).reshape(N_MOD, d)
        sh1, sc1, g1, sh2, sc2, g2 = [mod_x[:, i] for i in range(N_MOD)]
        csh1, csc1, cg1, csh2, csc2, cg2 = [mod_c[i] for i in range(N_MOD)]
        mix_w = (w_in[l], conv_w[l], conv_b[l], dt_bias[l], a_log[l], d_skip[l], ssd_norm[l],
                 w_fourier[l], w_ssd_out[l], b_gate[l], w_out[l])
        h0 = jnp.zeros((bn, SSD_GROUPS, SSD_HEADS // SSD_GROUPS, SSD_HEAD_DIM, D_STATE), jnp.float32)
        mix_c, hf_c, hb_c = token_mixer(modulate(hc, norm_mix_pre[l], csh1, csc1), 1, h0, h0, *mix_w)
        mix_x, _, _ = token_mixer(modulate(hx, norm_mix_pre[l], sh1, sc1), rows, hf_c, hb_c, *mix_w)
        hx = hx + g1 * rms_norm_2(mix_x, norm_mix_post[l])
        ffn_x = expert_choice_ffn(modulate(hx, norm_ffn_pre[l], sh2, sc2), w_router[l], w_e_gate[l], w_e_up[l], w_e_down[l])
        hx = hx + g2 * rms_norm_2(ffn_x, norm_ffn_post[l])
        if l + 1 < DEPTH_2:
            hc = hc + cg1 * rms_norm_2(mix_c, norm_mix_post[l])
            ffn_c = expert_choice_ffn(modulate(hc, norm_ffn_pre[l], csh2, csc2), w_router[l], w_e_gate[l], w_e_up[l], w_e_down[l])
            hc = hc + cg2 * rms_norm_2(ffn_c, norm_ffn_post[l])
    return hx


def setup_inputs(seed=0):
    out = dict(first_inputs(seed))
    for name, value in second_inputs(seed + 1).items():
        if name != "x":
            out[name + "_2"] = value
    return out


def reference(
    x, c, ctx, c_ctx, ada_w, ada_b, norm_mix_g, norm_ffn_g, even_w_in, even_w_out,
    hgrn_lb_logits, hgrn_onorm_g, diff_lambda, diff_subln_g, odd_w_qkv, odd_w_out, swa_sink,
    router_w, router_b, moe_w_gate, moe_w_up, moe_w_down, final_norm_g, c_2, ctx_2, c_ctx_2,
    w_mod_2, b_mod_2, norm_mix_pre_2, norm_mix_post_2, norm_ffn_pre_2, norm_ffn_post_2, w_in_2,
    conv_w_2, conv_b_2, dt_bias_2, a_log_2, d_skip_2, ssd_norm_2, w_fourier_2, w_ssd_out_2,
    b_gate_2, w_out_2, w_router_2, w_e_gate_2, w_e_up_2, w_e_down_2,
):
    x = first_block(
        x, c, ctx, c_ctx, ada_w, ada_b, norm_mix_g, norm_ffn_g, even_w_in, even_w_out,
        hgrn_lb_logits, hgrn_onorm_g, diff_lambda, diff_subln_g, odd_w_qkv, odd_w_out, swa_sink,
        router_w, router_b, moe_w_gate, moe_w_up, moe_w_down, final_norm_g,
    )
    return second_block(
        x, c_2, ctx_2, c_ctx_2, w_mod_2, b_mod_2, norm_mix_pre_2, norm_mix_post_2,
        norm_ffn_pre_2, norm_ffn_post_2, w_in_2, conv_w_2, conv_b_2, dt_bias_2, a_log_2,
        d_skip_2, ssd_norm_2, w_fourier_2, w_ssd_out_2, b_gate_2, w_out_2, w_router_2,
        w_e_gate_2, w_e_up_2, w_e_down_2,
    )


_drawn_inputs = setup_inputs


def setup_inputs(seed=0):
    import zlib

    import numpy as np

    out = dict(_drawn_inputs(seed))
    spreads = {}
    factors = {'hgrn_lb_logits': 3.872,
     'hgrn_onorm_g': 3.215,
     'swa_sink': 8.0,
     'norm_ffn_post_2': 4.029,
     'd_skip_2': 2.953}
    for name, (base, spread) in spreads.items():
        noise = np.random.default_rng([zlib.crc32(name.encode()), seed]).standard_normal(out[name].shape)
        drawn = base * np.exp(spread * noise) if base else spread * noise
        out[name] = __import__('jax').numpy.asarray(drawn.astype(out[name].dtype))
    for name, factor in factors.items():
        out[name] = (out[name] * factor).astype(out[name].dtype)
    return out
```

```python
import math
from contextlib import ExitStack

import numpy as np
import concourse.bass as bass
from concourse import mybir

P = 128
D = 1024
NS = 5
SLOT = 8 * 512
F32 = mybir.dt.float32
U32 = mybir.dt.uint32
I32 = mybir.dt.int32
ALU = mybir.AluOpType
ACT = mybir.ActivationFunctionType
AX = mybir.AxisListType
EPS = 1e-6
BIG = 1e30
XROWS = 23 * P

C_ID, C_LE, C_LT, C_GE, C_COS, C_SIN, C_ROT, C_NF, C_NB = 0, 128, 256, 384, 512, 768, 1024, 1152, 1280
C_IOTA, C_ONE, C_EX, C_GW, C_REP = 1408, 1440, 1441, 1457, 1461
C_KEEP = 1473
C_LEV = 1480
C_SWA = C_LEV + 15 * 128
C_DL = C_SWA + 1024
C_DW = C_DL + 1024
C_END = C_DW + 256


def constants():
    c = np.zeros((P, C_END), np.float32)
    i = np.arange(P)
    c[:, C_ID:C_ID + P] = np.eye(P)
    c[:, C_LE:C_LE + P] = i[:, None] <= i[None]
    c[:, C_LT:C_LT + P] = i[:, None] < i[None]
    c[:, C_GE:C_GE + P] = i[:, None] >= i[None]
    c[:, C_NF:C_NF + P] = np.where(i[:, None] <= i[None], 0, -BIG)
    c[:, C_NB:C_NB + P] = np.where(i[:, None] >= i[None], 0, -BIG)
    t = np.arange(256)
    inv = (1.0 / (np.float32(10000.0) ** (np.arange(0, 32, 2, dtype=np.float32) / np.float32(32)))).astype(np.float32)
    ar = (t // 64).astype(np.float32)[:, None] * inv
    ac = (t % 64).astype(np.float32)[:, None] * inv
    ang = np.concatenate([ar, ar, ac, ac], axis=-1).astype(np.float32)
    c[:, C_COS:C_COS + 256] = np.tile(np.cos(ang).T, (2, 1))
    c[:, C_SIN:C_SIN + 256] = np.tile(np.sin(ang).T, (2, 1))
    r = np.zeros((P, P), np.float32)
    for b in range(0, P, 32):
        for j in range(16):
            r[b + j, b + 16 + j] = -1
            r[b + 16 + j, b + j] = 1
    c[:, C_ROT:C_ROT + P] = r.T
    c[:, C_IOTA:C_IOTA + 32] = np.arange(32)
    c[[2, 3, 8, 9], C_ONE] = 1
    c[:, C_EX:C_EX + 16] = np.arange(16)
    c[:, C_GW:C_GW + 4] = [4, 3, 2, 1]
    for j in range(6):
        c[j, C_REP + 2 * j:C_REP + 2 * j + 2] = 1
    lev = []
    for b in (64, 32, 16, 8, 4, 2, 1):
        lev.append((i[:, None] // (2 * b) == i[None] // (2 * b)) & (i[:, None] // b % 2 == 0) & (i[None] // b % 2 == 1))
    allm = lev + [m.T for m in lev] + [np.eye(P, dtype=bool)]
    for n, m in enumerate(allm):
        c[:, C_LEV + n * P:C_LEV + (n + 1) * P] = m
    for q in range(2):
        ok = np.abs((q * P + i)[:, None] - t[None]) <= 128
        c[:, C_SWA + q * 512:C_SWA + q * 512 + 256] = np.where(ok, 0, -BIG)
    ll = 2 * np.pi * (np.outer(t, t) % 256) / 256
    s = 1 / math.sqrt(256 * 128)
    for q in range(2):
        c[:, C_DL + q * 512:C_DL + q * 512 + 256] = (np.cos(ll) * s)[q * P:(q + 1) * P]
        c[:, C_DL + q * 512 + 256:C_DL + (q + 1) * 512] = (np.sin(ll) * s)[q * P:(q + 1) * P]
    lw = 2 * np.pi * (np.outer(i, i) % 128) / 128
    c[:, C_DW:C_DW + P] = np.cos(lw)
    c[:, C_DW + P:C_DW + 2 * P] = -np.sin(lw)
    return c


class Lane:

    def __init__(self, eng, sem, own):
        self.eng, self.sem, self.n, self.own, self.met = eng, sem, 0, own, {}

    def after(self, *marks):
        for m in marks + ((self.mark(),) if self.own and self.n else ()):
            if m is not None and self.met.get(m[0], 0) < m[2]:
                self.eng.wait_ge(m[1], m[2])
                self.met[m[0]] = m[2]
        return self.eng

    def done(self, ins):
        ins.then_inc(self.sem, 1)
        self.n += 1
        return self.mark()

    def mark(self):
        return (id(self.sem), self.sem, self.n)


class Wire:

    def __init__(self, sem):
        self.sem, self.n = sem, 0

    def sent(self, ins):
        ins.then_inc(self.sem, 16)
        self.n += 16
        return (id(self.sem), self.sem, self.n)


class Banks:

    def __init__(self, ap, lane):
        self.ap, self.lane, self.at, self.freed = ap, lane, 0, [()] * 8

    def take(self, n=1):
        at = -(-self.at // n) * n % 8
        for _ in range(8 // n):
            if all(self.freed[b] is not None for b in range(at, at + n)):
                break
            at = (at + n) % 8
        self.at = (at + n) % 8
        for b in range(at, at + n):
            assert self.freed[b] is not None, "bank in use"
            self.lane.after(*self.freed[b])
            self.freed[b] = None
        return Bank(self, at, n)


class Bank:
    def __init__(self, banks, at, n):
        self.banks, self.at, self.n = banks, at, n
        self.ap = banks.ap[:, at * 512:(at + n) * 512]

    def free(self, *marks):
        for b in range(self.at, self.at + self.n):
            self.banks.freed[b] = marks


class Ring:

    def __init__(self, ap, lane, sems, plan):
        self.ap, self.lane, self.plan = ap, lane, plan
        self.wires = [Wire(s) for s in sems]
        self.marks, self.at = [], 0
        for n in range(NS):
            self.send(n)

    def send(self, n, *marks):
        if n >= len(self.plan):
            return
        _, src, k, cols, gate = self.plan[n]
        dst = self.ap[:, n % NS, :].rearrange("p (c n) -> p c n", c=8)[:, 0:k, 0:cols]
        self.lane.after(*marks)
        if gate is not None:
            src = gate()
        self.marks.append(self.wires[n % NS].sent(self.lane.eng.dma_start(dst, src)))

    def take(self, key):
        n = self.at
        assert self.plan[n][0] == key, (self.plan[n][0], key)
        self.at += 1
        return self.ap[:, n % NS, :].rearrange("p (c n) -> p c n", c=8), self.marks[n], n

    def free(self, n, mark):
        self.send(n + NS, mark)


def program(nc, I, out, upto=3):
    ctx = ExitStack()
    sb = lambda name, shape, dt=F32: ctx.enter_context(nc.sbuf_tensor(name, shape, dt))
    sem = lambda name: ctx.enter_context(nc.semaphore(name))
    pe = Lane(nc.tensor, sem("s_pe"), False)
    dve = Lane(nc.vector, sem("s_dve"), True)
    act = Lane(nc.scalar, sem("s_act"), True)
    pool = Lane(nc.gpsimd, sem("s_pool"), True)
    sp = Lane(nc.sync, sem("s_sp"), False)

    ringt = sb("ring", [P, NS, SLOT])
    X = sb("X", [P, 4, D])
    MOD = sb("MOD", [12, D])
    KC = sb("KC", [P, C_KEEP])
    ones = sb("ones", [P, P])
    CT = sb("CT", [P, 32])
    CP = sb("CP", [P, 2, 8, 6, 12])
    SM = sb("SM", [P, 2304])
    RT = sb("RT", [P, 8, 16])
    DST = sb("DST", [P, 8], U32)
    OE = sb("OE", [1, 16], I32)
    ar_words = 22300
    AR = sb("AR", [P, ar_words])
    PSt = ctx.enter_context(nc.psum_tensor("PS", [P, 4096], F32))
    ps = Banks(PSt[:, :], pe)
    XP = nc.dram_tensor("XP", [XROWS, D], F32).ap()
    YP = nc.dram_tensor("YP", [XROWS, D], F32).ap()

    ident = KC[:, C_ID:C_ID + P]
    at = [0]

    def take(n):
        a = at[0]
        at[0] += n
        assert at[0] <= ar_words, at[0]
        return AR[:, a:a + n]

    smat = [0]

    def small(n):
        a = smat[0]
        smat[0] += n
        assert smat[0] <= 2304, smat[0]
        return SM[:, a:a + n]

    def fence(*more):
        marks = [x.mark() for x in (pe, dve, act, pool) if x.n] + list(more)
        for x in (pe, dve, act, pool):
            x.after(*marks)
        return marks

    def mm(o, l, r, start, stop, **kw):
        return nc.tensor.matmul(o, l, r, start=start, stop=stop, **kw)

    flip = [0]

    def evac(dst, src, *marks):
        flip[0] ^= 1
        if flip[0]:
            return dve.done(dve.after(*marks).tensor_copy(dst, src))
        return act.done(act.after(*marks).copy(dst, src))

    def cols(w, n, k0=0, k=8, width=512):
        return w[k0:k0 + k * P, n:n + width].rearrange("(c p) n -> p c n", p=P)

    plan = []

    def add(key, src, k=8, width=512, gate=None):
        plan.append((key, src, k, width, gate))

    ada, win, wo = I["ada_w"], I["even_w_in"][0], I["even_w_out"][0]
    moe = {"g": I["moe_w_gate"], "u": I["moe_w_up"], "d": I["moe_w_down"]}
    over = {}

    def add_ada(tag, w):
        for n in range(12):
            add((tag, n), cols(w, 512 * n))

    def add_moe(layer, nover):
        for e in range(16):
            for m, h in (("g", 0), ("u", 0), ("g", 1), ("u", 1), ("d", 0), ("d", 1)):
                add((layer, e, m, h), cols(moe[m][layer, e], 512 * h))
        for b in range(nover):
            for m, h in (("g", 0), ("u", 0), ("g", 1), ("u", 1), ("d", 0), ("d", 1)):
                def gate(m=m, h=h, b=b):
                    if (m, h) == ("g", 0):
                        sp.after(*over["mark"])
                        over["e"] = nc.sync.value_load(OE[0:1, b:b + 1], min_val=0, max_val=15)
                    v = moe[m][layer].rearrange("e (c p) n -> p e c n", p=P)
                    return v[:, bass.ds(over["e"], 1), :, 512 * h:512 * h + 512]
                add((layer, 16 + b, m, h), None, gate=gate)

    add_ada("ada0", ada[0])
    for n in range(8):
        add(("in", n), cols(win, 512 * n))
    for n in range(2):
        add(("wo", n), cols(wo, 512 * n))
    add_moe(0, 7)
    cut = {1: len(plan)}
    add_ada("ada1", ada[1])
    for n in range(3):
        add(("qkv", n), cols(I["odd_w_qkv"][0], 512 * n))
    for n in range(2):
        add(("owo", n), cols(I["odd_w_out"][0], 512 * n))
    add_moe(1, 3)
    cut[2] = len(plan)
    add_ada("ada2", I["w_mod_2"][0])
    w2 = I["w_in_2"][0]
    for n in range(5):
        add(("xbc", n), cols(w2, 2048 + 512 * n))
    add(("dt", 0), cols(w2, 4608, width=48), width=48)
    for n in range(3):
        add(("z", n), cols(w2, 512 + 512 * n))
    for h in range(2):
        add(("sso", 0, h), cols(I["w_ssd_out_2"][0], 512 * h))
        add(("sso", 1, h), cols(I["w_ssd_out_2"][0], 512 * h, k0=1024, k=4), k=4)
    add(("uf", 0), cols(w2, 0))
    for h in range(2):
        add(("four", h), cols(I["w_fourier_2"][0], 512 * h, k=4), k=4)
    for n in (0, 2, 1, 3):
        add(("gate", n), cols(w2, 4656 + 512 * n))
    for h in range(2):
        add(("wout", h), cols(I["w_out_2"][0], 512 * h))
    for g in range(4):
        for e in range(4 * g, 4 * g + 4):
            for m, h in (("g", 0), ("u", 0), ("g", 1), ("u", 1)):
                add((2, e, m, h), cols(I["w_e_gate_2" if m == "g" else "w_e_up_2"][0, e], 512 * h))
        for h in range(2):
            for e in range(4 * g, 4 * g + 4):
                add((2, e, "d", h), cols(I["w_e_down_2"][0, e], 512 * h))

    if upto in cut:
        del plan[cut[upto]:]

    w_x, w_k, w_c, w_s = Wire(sem("w_x")), Wire(sem("w_k")), Wire(sem("w_c")), Wire(sem("w_s"))
    w_x2 = Wire(sem("w_x2"))
    w_z, w_xe = Wire(sem("w_z")), [Wire(sem("w_xe0")), Wire(sem("w_xe1"))]
    w_sc, w_y, w_g, w_o = Wire(sem("w_sc")), [Wire(sem("w_y0")), Wire(sem("w_y1"))], Wire(sem("w_g")), Wire(sem("w_o"))
    crow = AR[0:32, 0:P]
    for n, name in enumerate(("c", "c_ctx", "c_2", "c_ctx_2")):
        v = I[name] if name in ("c_ctx", "c_ctx_2") else I[name][0]
        mc = w_c.sent(nc.scalar.dma_start(AR[8 * n:8 * n + 8, 0:P], v.rearrange("(a b) -> a b", b=P)))
    mk = w_k.sent(nc.scalar.dma_start(KC[:, :], I["consts"][:, 0:C_KEEP]))
    mx = w_x.sent(nc.scalar.dma_start(X[:, 0:2, :], I["x"][0].rearrange("(c p) d -> p c d", p=P)))
    mx = w_x.sent(nc.scalar.dma_start(X[:, 2:4, :], I["ctx"][0].rearrange("(c p) d -> p c d", p=P)))
    ring = Ring(ringt, sp, [sem(f"w_r{n}") for n in range(NS)], plan)

    m_one = dve.done(dve.after().memset(ones[:, :], 1.0))
    m_cp = dve.done(dve.after().memset(CP[:, :, :, :, :], 0.0))
    zt = AR[:, 512:512 + D]
    m_z = pool.done(pool.after().memset(zt, 0.0))
    pool.after(m_z)
    for n in range(0, XROWS // P):
        mz = w_z.sent(nc.gpsimd.dma_start(XP[n * P:(n + 1) * P, :], zt))
    b = ps.take()
    pe.after(mc, mk)
    m = pe.done(nc.tensor.transpose(b.ap[:, 0:32], crow, ident[0:32, 0:32]))
    m = act.done(act.after(m).activation(CT[:, :], b.ap[:, 0:32], ACT.Silu))
    b.free(m)
    for half in range(2):
        for j in range(6):
            for r in range(2):
                m_cp = dve.done(dve.after(m, m_cp).tensor_copy(
                    CP[:, half, :, j, 2 * j + r], CT[:, 16 * half + 8 * r:16 * half + 8 * r + 8]))
    start_marks = fence(mx, mz, mk)

    def modulation(tag, half, bias, gains):
        at[0] = 0
        fence()
        br, GB = take(D)[0:6, :], take(D)[0:12, :]
        m = w_s.sent(nc.gpsimd.dma_start(br, bias.rearrange("(a b) -> a b", b=D)))
        mg = dve.done(dve.after().memset(GB, 1.0))
        pool.after(mg)
        for row, g in gains:
            for r in range(2):
                m = w_s.sent(nc.gpsimd.dma_start(GB[row + r:row + r + 1, :], g.rearrange("(a b) -> a b", a=1)))
        b = ps.take(2)
        pe.after(m)
        for h in range(2):
            mm(b.ap[0:12, h * 512:h * 512 + 512], KC[0:6, C_REP:C_REP + 12], br[:, h * 512:h * 512 + 512], True, False,
               skip_group_check=True)
        for n in range(12):
            w, mw, k = ring.take((tag, n))
            pe.after(mw)
            j, h = n // 2, n % 2
            for c in range(8):
                last = mm(b.ap[0:12, h * 512:h * 512 + 512], CP[:, half, c, j, :], w[:, c, :], False,
                          n >= 10 and c == 7, skip_group_check=True)
            m2 = pe.done(last)
            ring.free(k, m2)
        m = dve.done(dve.after(m, m2).scalar_tensor_tensor(
            out=MOD[:, :], in0=b.ap[0:12, :], scalar=KC[0:12, C_ONE:C_ONE + 1], in1=GB, op0=ALU.add, op1=ALU.mult))
        b.free(m)
        fence()

    def spread(row):
        b = ps.take(2)
        for h in range(2):
            last = mm(b.ap[:, h * 512:h * 512 + 512], ident[0:12, row:row + 1].to_broadcast([12, P]),
                      MOD[:, h * 512:h * 512 + 512], True, True)
        return b, pe.done(last)

    def rstd_of(srcs, width, marks, rs, junk):
        for n, s in enumerate(srcs):
            m = act.done(act.after(*marks).activation(junk, s, ACT.Square, accum_out=rs[:, n:n + 1]))
        n = len(srcs)
        m = dve.done(dve.after(m).tensor_scalar(rs[:, 0:n], rs[:, 0:n], 1.0 / width, EPS, ALU.mult, ALU.add))
        m = act.done(act.after(m).activation(rs[:, 0:n], rs[:, 0:n], ACT.Sqrt))
        return dve.done(dve.after(m).reciprocal(rs[:, 0:n], rs[:, 0:n]))

    def modulated(H, chunks, shift, scale, junk, rs):
        m = rstd_of([X[:, c, :] for c in chunks], D, [dve.mark()], rs, junk)
        marks = {}
        for r in range(2):
            mine = [c for c in chunks if c // 2 == r]
            if not mine:
                continue
            a, ma = spread(scale + r)
            s, ms = spread(shift + r)
            for c in mine:
                n = chunks.index(c)
                m = dve.done(dve.after(m, ma).scalar_tensor_tensor(
                    out=H[:, c, :], in0=X[:, c, :], scalar=rs[:, n:n + 1], in1=a.ap, op0=ALU.mult, op1=ALU.mult))
                m = dve.done(dve.after(m, ms).tensor_tensor(H[:, c, :], H[:, c, :], s.ap, ALU.add))
                marks[c] = m
            a.free(m)
            s.free(m)
        return marks

    def turned(dst, src, n, mark):
        for j in range(0, n, 4):
            b = ps.take()
            pe.after(mark)
            for i in range(j, min(n, j + 4)):
                last = nc.tensor.transpose(b.ap[:, (i - j) * P:(i - j + 1) * P], src[:, i * P:(i + 1) * P], ident)
            m = pe.done(last)
            k = min(4, n - j)
            m = evac(dst[:, j:j + k, :], b.ap[:, 0:k * P].rearrange("p (a b) -> p a b", a=k), m)
            b.free(m)
            last_marks.append(m)
        return m

    last_marks = []

    def turn_all(HT, H, chunks, marks, n=8):
        last_marks.clear()
        for c in chunks:
            turned(HT[:, :, c * P:(c + 1) * P], H[:, c, :], n, marks[c])
        out_marks = list(last_marks)
        return out_marks

    def project_T(w, mw, j, HT, t0, t1, M=P, out_p=0, bank=None, wcols=None):
        b = ps.take()
        pe.after(*mw)
        for c in range(8):
            last = mm(b.ap[:, 0:t1 - t0], w[:, c, j * P:(j + 1) * P], HT[:, c, t0:t1], c == 0, c == 7)
        return b, pe.done(last)

    def project(w, mw, HT, c, width=512, K=8):
        b = ps.take()
        pe.after(*mw)
        for k in range(K):
            last = mm(b.ap[:, 0:width], HT[:, k, c * P:(c + 1) * P], w[:, k, 0:width], k == 0, k == K - 1)
        return b, pe.done(last)

    def add_branch(keys, YT, chunks, gate_row, marks, tmp):
        gates = {}
        for r in sorted({c // 2 for c in chunks}):
            g, mg = spread(gate_row + r)
            dst = tmp[r]
            m = dve.done(dve.after(mg).tensor_copy(dst, g.ap))
            g.free(m)
            gates[r] = m
        for h, key in enumerate(keys):
            w, mw, k = ring.take(key)
            for c in chunks:
                b, m = project(w, [mw] + marks, YT, c)
                last = m
                sl = slice(h * 512, h * 512 + 512)
                m = dve.done(dve.after(m, gates[c // 2]).tensor_tensor(tmp[2], b.ap, tmp[c // 2][:, sl], ALU.mult))
                b.free(m)
                m = dve.done(dve.after(m).tensor_tensor(X[:, c, sl], X[:, c, sl], tmp[2], ALU.add))
            ring.free(k, last)

    def rope(dst, raw, marks):
        b = ps.take()
        pe.after(*marks)
        m = pe.done(mm(b.ap[:, 0:256], KC[:, C_ROT:C_ROT + P], raw, True, True))
        t = rtmp
        m = dve.done(dve.after(m).tensor_tensor(t, b.ap[:, 0:256], KC[:, C_SIN:C_SIN + 256], ALU.mult))
        b.free(m)
        m = dve.done(dve.after(m).tensor_tensor(dst, raw, KC[:, C_COS:C_COS + 256], ALU.mult))
        return dve.done(dve.after(m).tensor_tensor(dst, dst, t, ALU.add))

    def softmax_tail(o, a, ):
        pass

    def broadcast_load(dst, src, n):
        return w_s.sent(nc.gpsimd.dma_start(dst, src.rearrange("(a b) -> a b", a=1).to_broadcast([P, n])))

    def routed(layer, chunks, nover):
        at[0] = 0
        smat[0] = 0
        fence()
        nch = len(chunks)
        nb = 16 + nover
        rs, rb, rw = small(8), small(16), small(8 * 16)
        w_r = w_s.sent(nc.gpsimd.dma_start(rw.rearrange("p (c e) -> p c e", c=8),
                                           I["router_w"].rearrange("(c p) e -> p c e", p=P)))
        w_r = broadcast_load(rb, I["router_b"], 16)
        H = take(4 * D).rearrange("p (c d) -> p c d", c=4)
        HT = take(8 * 512).rearrange("p (c t) -> p c t", c=8)
        junk = take(D)
        marks = modulated(H, chunks, 6, 8, junk, rs)
        tm = turn_all(HT, H, chunks, marks)
        N = nch * 16
        b = ps.take()
        pe.after(w_r, *tm)
        for i, c in enumerate(chunks):
            for k in range(8):
                last = mm(b.ap[:, i * 16:i * 16 + 16], HT[:, k, c * P:(c + 1) * P],
                          rw.rearrange("p (c e) -> p c e", c=8)[:, k, :], k == 0, k == 7)
        m = pe.done(last)
        aff, sel, o1, o2, t1, t2 = (small(N) for _ in range(6))
        m = act.done(act.after(m).activation(aff, b.ap[:, 0:N], ACT.Sigmoid))
        b.free(m)
        v3 = lambda a: a.rearrange("p (c e) -> p c e", e=16)
        g4 = lambda a: a.rearrange("p (g e) -> p g e", e=4)
        D_ = lambda ins: dve.done(ins)
        dve.after(m, w_r)
        D_(dve.after().tensor_tensor(v3(sel), v3(aff), rb.unsqueeze(1).to_broadcast([P, nch, 16]), ALU.add))
        G = nch * 4
        hi, lo, mid, gs, gt = small(2 * G), small(2 * G), small(G), small(G), small(G)
        s4 = g4(sel)
        h2, l2 = hi.rearrange("p (g e) -> p g e", e=2), lo.rearrange("p (g e) -> p g e", e=2)
        D_(dve.after().tensor_tensor(h2, s4[:, :, 0:2], s4[:, :, 2:4], ALU.max))
        D_(dve.after().tensor_tensor(l2, s4[:, :, 0:2], s4[:, :, 2:4], ALU.min))
        D_(dve.after().tensor_tensor(gs, h2[:, :, 0], h2[:, :, 1], ALU.max))
        D_(dve.after().tensor_tensor(mid, h2[:, :, 0], h2[:, :, 1], ALU.min))
        D_(dve.after().tensor_tensor(gt, l2[:, :, 0], l2[:, :, 1], ALU.max))
        D_(dve.after().tensor_tensor(mid, mid, gt, ALU.max))
        D_(dve.after().tensor_tensor(gs, gs, mid, ALU.add))
        red = small(nch)
        c4 = lambda a: a.rearrange("p (c g) -> p c g", g=4)

        def first_of_max(dst, val, weights, view, k):
            D_(dve.after().tensor_reduce(red, view(val), AX.X, ALU.max))
            D_(dve.after().tensor_tensor(view(dst), view(val), red.unsqueeze(2).to_broadcast([P, nch, k]), ALU.is_equal))
            D_(dve.after().tensor_tensor(view(dst), view(dst), weights.unsqueeze(1).to_broadcast([P, nch, k]), ALU.mult))
            D_(dve.after().tensor_reduce(red, view(dst), AX.X, ALU.max))
            return D_(dve.after().tensor_tensor(view(dst), view(dst), red.unsqueeze(2).to_broadcast([P, nch, k]), ALU.is_equal))

        first_of_max(gt, gs, KC[:, C_GW:C_GW + 4], c4, 4)
        D_(dve.after().tensor_scalar(gt, gt, 1.0, 2 * BIG, ALU.subtract, ALU.mult))
        D_(dve.after().tensor_tensor(g4(t1), g4(sel), gt.unsqueeze(2).to_broadcast([P, G, 4]), ALU.add))
        ew = small(16)
        D_(dve.after().tensor_scalar(ew, KC[:, C_EX:C_EX + 16], -1.0, 16.0, ALU.mult, ALU.add))
        first_of_max(o1, t1, ew, v3, 16)
        D_(dve.after().scalar_tensor_tensor(out=t1, in0=o1, scalar=-4 * BIG, in1=t1, op0=ALU.mult, op1=ALU.add))
        first_of_max(o2, t1, ew, v3, 16)
        wk = [small(nch), small(nch)]
        den = small(nch)
        for k, o in enumerate((o1, o2)):
            D_(dve.after().tensor_tensor(t2, o, aff, ALU.mult))
            D_(dve.after().tensor_reduce(wk[k], v3(t2), AX.X, ALU.add))
        D_(dve.after().tensor_tensor(den, wk[0], wk[1], ALU.add))
        D_(dve.after().reciprocal(den, den))
        for k in range(2):
            D_(dve.after().tensor_tensor(wk[k], wk[k], den, ALU.mult))
        M = small(N)
        m = D_(dve.after().tensor_tensor(M, o1, o2, ALU.add))
        b = ps.take()
        pe.after(m)
        for i in range(nch):
            for j in range(i):
                mm(b.ap[:, i * 16:i * 16 + 16], ones[:, :], M[:, j * 16:j * 16 + 16], j == 0, False)
            mm(b.ap[:, i * 16:i * 16 + 16], KC[:, C_LT:C_LT + P], M[:, i * 16:i * 16 + 16], i == 0, True)
        for j in range(nch):
            last = mm(b.ap[:, 64:80], ones[:, :], M[:, j * 16:j * 16 + 16], j == 0, j == nch - 1)
        m = pe.done(last)
        pos, blk, tt, cnt, inc, exc = small(N), small(N), small(N), small(16), small(16), small(16)
        D_(dve.after(m).tensor_copy(pos, b.ap[:, 0:N]))
        m = D_(dve.after().tensor_copy(cnt, b.ap[:, 64:80]))
        b.free(m)
        D_(dve.after().tensor_scalar(exc, cnt, 128.0, None, ALU.is_gt))
        for q in (256.0, 384.0):
            D_(dve.after().scalar_tensor_tensor(out=exc, in0=cnt, scalar=q, in1=exc, op0=ALU.is_gt, op1=ALU.add))
        D_(dve.after().tensor_tensor_scan(inc, ones[:, 0:16], exc, 0.0, ALU.mult, ALU.add))
        D_(dve.after().tensor_tensor(exc, inc, exc, ALU.subtract))
        D_(dve.after().tensor_scalar(blk, pos, 128.0, None, ALU.is_ge))
        for q in (256.0, 384.0):
            D_(dve.after().scalar_tensor_tensor(out=blk, in0=pos, scalar=q, in1=blk, op0=ALU.is_ge, op1=ALU.add))
        e3 = KC[:, C_EX:C_EX + 16].unsqueeze(1).to_broadcast([P, nch, 16])
        D_(dve.after().tensor_tensor(v3(tt), v3(blk), e3, ALU.subtract))
        D_(dve.after().tensor_tensor(v3(t1), v3(tt), exc.unsqueeze(1).to_broadcast([P, nch, 16]), ALU.add))
        D_(dve.after().tensor_scalar(t1, t1, 15.0, None, ALU.add))
        D_(dve.after().tensor_scalar(t2, blk, 0.0, None, ALU.is_gt))
        D_(dve.after().tensor_tensor(t1, t1, t2, ALU.mult))
        D_(dve.after().tensor_tensor(t1, t1, tt, ALU.subtract))
        D_(dve.after().scalar_tensor_tensor(out=t1, in0=t1, scalar=128.0, in1=pos, op0=ALU.mult, op1=ALU.add))
        rowf = small(2 * nch)
        for k, o in enumerate((o1, o2)):
            D_(dve.after().tensor_tensor(t2, o, t1, ALU.mult))
            D_(dve.after().tensor_reduce(rowf[:, k * nch:(k + 1) * nch], v3(t2), AX.X, ALU.add))
        m_dst = D_(dve.after().tensor_copy(DST[:, 0:2 * nch], rowf))
        oe = small(16)
        for j in range(nover):
            D_(dve.after().tensor_scalar(t2[:, 0:16], inc, float(j), None, ALU.is_le))
            D_(dve.after().tensor_reduce(oe[:, j:j + 1], t2[:, 0:16], AX.X, ALU.add))
        D_(dve.after().tensor_scalar(oe[:, 0:nover], oe[:, 0:nover], 15.0, None, ALU.min))
        m_oe = D_(dve.after().tensor_copy(OE[0:1, 0:nover], oe[0:1, 0:nover]))
        over["mark"] = [m_oe]
        pool.after(m_dst, *[marks[c] for c in chunks])
        for i, c in enumerate(chunks):
            for k in range(2):
                msc = w_sc.sent(nc.gpsimd.indirect_dma_start(
                    out=XP[:, :], out_offset=bass.IndirectOffsetOnAxis(ap=DST[:, k * nch + i:k * nch + i + 1], axis=0),
                    in_=H[:, c, :], in_offset=None))
        keep = at[0]
        at[0] = 0
        fence(msc)
        xe = [take(D) for _ in range(2)]
        xeT = [take(D).rearrange("p (c t) -> p c t", c=8) for _ in range(2)]
        hid = [take(D) for _ in range(2)]
        hidT = [take(D).rearrange("p (c t) -> p c t", c=8) for _ in range(2)]
        yo = [take(D) for _ in range(2)]
        gg = [take(512) for _ in range(2)]
        m_in, free_xe, free_xeT, free_hid, free_hT = {}, {}, {}, {}, {}
        m_st = {}

        def fetch(n):
            if n < nb:
                pool.after(*free_xe.get(n - 2, ()))
                m_in[n] = w_xe[n % 2].sent(nc.gpsimd.dma_start(xe[n % 2], XP[n * P:(n + 1) * P, :]))

        def turn_in(n):
            if n >= nb:
                return
            last_marks.clear()
            pe.after(*free_xeT.get(n - 2, ()))
            turned(xeT[n % 2], xe[n % 2], 8, m_in[n])
            xeT_ready[n] = list(last_marks)
            free_xe[n] = (pe.mark(),)
            fetch(n + 2)

        xeT_ready = {}
        fetch(0)
        fetch(1)
        turn_in(0)
        for n in range(nb):
            i = n % 2
            m_h = []
            for h in range(2):
                sl = slice(h * 512, h * 512 + 512)
                w, mw, k = ring.take((layer, n, "g", h))
                b, m = project(w, [mw] + xeT_ready[n], xeT[i], 0)
                ring.free(k, m)
                m = act.done(act.after(m, *free_hid.get(n - 2, ())).activation(hid[i][:, sl], b.ap, ACT.Silu))
                b.free(m)
                w, mw, k = ring.take((layer, n, "u", h))
                b, m2 = project(w, [mw], xeT[i], 0)
                ring.free(k, m2)
                m = dve.done(dve.after(m, m2).tensor_tensor(hid[i][:, sl], hid[i][:, sl], b.ap, ALU.mult))
                b.free(m)
                m_h.append(m)
            free_xeT[n] = (pe.mark(),)
            turn_in(n + 1)
            last_marks.clear()
            turned(hidT[i][:, 0:4, :], hid[i][:, 0:512], 4, m_h[0])
            turned(hidT[i][:, 4:8, :], hid[i][:, 512:D], 4, m_h[1])
            hm = list(last_marks)
            free_hid[n] = (pe.mark(),)
            ms = []
            for h in range(2):
                w, mw, k = ring.take((layer, n, "d", h))
                b, m = project(w, [mw] + hm, hidT[i], 0)
                ring.free(k, m)
                m = evac(yo[i][:, h * 512:h * 512 + 512], b.ap, m, m_st.get(n - 2))
                b.free(m)
                ms.append(m)
            act.after(*ms)
            m_st[n] = w_y[i].sent(nc.scalar.dma_start(YP[n * P:(n + 1) * P, :], yo[i]))
        at[0] = 0
        fence(m_st[nb - 1], m_st[nb - 2])
        R = [take(D) for _ in range(2 * nch)]
        for i, c in enumerate(chunks):
            for k in range(2):
                mg = w_g.sent(nc.gpsimd.indirect_dma_start(
                    out=R[2 * i + k], out_offset=None, in_=YP[:, :],
                    in_offset=bass.IndirectOffsetOnAxis(ap=DST[:, k * nch + i:k * nch + i + 1], axis=0)))
        for r in sorted({c // 2 for c in chunks}):
            g, m = spread(10 + r)
            for i, c in enumerate(chunks):
                if c // 2 != r:
                    continue
                a, b2 = R[2 * i], R[2 * i + 1]
                m = dve.done(dve.after(m, mg).tensor_scalar(b2, b2, wk[1][:, i:i + 1], None, ALU.mult))
                m = dve.done(dve.after(m).scalar_tensor_tensor(
                    out=a, in0=a, scalar=wk[0][:, i:i + 1], in1=b2, op0=ALU.mult, op1=ALU.add))
                m = dve.done(dve.after(m).tensor_tensor(a, a, g.ap, ALU.mult))
                m = dve.done(dve.after(m).tensor_tensor(X[:, c, :], X[:, c, :], a, ALU.add))
            g.free(m)

    modulation("ada0", 0, I["ada_b"][0], [(2, I["norm_mix_g"][0]), (8, I["norm_ffn_g"][0])])
    at[0] = 0
    allc = [0, 1, 2, 3]
    HT = take(8 * 512).rearrange("p (c t) -> p c t", c=8)
    G = take(4 * 512).rearrange("p (c n) -> p c n", c=4)
    base = at[0]
    H = take(4 * D).rearrange("p (c d) -> p c d", c=4)
    junk = take(D)
    smat[0] = 0
    rs = small(8)
    marks = modulated(H, allc, 0, 2, junk, rs)
    tm = turn_all(HT, H, allc, marks)
    at[0] = base
    fence(*tm)
    fm = lambda a: a.rearrange("p (c h t) -> p c h t", c=4, h=4)
    Q, FF, FB = (fm(take(2048)) for _ in range(3))
    V = take(2048).rearrange("p (c n) -> p c n", c=4)
    O = take(2048).rearrange("p (c n) -> p c n", c=4)
    S = take(512).rearrange("p (h v) -> p h v", h=4)
    lv = take(8 * 128)
    kt_, cum, ek, eq, kk, qq, A_, tA = (take(512) for _ in range(8))
    lf = tA
    lbr = take(128)
    m_lv = w_s.sent(nc.gpsimd.dma_start(lv[:, 7 * P:8 * P], I["consts"][:, C_LEV + 14 * P:C_LEV + 15 * P]))
    m_lv = w_s.sent(nc.gpsimd.dma_start(lbr[0:24, :], I["hgrn_lb_logits"].rearrange("a d (h k) -> (a d h) k", k=P)))
    on = small(128)
    m_lv = broadcast_load(on, I["hgrn_onorm_g"][0], P)
    for n in range(3):
        w, mw, k = ring.take(("in", n))
        for h in range(4):
            b, m = project_T(w, [mw], h, HT, 0, 512)
            dst = (Q, FF, FB)[n][:, :, h, :]
            src = b.ap.rearrange("p (c t) -> p c t", c=4)
            m2 = act.done(act.after(m).activation(dst, src, ACT.Silu if n == 0 else ACT.Sigmoid))
            b.free(m2)
        ring.free(k, m)
    for n, dst in ((3, V), (4, G)):
        w, mw, k = ring.take(("in", n))
        for c in allc:
            b, m = project(w, [mw], HT, c)
            if n == 3:
                m2 = dve.done(dve.after(m).tensor_copy(dst[:, c, :], b.ap))
            else:
                m2 = act.done(act.after(m).activation(dst[:, c, :], b.ap, ACT.Silu))
            b.free(m2)
        ring.free(k, m)
    b = ps.take()
    pe.after(m_lv)
    m = pe.done(nc.tensor.transpose(b.ap[:, 0:24], lbr[0:24, :], ident[0:24, 0:24]))
    lg, lb, oml, t8 = small(24), small(8), small(8), small(8)
    m = dve.done(dve.after(m).tensor_copy(lg, b.ap[:, 0:24]))
    b.free(m)
    dve.done(dve.after().tensor_tensor(t8, lg[:, 0:8], lg[:, 8:16], ALU.max))
    dve.done(dve.after().tensor_tensor(t8, t8, lg[:, 16:24], ALU.max))
    l3 = lg.rearrange("p (a b) -> p a b", a=3)
    m = dve.done(dve.after().tensor_tensor(l3, l3, t8.unsqueeze(1).to_broadcast([P, 3, 8]), ALU.subtract))
    m = act.done(act.after(m).activation(lg, lg, ACT.Exp))
    dve.done(dve.after(m).tensor_tensor(t8, lg[:, 0:8], lg[:, 8:16], ALU.add))
    dve.done(dve.after().tensor_tensor(t8, t8, lg[:, 16:24], ALU.add))
    dve.done(dve.after().reciprocal(t8, t8))
    dve.done(dve.after().tensor_tensor(lb, lg[:, 0:8], t8, ALU.mult))
    m_lb = dve.done(dve.after().tensor_scalar(oml, lb, -1.0, 1.0, ALU.mult, ALU.add))
    fence(m_lb)
    et = small(4)
    SC = 128 ** -0.5
    h4 = lambda a: a.rearrange("p (h t) -> p h t", h=4)
    for d in range(2):
        order = (2, 3, 0, 1) if d == 0 else (3, 2, 1, 0)
        FX = (FF, FB)[d]
        pool.after(dve.mark())
        m_lv = w_s.sent(nc.gpsimd.dma_start(lv[:, 0:7 * P], I["consts"][:, C_LEV + 7 * d * P:C_LEV + 7 * (d + 1) * P]))
        for step, c in enumerate(order):
            q4 = Q[:, c, :, :]
            for h in range(4):
                m = dve.done(dve.after().tensor_scalar(FX[:, c, h, :], FX[:, c, h, :], oml[:, 4 * d + h:4 * d + h + 1],
                                                       lb[:, 4 * d + h:4 * d + h + 1], ALU.mult, ALU.add))
            m_lf = act.done(act.after(m).activation(h4(lf), FX[:, c, :, :], ACT.Ln))
            m_k = dve.done(dve.after().tensor_scalar(h4(kt_), FX[:, c, :, :], -1.0, 1.0, ALU.mult, ALU.add))
            for h in range(4):
                i_, o_ = h4(lf)[:, h, :], h4(cum)[:, h, :]
                if d == 1:
                    i_, o_ = i_[:, ::-1], o_[:, ::-1]
                m = dve.done(dve.after(m_lf).tensor_tensor_scan(o_, ones[:, :], i_, 0.0, ALU.mult, ALU.add))
            end = 127 if d == 0 else 0
            m_et = act.done(act.after(m).activation(et, h4(cum)[:, :, end], ACT.Exp))
            for l in range(8):
                if l < 7:
                    hb = 64 >> l
                    v = lambda a: a.rearrange("p (n s b) -> p n s b", s=2, b=hb)
                    qs, ks, ref = (1, 0, hb - 1) if d == 0 else (0, 1, 0)
                    cv = v(cum)
                    r_ = (cv[:, :, ks, ref] if d == 0 else cv[:, :, ks, ref]).unsqueeze(2).to_broadcast([P, 256 // hb, hb])
                    ew_, kw_ = eq[:, 0:256].rearrange("p (n b) -> p n b", b=hb), ek[:, 0:256].rearrange("p (n b) -> p n b", b=hb)
                    m1 = dve.done(dve.after(pe.mark()).tensor_tensor(ew_, cv[:, :, qs, :], r_, ALU.subtract))
                    m2 = dve.done(dve.after().tensor_tensor(kw_, r_, cv[:, :, ks, :], ALU.subtract))
                    m1 = act.done(act.after(m1).activation(eq[:, 0:256], eq[:, 0:256], ACT.Exp))
                    m2 = act.done(act.after(m2).activation(ek[:, 0:256], ek[:, 0:256], ACT.Exp))
                    if l == 0:
                        dve.done(dve.after().memset(qq, 0.0))
                        dve.done(dve.after().memset(kk, 0.0))
                    n2 = 64 // hb
                    for h in range(4):
                        qv = Q[:, c, h, :].rearrange("p (n s b) -> p n s b", s=2, b=hb)[:, :, qs, :]
                        m3 = dve.done(dve.after(m1).scalar_tensor_tensor(
                            out=v(qq)[:, h * n2:(h + 1) * n2, qs, :], in0=qv, scalar=SC,
                            in1=ew_[:, h * n2:(h + 1) * n2, :], op0=ALU.mult, op1=ALU.mult))
                    m3 = dve.done(dve.after(m2).tensor_tensor(v(kk)[:, :, ks, :], v(kt_)[:, :, ks, :], kw_, ALU.mult))
                else:
                    m3 = dve.done(dve.after(pe.mark()).tensor_scalar(h4(qq), q4, SC, None, ALU.mult))
                b = ps.take()
                pe.after(m3, m_k)
                kl = kk if l < 7 else kt_
                for h in range(4):
                    last = mm(b.ap[:, h * P:(h + 1) * P], h4(kl)[:, h, :], h4(qq)[:, h, :], True, True)
                m = pe.done(last)
                mask = lv[:, l * P:(l + 1) * P]
                dst = A_ if l == 0 else tA
                m = dve.done(dve.after(m, m_lv).tensor_tensor(h4(dst), h4(b.ap), mask.unsqueeze(1).to_broadcast([P, 4, P]), ALU.mult))
                b.free(m)
                if l:
                    m = dve.done(dve.after(m).tensor_tensor(A_, A_, tA, ALU.add))
            m_A = m
            m1 = act.done(act.after(m_A, pe.mark()).activation(eq, cum, ACT.Exp))
            for h in range(4):
                m1 = dve.done(dve.after(m1).scalar_tensor_tensor(out=h4(qq)[:, h, :], in0=Q[:, c, h, :], scalar=SC,
                                                                 in1=h4(eq)[:, h, :], op0=ALU.mult, op1=ALU.mult))
            b = ps.take()
            pe.after(m_A, m1)
            for h in range(4):
                last = mm(b.ap[:, h * P:(h + 1) * P], h4(A_)[:, h, :], V[:, c, h * P:(h + 1) * P], True, step == 0)
                if step:
                    last = mm(b.ap[:, h * P:(h + 1) * P], h4(qq)[:, h, :], S[:, h, :], False, True)
            m = pe.done(last)
            if d == 0:
                m = dve.done(dve.after(m).tensor_copy(O[:, c, :], b.ap))
            else:
                m = dve.done(dve.after(m).tensor_tensor(O[:, c, :], O[:, c, :], b.ap, ALU.add))
            b.free(m)
            if step == 3:
                continue
            m = dve.done(dve.after().tensor_tensor(h4(ek), h4(cum)[:, :, end:end + 1].to_broadcast([P, 4, P]), h4(cum), ALU.subtract))
            m = act.done(act.after(m).activation(ek, ek, ACT.Exp))
            m = dve.done(dve.after(m).tensor_tensor(kk, kt_, ek, ALU.mult))
            b = ps.take()
            pe.after(m)
            for h in range(4):
                last = nc.tensor.transpose(b.ap[:, h * P:(h + 1) * P], h4(kk)[:, h, :], ident)
            m = pe.done(last)
            m = act.done(act.after(m).copy(tA, b.ap))
            b.free(m)
            b = ps.take()
            pe.after(m)
            for h in range(4):
                last = mm(b.ap[:, h * P:(h + 1) * P], h4(tA)[:, h, :], V[:, c, h * P:(h + 1) * P], True, True)
            m = pe.done(last)
            if step == 0:
                m = dve.done(dve.after(m).tensor_copy(S[:, :, :], h4(b.ap)))
            else:
                for h in range(4):
                    m = dve.done(dve.after(m, m_et).scalar_tensor_tensor(
                        out=S[:, h, :], in0=S[:, h, :], scalar=et[:, h:h + 1], in1=b.ap[:, h * P:(h + 1) * P],
                        op0=ALU.mult, op1=ALU.add))
            b.free(m)
    ss = small(16)
    for c in allc:
        m = dve.done(dve.after(pe.mark()).tensor_tensor(tA, O[:, c, :], O[:, c, :], ALU.mult))
        m = dve.done(dve.after().tensor_reduce(ss[:, 4 * c:4 * c + 4], h4(tA), AX.X, ALU.add))

    def finish_rstd(ss, n, width):
        m = dve.done(dve.after().tensor_scalar(ss[:, 0:n], ss[:, 0:n], 1.0 / width, EPS, ALU.mult, ALU.add))
        m = act.done(act.after(m).activation(ss[:, 0:n], ss[:, 0:n], ACT.Sqrt))
        return dve.done(dve.after(m).reciprocal(ss[:, 0:n], ss[:, 0:n]))

    m = finish_rstd(ss, 16, 128)
    for c in allc:
        for h in range(4):
            m = dve.done(dve.after(m).scalar_tensor_tensor(
                out=O[:, c, h * P:(h + 1) * P], in0=O[:, c, h * P:(h + 1) * P], scalar=ss[:, 4 * c + h:4 * c + h + 1],
                in1=on, op0=ALU.mult, op1=ALU.mult))
        m = dve.done(dve.after(m).tensor_tensor(G[:, c, :], G[:, c, :], O[:, c, :], ALU.mult))
    at[0] = base
    smat[0] = 0
    fence()
    hm = lambda a: a.rearrange("p (h t) -> p h t", h=4)
    QA, KA = hm(take(2048)), hm(take(2048))
    VA = take(2048).rearrange("p (c n) -> p c n", c=4)
    YB = take(2048).rearrange("p (c n) -> p c n", c=4)
    P0, P1, aT = [take(512) for _ in range(2)], [take(512) for _ in range(2)], [take(512) for _ in range(2)]
    rtmp = take(256)
    rot2 = take(256)
    lam4, sub = small(256), small(128)
    m_l = broadcast_load(lam4, I["diff_lambda"][0].rearrange("a b -> (a b)"), 256)
    m_l = broadcast_load(sub, I["diff_subln_g"][0], 128)
    lt, l2 = small(128), small(2)
    for j in range(2):
        dve.done(dve.after(m_l).tensor_tensor(lt[:, j * 64:j * 64 + 64], lam4[:, 128 * j:128 * j + 64],
                                              lam4[:, 128 * j + 64:128 * j + 128], ALU.mult))
    m = dve.done(dve.after().tensor_reduce(l2, lt.rearrange("p (a b) -> p a b", a=2), AX.X, ALU.add))
    m = act.done(act.after(m).activation(l2, l2, ACT.Exp))
    lam = small(1)
    dve.done(dve.after(m).tensor_tensor(lam, l2[:, 1:2], l2[:, 0:1], ALU.subtract))
    m = dve.done(dve.after(m).tensor_scalar(lam, lam, 0.8 - 0.6 * math.exp(-0.0), None, ALU.subtract))
    for n, dst in ((5, QA), (6, KA)):
        w, mw, k = ring.take(("in", n))
        for h in range(4):
            b, m = project_T(w, [mw], h, HT, 0, 512)
            last = m
            m = evac(dst[:, h, :], b.ap, m)
            b.free(m)
            m = dve.done(dve.after(m, pe.mark()).tensor_copy(rot2, dst[:, h, 0:256]))
            rope(dst[:, h, 0:256], rot2, [m])
        ring.free(k, last)
    w, mw, k = ring.take(("in", 7))
    for c in allc:
        b, m = project(w, [mw], HT, c)
        last = m
        m = evac(VA[:, c, :], b.ap, m)
        b.free(m)
    ring.free(k, last)
    fence()
    st = small(8)
    u = 0
    old = {}
    for qi in allc:
        k0, k1 = (0, 512) if qi < 2 else (256, 512)
        nk = k1 - k0
        ob = ps.take()
        for h in range(4):
            for mp in range(2):
                b = ps.take()
                pr = slice(64 * mp, 64 * mp + 64)
                m = pe.done(mm(b.ap[:, 0:nk], QA[pr, h, qi * P:(qi + 1) * P], KA[pr, h, k0:k1], True, True))
                Pm = (P0, P1)[mp][u % 2]
                m = dve.done(dve.after(m).tensor_reduce(st[:, mp:mp + 1], b.ap[:, 0:nk], AX.X, ALU.max))
                m = dve.done(dve.after(m).tensor_scalar(st[:, mp:mp + 1], st[:, mp:mp + 1], -0.125, None, ALU.mult))
                m = act.done(act.after(m, old.get(u - 2)).activation(Pm[:, 0:nk], b.ap[:, 0:nk], ACT.Exp, bias=st[:, mp:mp + 1],
                                                                     scale=0.125, accum_out=st[:, 2 + mp:3 + mp]))
                b.free(m)
            m = dve.done(dve.after(m).reciprocal(st[:, 4:6], st[:, 2:4]))
            m = dve.done(dve.after(m).tensor_tensor(st[:, 5:6], st[:, 5:6], lam, ALU.mult))
            a0, a1 = P0[u % 2][:, 0:nk], P1[u % 2][:, 0:nk]
            m = dve.done(dve.after(m).tensor_scalar(a1, a1, st[:, 5:6], None, ALU.mult))
            m = dve.done(dve.after(m).scalar_tensor_tensor(out=a0, in0=a0, scalar=st[:, 4:5], in1=a1, op0=ALU.mult, op1=ALU.add))
            b = ps.take()
            pe.after(m)
            for j in range(nk // P):
                last = nc.tensor.transpose(b.ap[:, j * P:(j + 1) * P], a0[:, j * P:(j + 1) * P], ident)
            m = pe.done(last)
            old[u] = m
            m = evac(aT[u % 2][:, 0:nk], b.ap[:, 0:nk], m, old.get(("av", u - 2)))
            b.free(m)
            pe.after(m)
            for j in range(nk // P):
                last = mm(ob.ap[:, h * P:(h + 1) * P], aT[u % 2][:, j * P:(j + 1) * P],
                          VA[:, k0 // P + j, h * P:(h + 1) * P], j == 0, j == nk // P - 1)
            m = pe.done(last)
            old[("av", u)] = m
            u += 1
        m = dve.done(dve.after(m).tensor_copy(YB[:, qi, :], ob.ap))
        ob.free(m)
    ss = small(16)
    for c in allc:
        m = dve.done(dve.after().tensor_tensor(P0[0], YB[:, c, :], YB[:, c, :], ALU.mult))
        m = dve.done(dve.after().tensor_reduce(ss[:, 4 * c:4 * c + 4], h4(P0[0]), AX.X, ALU.add))
    m = finish_rstd(ss, 16, 128)
    m = dve.done(dve.after().tensor_scalar(ss, ss, 1.0 - (0.8 - 0.6 * math.exp(-0.0)), None, ALU.mult))
    for c in allc:
        for h in range(4):
            m = dve.done(dve.after(m).scalar_tensor_tensor(
                out=YB[:, c, h * P:(h + 1) * P], in0=YB[:, c, h * P:(h + 1) * P], scalar=ss[:, 4 * c + h:4 * c + h + 1],
                in1=sub, op0=ALU.mult, op1=ALU.mult))
    fence()
    last_marks.clear()
    for c in allc:
        turned(HT[:, 0:4, c * P:(c + 1) * P], G[:, c, :], 4, None)
        turned(HT[:, 4:8, c * P:(c + 1) * P], YB[:, c, :], 4, None)
    tm = list(last_marks)
    at[0] = base
    fence(*tm)
    tmp = [take(D), take(D), take(512)]
    add_branch([("wo", 0), ("wo", 1)], HT, allc, 4, tm, tmp)
    routed(0, allc, 7)

    def finish(src_marks, final=None):
        mo = w_o.sent(nc.scalar.dma_start(out[0].rearrange("(c p) d -> p c d", p=P), final if final is not None else X[:, 0:2, :]))
        act.after(mo)
        ctx.close()

    if upto == 1:
        fence()
        return finish(None)

    modulation("ada1", 0, I["ada_b"][1], [(2, I["norm_mix_g"][1]), (8, I["norm_ffn_g"][1])])
    at[0] = 0
    smat[0] = 0
    HT = take(8 * 512).rearrange("p (c t) -> p c t", c=8)
    base = at[0]
    H = take(4 * D).rearrange("p (c d) -> p c d", c=4)
    junk = take(D)
    rs = small(8)
    marks = modulated(H, allc, 0, 2, junk, rs)
    tm = turn_all(HT, H, allc, marks)
    at[0] = base
    fence(*tm)
    QC = take(8 * 256).rearrange("p (c t) -> p c t", c=8)
    KK = take(4 * 512).rearrange("p (c t) -> p c t", c=4)
    VC = take(4 * 256).rearrange("p (c n) -> p c n", c=4)
    YC = take(2 * D).rearrange("p (c n) -> p c n", c=2)
    swa = take(1024).rearrange("p (q n) -> p q n", q=2)
    Sx, aT = [take(512) for _ in range(2)], [take(512) for _ in range(2)]
    rtmp = take(256)
    rot2 = take(256)
    sink = small(16)
    w_sw = w_s.sent(nc.gpsimd.dma_start(swa, I["consts"][:, C_SWA:C_SWA + 1024].rearrange("p (q n) -> p q n", q=2)))
    w_sw = broadcast_load(sink, I["swa_sink"][0], 16)
    for n in range(2):
        w, mw, k = ring.take(("qkv", n))
        for j in range(4):
            b, m = project_T(w, [mw], j, HT, 0, 256)
            last = m
            m = evac(rot2, b.ap[:, 0:256], m, dve.mark(), pe.mark())
            b.free(m)
            rope(QC[:, 4 * n + j, :], rot2, [m])
        ring.free(k, last)
    w, mw, k = ring.take(("qkv", 2))
    pe.after(mw)
    for j in range(4):
        b = ps.take()
        for half in range(2):
            for c in range(8):
                last = mm(b.ap[64 * half:64 * half + 64, :], w[:, c, 64 * j:64 * j + 64], HT[:, c, :], c == 0, c == 7)
        m = pe.done(last)
        m = evac(KK[:, j, :], b.ap, m)
        b.free(m)
        m = dve.done(dve.after(m, pe.mark()).tensor_copy(rot2, KK[:, j, 0:256]))
        rope(KK[:, j, 0:256], rot2, [m])
    for c in allc:
        b = ps.take()
        for k8 in range(8):
            last = mm(b.ap[:, 0:256], HT[:, k8, c * P:(c + 1) * P], w[:, k8, 256:512], k8 == 0, k8 == 7)
        m = pe.done(last)
        m2 = evac(VC[:, c, :], b.ap[:, 0:256], m)
        b.free(m2)
    ring.free(k, m)
    fence()
    st, rr = small(8), small(16)
    old = {}
    u = 0
    for qi in range(2):
        for h in range(16):
            if h % 8 == 0:
                ob = ps.take()
            g = h // 4
            pr = slice(64 * (h % 2), 64 * (h % 2) + 64)
            b = ps.take()
            m = pe.done(mm(b.ap, QC[pr, h // 2, qi * P:(qi + 1) * P], KK[pr, g, :], True, True))
            s = Sx[u % 2]
            m = dve.done(dve.after(m, w_sw, old.get(u - 2)).scalar_tensor_tensor(
                out=s, in0=b.ap, scalar=0.125, in1=swa[:, qi, :], op0=ALU.mult, op1=ALU.add))
            b.free(m)
            m = dve.done(dve.after(m).tensor_reduce(st[:, 0:1], s, AX.X, ALU.max))
            m = dve.done(dve.after(m).tensor_scalar(st[:, 0:1], st[:, 0:1], sink[:, h:h + 1], -1.0, ALU.max, ALU.mult))
            m = act.done(act.after(m).activation(s, s, ACT.Exp, bias=st[:, 0:1], accum_out=st[:, 1:2]))
            m1 = act.done(act.after(m).activation(st[:, 2:3], sink[:, h:h + 1], ACT.Exp, bias=st[:, 0:1]))
            m2 = dve.done(dve.after(m1).tensor_tensor(st[:, 1:2], st[:, 1:2], st[:, 2:3], ALU.add))
            m_r = dve.done(dve.after(m2).reciprocal(rr[:, h:h + 1], st[:, 1:2]))
            b = ps.take()
            pe.after(m)
            for j in range(4):
                last = nc.tensor.transpose(b.ap[:, j * P:(j + 1) * P], s[:, j * P:(j + 1) * P], ident)
            m = pe.done(last)
            old[u] = m
            m = evac(aT[u % 2], b.ap, m, old.get(("av", u - 2)))
            b.free(m)
            pe.after(m)
            o8 = (h % 8) * 64
            for j in range(4):
                last = mm(ob.ap[:, o8:o8 + 64], aT[u % 2][:, j * P:(j + 1) * P], VC[:, j, 64 * g:64 * g + 64], j == 0, j == 3)
            m = pe.done(last)
            old[("av", u)] = m
            u += 1
            if h % 8 == 7:
                h0 = h - 7
                m = dve.done(dve.after(m, m_r).tensor_tensor(
                    YC[:, qi, h0 * 64:h0 * 64 + 512].rearrange("p (h d) -> p h d", h=8),
                    ob.ap.rearrange("p (h d) -> p h d", h=8),
                    rr[:, h0:h0 + 8].unsqueeze(2).to_broadcast([P, 8, 64]), ALU.mult))
                ob.free(m)
    fence()
    xc = [0, 1]
    tm = turn_all(HT, YC, xc, {0: None, 1: None})
    at[0] = base
    fence(*tm)
    tmp = [take(D), take(D), take(512)]
    add_branch([("owo", 0), ("owo", 1)], HT, xc, 4, tm, tmp)
    routed(1, xc, 3)
    at[0] = 0
    smat[0] = 0
    fence()
    mx = w_x2.sent(nc.gpsimd.dma_start(X[:, 2:4, :], I["ctx_2"][0].rearrange("(c p) d -> p c d", p=P)))
    fg = take(D)
    junk = take(D)
    m_f = broadcast_load(fg, I["final_norm_g"], D)
    rs = small(8)
    m = rstd_of([X[:, c, :] for c in xc], D, [], rs, junk)
    for c in xc:
        m = dve.done(dve.after(m, m_f).scalar_tensor_tensor(out=X[:, c, :], in0=X[:, c, :], scalar=rs[:, c:c + 1], in1=fg,
                                                            op0=ALU.mult, op1=ALU.mult))
    fence(mx)
    if upto == 2:
        return finish(None)

    modulation("ada2", 1, I["b_mod_2"][0], [(2, I["norm_mix_pre_2"][0]), (4, I["norm_mix_post_2"][0]),
                                            (8, I["norm_ffn_pre_2"][0]), (10, I["norm_ffn_post_2"][0])])
    at[0] = 0
    smat[0] = 0
    HT = take(8 * 512).rearrange("p (c t) -> p c t", c=8)
    base = at[0]
    H = take(4 * D).rearrange("p (c d) -> p c d", c=4)
    junk = take(D)
    rs = small(8)
    marks = modulated(H, allc, 0, 2, junk, rs)
    tm = turn_all(HT, H, allc, marks)
    at[0] = base
    fence(*tm)
    BT = take(4 * 512).rearrange("p (g t) -> p g t", g=4)
    CTt = take(4 * 256).rearrange("p (g t) -> p g t", g=4)
    XH = take(4 * 1536).rearrange("p (c n) -> p c n", c=4)
    BK = take(4 * 512).rearrange("p (c n) -> p c n", c=4)
    HS = [take(1536) for _ in range(2)]
    XW = take(1536)
    cv = [XW[:, 0:512], XW[:, 512:1024]]
    Y2 = XH[:, 2:4, :]
    cw = small(80)
    cwr = small(128)
    w_cv = w_s.sent(nc.gpsimd.dma_start(cwr[0:60, :], I["conv_w_2"][0].rearrange("k (c p) -> (k c) p", p=P)))
    w_cv = w_s.sent(nc.gpsimd.dma_start(cwr[60:80, :], I["conv_b_2"][0].rearrange("(c p) -> c p", p=P)))
    dtb, alog, dsk = small(48), small(48), small(24)
    w_cv = broadcast_load(dtb, I["dt_bias_2"][0].rearrange("a b -> (a b)"), 48)
    w_cv = broadcast_load(alog, I["a_log_2"][0].rearrange("a b -> (a b)"), 48)
    w_cv = broadcast_load(dsk, I["d_skip_2"][0], 24)
    b = ps.take()
    pe.after(w_cv)
    m = pe.done(nc.tensor.transpose(b.ap[:, 0:80], cwr[0:80, :], ident[0:80, 0:80]))
    m_cw = dve.done(dve.after(m).tensor_copy(cw, b.ap[:, 0:80]))
    b.free(m_cw)
    cvm = {}
    for n in range(5):
        w, mw, k = ring.take(("xbc", n))
        for j in range(4):
            ch = 4 * n + j
            T = 512 if ch < 16 else 256
            b, m = project_T(w, [mw], j, HT, 0, T)
            last = m
            a = cv[ch % 2]
            m = act.done(act.after(m, m_cw, *cvm.get(ch - 2, ())).activation(a[:, 0:T], b.ap[:, 0:T], ACT.Identity, bias=cw[:, 60 + ch:61 + ch],
                                                 scale=cw[:, 20 + ch:21 + ch]))
            rows = [(a[:, 0:256].rearrange("p (r t) -> p r t", r=4), b.ap[:, 0:256].rearrange("p (r t) -> p r t", r=4), 64)]
            if T == 512:
                rows.append((a[:, 256:512].rearrange("p (r t) -> p r t", r=1),
                             b.ap[:, 256:512].rearrange("p (r t) -> p r t", r=1), 256))
            for av, bv, L in rows:
                m = dve.done(dve.after(m).scalar_tensor_tensor(out=av[:, :, 1:L], in0=bv[:, :, 0:L - 1], scalar=cw[:, ch:ch + 1],
                                                               in1=av[:, :, 1:L], op0=ALU.mult, op1=ALU.add))
                m = dve.done(dve.after(m).scalar_tensor_tensor(out=av[:, :, 0:L - 1], in0=bv[:, :, 1:L],
                                                               scalar=cw[:, 40 + ch:41 + ch], in1=av[:, :, 0:L - 1],
                                                               op0=ALU.mult, op1=ALU.add))
            b.free(m)
            dst = a if ch < 12 else BT[:, ch - 12, :] if ch < 16 else CTt[:, ch - 16, :]
            m = act.done(act.after(m).activation(dst[:, 0:T], a[:, 0:T], ACT.Silu))
            cvm[ch] = (m,)
            if ch < 16:
                b = ps.take()
                pe.after(m)
                for c in allc:
                    last2 = nc.tensor.transpose(b.ap[:, c * P:(c + 1) * P], dst[:, c * P:(c + 1) * P], ident)
                m = pe.done(last2)
                cvm[ch] = (m,)
                d2 = XH[:, :, ch * P:(ch + 1) * P] if ch < 12 else BK[:, :, (ch - 12) * P:(ch - 11) * P]
                m = evac(d2, b.ap.rearrange("p (c t) -> p c t", c=4), m)
                b.free(m)
        ring.free(k, last)
    w, mw, k = ring.take(("dt", 0))
    b = ps.take()
    pe.after(mw)
    for c in allc:
        for k8 in range(8):
            last = mm(b.ap[:, c * 48:c * 48 + 48], HT[:, k8, c * P:(c + 1) * P], w[:, k8, 0:48], k8 == 0, k8 == 7)
    m = pe.done(last)
    ring.free(k, m)
    DT, U, DA, AC, NA, EA, WS, ET = (small(192) for _ in range(8))
    v4 = lambda a: a.rearrange("p (c n) -> p c n", c=4)
    m = dve.done(dve.after(m).tensor_tensor(v4(DT), v4(b.ap[:, 0:192]), dtb.unsqueeze(1).to_broadcast([P, 4, 48]), ALU.add))
    b.free(m)
    dve.done(dve.after().tensor_scalar(U, DT, -1.0, None, ALU.mult))
    m = dve.done(dve.after().tensor_tensor(U, DT, U, ALU.min))
    m = act.done(act.after(m).activation(U, U, ACT.Exp))
    m = act.done(act.after(m).activation(U, U, ACT.Ln, bias=1.0))
    m = act.done(act.after(m).activation(alog, alog, ACT.Exp))
    dve.done(dve.after(m).tensor_scalar(DT, DT, 0.0, None, ALU.max))
    dve.done(dve.after().tensor_tensor(DT, DT, U, ALU.add))
    dve.done(dve.after().tensor_scalar(alog, alog, -1.0, None, ALU.mult))
    m = dve.done(dve.after().tensor_tensor(v4(DA), v4(DT), alog.unsqueeze(1).to_broadcast([P, 4, 48]), ALU.mult))
    b = ps.take()
    pe.after(m)
    for d in range(2):
        tri = KC[:, (C_LE, C_GE)[d]:(C_LE, C_GE)[d] + P]
        mm(v4(b.ap[:, 0:192])[:, :, 24 * d:24 * d + 24], tri, v4(DA)[:, :, 24 * d:24 * d + 24], True, True)
    m = pe.done(mm(b.ap[:, 192:384], ones[:, :], DA, True, True))
    m = dve.done(dve.after(m).tensor_copy(AC, b.ap[:, 0:192]))
    m = dve.done(dve.after().tensor_tensor(WS, b.ap[:, 192:384], AC, ALU.subtract))
    m = act.done(act.after(m).activation(ET, b.ap[:, 192:384], ACT.Exp))
    b.free(m)
    m = act.done(act.after(m).activation(WS, WS, ACT.Exp))
    m = act.done(act.after(m).activation(EA, AC, ACT.Exp))
    dve.done(dve.after(m).tensor_tensor(WS, WS, DT, ALU.mult))
    m_s = dve.done(dve.after().tensor_scalar(NA, AC, -1.0, None, ALU.mult))
    fence()

    def heads(a):
        return a.rearrange("p (h d) -> p h d", d=64)

    def four(b):
        return b.ap.rearrange("p (g n) -> p g n", g=4)[:, :, 0:384].rearrange("p g (h d) -> p g h d", d=64)

    def g6(a):
        return a.rearrange("p (g h d) -> p g h d", g=4, d=64)

    def s6(a, c, d):
        return a[:, c * 48 + d * 24:c * 48 + d * 24 + 24].rearrange("p (g h) -> p g h", g=4).unsqueeze(3).to_broadcast([P, 4, 6, 64])

    def advance(d, c, first):
        m = dve.done(dve.after(pe.mark()).tensor_tensor(
            heads(XW), heads(XH[:, c, :]),
            WS[:, c * 48 + d * 24:c * 48 + d * 24 + 24].unsqueeze(2).to_broadcast([P, 24, 64]), ALU.mult))
        b = ps.take(4)
        pe.after(m)
        for g in range(4):
            last = mm(b.ap[:, g * 512:g * 512 + 384], BK[:, c, g * P:(g + 1) * P], XW[:, g * 384:(g + 1) * 384], True, True)
        m = pe.done(last)
        for g in range(4):
            hs = HS[d][:, g * 384:(g + 1) * 384]
            if first:
                m = dve.done(dve.after(m).tensor_copy(hs, b.ap[:, g * 512:g * 512 + 384]))
            else:
                e6 = ET[:, c * 48 + d * 24 + 6 * g:c * 48 + d * 24 + 6 * g + 6].unsqueeze(2).to_broadcast([P, 6, 64])
                m = dve.done(dve.after(m).tensor_tensor(heads(hs), heads(hs), e6, ALU.mult))
                m = dve.done(dve.after(m).tensor_tensor(hs, hs, b.ap[:, g * 512:g * 512 + 384], ALU.add))
        b.free(m)

    advance(0, 2, True)
    advance(0, 3, False)
    advance(1, 3, True)
    advance(1, 2, False)
    fence()

    def from_state(d, c, first):
        b = ps.take(4)
        pe.after(dve.mark())
        for g in range(4):
            last = mm(b.ap[:, g * 512:g * 512 + 384], CTt[:, g, c * P:(c + 1) * P], HS[d][:, g * 384:(g + 1) * 384], True, True)
        m = pe.done(last)
        for g in range(4):
            e6 = EA[:, c * 48 + d * 24 + 6 * g:c * 48 + d * 24 + 6 * g + 6].unsqueeze(2).to_broadcast([P, 6, 64])
            y = Y2[:, c, g * 384:(g + 1) * 384]
            if first:
                m = dve.done(dve.after(m).tensor_tensor(heads(y), heads(b.ap[:, g * 512:g * 512 + 384]), e6, ALU.mult))
            else:
                m = dve.done(dve.after(m).tensor_tensor(heads(XW[:, 0:384]), heads(b.ap[:, g * 512:g * 512 + 384]), e6, ALU.mult))
                m = dve.done(dve.after(m).tensor_tensor(y, y, XW[:, 0:384], ALU.add))
        b.free(m)

    from_state(0, 0, True)
    advance(0, 0, False)
    from_state(0, 1, True)
    from_state(1, 1, False)
    advance(1, 1, False)
    from_state(1, 0, False)
    fence()
    CB = XW[:, 0:512]
    Dd = [XW[:, 512:1024], XW[:, 1024:1536]]
    WW = [HS[0][:, 0:256], HS[0][:, 256:512]]
    xd = HS[1]
    for c in range(2):
        b = ps.take()
        pe.after(dve.mark())
        for g in range(4):
            last = mm(b.ap[:, g * P:(g + 1) * P], BT[:, g, c * P:(c + 1) * P], CTt[:, g, c * P:(c + 1) * P], True, True)
        m = pe.done(last)
        m = dve.done(dve.after(m).tensor_copy(CB, b.ap))
        b.free(m)
        m = dve.done(dve.after(m).tensor_tensor(heads(xd), heads(XH[:, c, :]), dsk.unsqueeze(2).to_broadcast([P, 24, 64]), ALU.mult))
        m = dve.done(dve.after(m).tensor_tensor(Y2[:, c, :], Y2[:, c, :], xd, ALU.add))
        for g in range(4):
            yb = ps.take()
            for hp in range(3):
                u = g * 3 + hp
                b = ps.take()
                for hh in range(2):
                    h = g * 6 + hp * 2 + hh
                    for d in range(2):
                        o = b.ap[:, (hh * 2 + d) * P:(hh * 2 + d + 1) * P]
                        col = c * 48 + d * 24 + h
                        mm(o, DA[:, col:col + 1].to_broadcast([P, P]), KC[:, (C_LE, C_GE)[d]:(C_LE, C_GE)[d] + P], True, False)
                        last = mm(o, ident, KC[:, (C_NF, C_NB)[d]:(C_NF, C_NB)[d] + P], False, True)
                m = pe.done(last)
                dd = Dd[u % 2]
                for hh in range(2):
                    h = g * 6 + hp * 2 + hh
                    for d in range(2):
                        col = c * 48 + d * 24 + h
                        sl = slice((hh * 2 + d) * P, (hh * 2 + d + 1) * P)
                        m = act.done(act.after(m, old.get(("dd", u - 2))).activation(dd[:, sl], b.ap[:, sl], ACT.Exp, bias=NA[:, col:col + 1]))
                b.free(m)
                ww = WW[u % 2]
                for hh in range(2):
                    h = g * 6 + hp * 2 + hh
                    cf, cb_ = c * 48 + h, c * 48 + 24 + h
                    wv = ww[:, hh * P:(hh + 1) * P]
                    m = dve.done(dve.after(m, old.get(("ww", u - 2))).tensor_scalar(wv, dd[:, hh * 256:hh * 256 + P], DT[:, cf:cf + 1], None, ALU.mult))
                    m = dve.done(dve.after(m).scalar_tensor_tensor(out=wv, in0=dd[:, hh * 256 + P:hh * 256 + 256], scalar=DT[:, cb_:cb_ + 1],
                                                                   in1=wv, op0=ALU.mult, op1=ALU.add))
                    m = dve.done(dve.after(m).tensor_tensor(wv, wv, CB[:, g * P:(g + 1) * P], ALU.mult))
                old[("dd", u)] = m
                pe.after(m)
                for hh in range(2):
                    h = g * 6 + hp * 2 + hh
                    last = mm(yb.ap[:, (hp * 2 + hh) * 64:(hp * 2 + hh + 1) * 64], ww[:, hh * P:(hh + 1) * P],
                              XH[:, c, h * 64:(h + 1) * 64], True, True)
                m = pe.done(last)
                old[("ww", u)] = m
            y = Y2[:, c, g * 384:(g + 1) * 384]
            m = dve.done(dve.after(m).tensor_tensor(y, y, yb.ap[:, 0:384], ALU.add))
            yb.free(m)
    smat[0] = 0
    at[0] = base
    fence()
    take(2048 + 1024 + 2 * 1536)
    at2 = at[0]
    take(2 * 1536)
    at3 = at[0]
    at[0] = base
    YT = take(12 * 256).rearrange("p (c t) -> p c t", c=12)
    at[0] = at3
    zz = [take(512) for _ in range(2)]
    sn = take(1536)
    m_sn = broadcast_load(sn, I["ssd_norm_2"][0], 1536)
    for n in range(3):
        w, mw, k = ring.take(("z", n))
        for c in range(2):
            b, m = project(w, [mw], HT, c)
            last = m
            m = act.done(act.after(m, dve.mark()).activation(zz[c], b.ap, ACT.Silu))
            b.free(m)
            y = Y2[:, c, n * 512:n * 512 + 512]
            m = dve.done(dve.after(m).tensor_tensor(y, y, zz[c], ALU.mult))
        ring.free(k, last)
    rs = small(8)
    junk = take(1536)
    m = rstd_of([Y2[:, c, :] for c in range(2)], 1536, [m], rs, junk)
    for c in range(2):
        m = dve.done(dve.after(m, m_sn).scalar_tensor_tensor(out=Y2[:, c, :], in0=Y2[:, c, :], scalar=rs[:, c:c + 1], in1=sn,
                                                             op0=ALU.mult, op1=ALU.mult))
    tm = turn_all(YT, Y2, [0, 1], {0: m, 1: m}, n=12)
    at[0] = base + 12 * 256
    fence(*tm)
    SB = take(2 * D).rearrange("p (c n) -> p c n", c=2)
    FBR = take(2 * D).rearrange("p (c n) -> p c n", c=2)
    UF = take(2 * 512).rearrange("p (c n) -> p c n", c=2)
    V1 = take(4 * 512).rearrange("p (g n) -> p g n", g=4)
    FT = take(4 * 256).rearrange("p (g t) -> p g t", g=4)
    dft = take(1280)
    bgt = take(2 * D)[0:1, :]
    m_df = w_s.sent(nc.gpsimd.dma_start(dft, I["consts"][:, C_DL:C_DL + 1280]))
    m_df = w_s.sent(nc.gpsimd.dma_start(bgt, I["b_gate_2"][0].rearrange("a b -> (a b)").rearrange("(a b) -> a b", a=1)))
    for h in range(2):
        w, mw, k = ring.take(("sso", 0, h))
        w_, mw_, k_ = ring.take(("sso", 1, h))
        for c in range(2):
            b = ps.take()
            pe.after(mw, mw_)
            for kk_ in range(12):
                last = mm(b.ap, YT[:, kk_, c * P:(c + 1) * P], w[:, kk_, :] if kk_ < 8 else w_[:, kk_ - 8, :], kk_ == 0, kk_ == 11)
            m = pe.done(last)
            last = m
            m = evac(SB[:, c, h * 512:h * 512 + 512], b.ap, m)
            b.free(m)
        ring.free(k, last)
        ring.free(k_, last)
    w, mw, k = ring.take(("uf", 0))
    um = []
    for c in range(2):
        b, m = project(w, [mw], HT, c)
        last = m
        m = evac(UF[:, c, :], b.ap, m)
        um.append(m)
        b.free(m)
    ring.free(k, last)
    vm = []
    for g in range(4):
        b = ps.take()
        pe.after(m_df, *um)
        for c in range(2):
            last = mm(b.ap, UF[:, c, g * P:(g + 1) * P], dft[:, c * 512:c * 512 + 512], c == 0, c == 1)
        m = pe.done(last)
        m = evac(V1[:, g, :], b.ap, m)
        vm.append(m)
        b.free(m)
    fmk = []
    for g in range(4):
        b = ps.take()
        pe.after(*vm)
        for c in range(2):
            last = mm(b.ap[:, 0:256], dft[:, 1024 + c * P:1024 + (c + 1) * P], V1[:, g, c * 256:c * 256 + 256], c == 0, c == 1)
        m = pe.done(last)
        m = evac(FT[:, g, :], b.ap[:, 0:256], m)
        fmk.append(m)
        b.free(m)
    for h in range(2):
        w, mw, k = ring.take(("four", h))
        for c in range(2):
            b, m = project(w, [mw] + fmk, FT, c, K=4)
            last = m
            m = evac(FBR[:, c, h * 512:h * 512 + 512], b.ap, m)
            b.free(m)
        ring.free(k, last)
    fence()
    gt2 = [V1[:, 0, :], V1[:, 1, :]]
    MG = FBR
    for n in (0, 2, 1, 3):
        w, mw, k = ring.take(("gate", n))
        for c in range(2):
            b = ps.take()
            pe.after(mw)
            mm(b.ap, ones[0:1, :], bgt[:, n * 512:n * 512 + 512], True, False)
            for k8 in range(8):
                last = mm(b.ap, HT[:, k8, c * P:(c + 1) * P], w[:, k8, :], False, k8 == 7)
            m = pe.done(last)
            last = m
            m = act.done(act.after(m, dve.mark()).activation(gt2[c], b.ap, ACT.Sigmoid))
            b.free(m)
            sl = slice((n % 2) * 512, (n % 2) * 512 + 512)
            src = (FBR, SB)[n // 2][:, c, sl]
            m = dve.done(dve.after(m).tensor_tensor(src, src, gt2[c], ALU.mult))
            if n >= 2:
                m = dve.done(dve.after(m).tensor_tensor(FBR[:, c, sl], FBR[:, c, sl], src, ALU.add))
        ring.free(k, last)
    MT = YT[:, 0:8, :]
    tm = turn_all(MT, MG, [0, 1], {0: m, 1: m})
    mixed = []
    for h in range(2):
        w, mw, k = ring.take(("wout", h))
        for c in range(2):
            b, m = project(w, [mw] + tm, MT, c)
            last = m
            m = evac(SB[:, c, h * 512:h * 512 + 512], b.ap, m)
            mixed.append(m)
            b.free(m)
        ring.free(k, last)

    def add_normed(src, row, marks, junk, rs):
        m = rstd_of([src[:, c, :] for c in range(2)], D, marks, rs, junk)
        g, mg = spread(row)
        for c in range(2):
            m = dve.done(dve.after(m, mg).scalar_tensor_tensor(out=src[:, c, :], in0=src[:, c, :], scalar=rs[:, c:c + 1],
                                                               in1=g.ap, op0=ALU.mult, op1=ALU.mult))
            m = dve.done(dve.after(m).tensor_tensor(X[:, c, :], X[:, c, :], src[:, c, :], ALU.add))
        g.free(m)

    fence()
    add_normed(SB, 4, mixed, V1.rearrange("p g n -> p (g n)")[:, 0:D], rs)
    at[0] = 0
    smat[0] = 0
    fence()
    rs, rw = small(8), small(8 * 16)
    w_r = w_s.sent(nc.gpsimd.dma_start(rw.rearrange("p (c e) -> p c e", c=8),
                                       I["w_router_2"][0].rearrange("(c p) e -> p c e", p=P)))
    XE = take(8 * 512).rearrange("p (c s) -> p c s", c=8)
    SWT = take(4 * 256).rearrange("p (g t) -> p g t", g=4)
    YE = take(4 * D).rearrange("p (g n) -> p g n", g=4)
    base2 = at[0]
    H = take(2 * D).rearrange("p (c d) -> p c d", c=2)
    HT2 = take(8 * 256).rearrange("p (c t) -> p c t", c=8)
    junk = take(D)
    SS = take(2 * 512).rearrange("p (c e s) -> p c e s", c=2, e=16)
    SW = take(2 * 512).rearrange("p (c e s) -> p c e s", c=2, e=16)
    m16 = take(1024)
    marks = modulated(H, xc, 6, 8, junk, rs)
    tm = turn_all(HT2, H, xc, marks)
    b = ps.take()
    pe.after(w_r, *tm)
    for c in xc:
        for k in range(8):
            last = mm(b.ap[:, c * 16:c * 16 + 16], HT2[:, k, c * P:(c + 1) * P],
                      rw.rearrange("p (c e) -> p c e", c=8)[:, k, :], k == 0, k == 7)
    m = pe.done(last)
    af, rm = small(32), small(2)
    a3 = af.rearrange("p (c e) -> p c e", c=2)
    m = dve.done(dve.after(m).tensor_copy(af, b.ap[:, 0:32]))
    b.free(m)
    dve.done(dve.after().tensor_reduce(rm, a3, AX.X, ALU.max))
    m = dve.done(dve.after().tensor_tensor(a3, a3, rm.unsqueeze(2).to_broadcast([P, 2, 16]), ALU.subtract))
    m = act.done(act.after(m).activation(af, af, ACT.Exp))
    dve.done(dve.after(m).tensor_reduce(rm, a3, AX.X, ALU.add))
    dve.done(dve.after().reciprocal(rm, rm))
    m = dve.done(dve.after().tensor_tensor(a3, a3, rm.unsqueeze(2).to_broadcast([P, 2, 16]), ALU.mult))
    b = ps.take()
    pe.after(m)
    for c in xc:
        last = nc.tensor.transpose(b.ap[0:16, c * P:(c + 1) * P], af[:, c * 16:c * 16 + 16], ident)
    m = pe.done(last)
    wk_, pz, mv = m16[0:16, 0:256], m16[0:16, 256:512], m16[0:16, 512:520]
    m = dve.done(dve.after(m).tensor_copy(wk_, b.ap[0:16, 0:256]))
    b.free(m)
    for r in range(4):
        dve.done(dve.after().max(mv, wk_))
        m = dve.done(dve.after().match_replace(wk_, mv, wk_, -1.0))
    dve.done(dve.after().tensor_scalar(wk_, wk_, 0.0, None, ALU.is_lt))
    dve.done(dve.after().tensor_tensor_scan(pz[:, 0:P], ones[0:16, :], wk_[:, 0:P], 0.0, ALU.mult, ALU.add))
    dve.done(dve.after().tensor_tensor_scan(pz[:, P:256], ones[0:16, :], wk_[:, P:256], pz[:, P - 1:P], ALU.mult, ALU.add))
    dve.done(dve.after().tensor_tensor(pz, pz, wk_, ALU.mult))
    m = dve.done(dve.after().tensor_scalar(pz, pz, 1.0, None, ALU.subtract))
    b = ps.take()
    pe.after(m)
    for c in xc:
        last = nc.tensor.transpose(b.ap[:, c * 16:c * 16 + 16], pz[:, c * P:(c + 1) * P], ident[0:16, 0:16])
    m = pe.done(last)
    pt = small(32)
    m = dve.done(dve.after(m).tensor_copy(pt, b.ap[:, 0:32]))
    b.free(m)
    for c in xc:
        m = dve.done(dve.after(m).tensor_tensor(
            SS[:, c, :, :], KC[:, C_IOTA:C_IOTA + 32].unsqueeze(1).to_broadcast([P, 16, 32]),
            pt[:, c * 16:c * 16 + 16].unsqueeze(2).to_broadcast([P, 16, 32]), ALU.is_equal))
        m = dve.done(dve.after(m).tensor_tensor(
            SW[:, c, :, :], SS[:, c, :, :], a3[:, c, :].unsqueeze(2).to_broadcast([P, 16, 32]), ALU.mult))
    fence()
    for k in range(8):
        b = ps.take()
        for c in xc:
            last = mm(b.ap, H[:, c, k * P:(k + 1) * P], SS[:, c, :, :].rearrange("p e s -> p (e s)"), c == 0, c == 1)
        m = pe.done(last)
        m = evac(XE[:, k, :], b.ap, m)
        b.free(m)
    for c in xc:
        turned(SWT[:, :, c * P:(c + 1) * P], SW[:, c, :, :].rearrange("p e s -> p (e s)"), 4, None)
    at[0] = base2
    fence()
    hid = [take(D) for _ in range(2)]
    hidT = [take(D).rearrange("p (c s) -> p c s", c=8) for _ in range(2)]
    for g in range(4):
        i = g % 2
        bg, bu = ps.take(2), ps.take(2)
        for j in range(4):
            e = 4 * g + j
            pr = slice(32 * j, 32 * j + 32)
            for h in range(2):
                sl = slice(h * 512, h * 512 + 512)
                for mt, bb in (("g", bg), ("u", bu)):
                    w, mw, k = ring.take((2, e, mt, h))
                    pe.after(mw)
                    for c in range(8):
                        last = mm(bb.ap[pr, sl], XE[:, c, e * 32:e * 32 + 32], w[:, c, :], c == 0, c == 7)
                    m = pe.done(last)
                    ring.free(k, m)
        m_u = m
        m = act.done(act.after(m).activation(hid[i], bg.ap, ACT.Silu))
        bg.free(m)
        m = dve.done(dve.after(m, m_u).tensor_tensor(hid[i], hid[i], bu.ap, ALU.mult))
        bu.free(m)
        last_marks.clear()
        turned(hidT[i], hid[i], 8, m)
        hm_ = list(last_marks)
        for h in range(2):
            sl = slice(h * 512, h * 512 + 512)
            b = ps.take()
            pe.after(*hm_)
            for j in range(4):
                w, mw, k = ring.take((2, 4 * g + j, "d", h))
                pe.after(mw)
                for c in range(8):
                    last = mm(b.ap[32 * j:32 * j + 32, :], hidT[i][:, c, 32 * j:32 * j + 32], w[:, c, :], c == 0, c == 7)
                m = pe.done(last)
                ring.free(k, m)
            m = evac(YE[:, g, sl], b.ap, m)
            b.free(m)
    fence()
    F2 = XE.rearrange("p c s -> p (c s)")[:, 0:2 * D].rearrange("p (c n) -> p c n", c=2)
    fm_ = []
    for c in xc:
        for h in range(2):
            b = ps.take()
            for g in range(4):
                last = mm(b.ap, SWT[:, g, c * P:(c + 1) * P], YE[:, g, h * 512:h * 512 + 512], g == 0, g == 3)
            m = pe.done(last)
            m = evac(F2[:, c, h * 512:h * 512 + 512], b.ap, m)
            fm_.append(m)
            b.free(m)
    add_normed(F2, 10, fm_, hid[0], rs)
    fence()
    finish(None)


_INS = ['x', 'c', 'ctx', 'c_ctx', 'ada_w', 'ada_b', 'norm_mix_g', 'norm_ffn_g', 'even_w_in', 'even_w_out',
        'hgrn_lb_logits', 'hgrn_onorm_g', 'diff_lambda', 'diff_subln_g', 'odd_w_qkv', 'odd_w_out', 'swa_sink',
        'router_w', 'router_b', 'moe_w_gate', 'moe_w_up', 'moe_w_down', 'final_norm_g', 'c_2', 'ctx_2', 'c_ctx_2',
        'w_mod_2', 'b_mod_2', 'norm_mix_pre_2', 'norm_mix_post_2', 'norm_ffn_pre_2', 'norm_ffn_post_2', 'w_in_2',
        'conv_w_2', 'conv_b_2', 'dt_bias_2', 'a_log_2', 'd_skip_2', 'ssd_norm_2', 'w_fourier_2', 'w_ssd_out_2',
        'b_gate_2', 'w_out_2', 'w_router_2', 'w_e_gate_2', 'w_e_up_2', 'w_e_down_2']


def kernel(**inputs):
    import concourse.bacc as _bacc
    from concourse.bass_utils import run_bass_kernel_spmd as _run

    nc = _bacc.Bacc("TRN2", target_bir_lowering=False, num_devices=1)
    arrays, ins = {}, {}
    for name in _INS + ["consts"]:
        a = constants() if name == "consts" else np.ascontiguousarray(inputs[name])
        arrays[f"in_{name}"] = a
        ins[name] = nc.dram_tensor(f"in_{name}", a.shape, F32, kind="ExternalInput").ap()
    out = nc.dram_tensor("out_0", (1, 256, 1024), F32, kind="ExternalOutput").ap()
    program(nc, ins, out)
    r = _run(nc, [arrays], core_ids=[0])
    return r.results[0]["out_0"]
```

```python
import math
from contextlib import ExitStack

import numpy as np
import concourse.bass as bass
from concourse import mybir

P = 128
D = 1024
NS = 5
SLOT = 8 * 512
F32 = mybir.dt.float32
U32 = mybir.dt.uint32
I32 = mybir.dt.int32
ALU = mybir.AluOpType
ACT = mybir.ActivationFunctionType
AX = mybir.AxisListType
EPS = 1e-6
BIG = 1e30
XROWS = 23 * P

C_ID, C_LE, C_LT, C_GE, C_COS, C_SIN, C_ROT, C_NF, C_NB = 0, 128, 256, 384, 512, 768, 1024, 1152, 1280
C_IOTA, C_ONE, C_EX, C_GW, C_REP, C_SUM = 1408, 1440, 1441, 1457, 1461, 1473
C_KEEP = 1485
C_LEV = 1488
C_SWA = C_LEV + 15 * 128
C_DL = C_SWA + 1024
C_DW = C_DL + 1024
C_END = C_DW + 256


def constants():
    c = np.zeros((P, C_END), np.float32)
    i = np.arange(P)
    c[:, C_ID:C_ID + P] = np.eye(P)
    c[:, C_LE:C_LE + P] = i[:, None] <= i[None]
    c[:, C_LT:C_LT + P] = i[:, None] < i[None]
    c[:, C_GE:C_GE + P] = i[:, None] >= i[None]
    c[:, C_NF:C_NF + P] = np.where(i[:, None] <= i[None], 0, -BIG)
    c[:, C_NB:C_NB + P] = np.where(i[:, None] >= i[None], 0, -BIG)
    t = np.arange(256)
    inv = (1.0 / (np.float32(10000.0) ** (np.arange(0, 32, 2, dtype=np.float32) / np.float32(32)))).astype(np.float32)
    ar = (t // 64).astype(np.float32)[:, None] * inv
    ac = (t % 64).astype(np.float32)[:, None] * inv
    ang = np.concatenate([ar, ar, ac, ac], axis=-1).astype(np.float32)
    c[:, C_COS:C_COS + 256] = np.tile(np.cos(ang).T, (2, 1))
    c[:, C_SIN:C_SIN + 256] = np.tile(np.sin(ang).T, (2, 1))
    r = np.zeros((P, P), np.float32)
    for b in range(0, P, 32):
        for j in range(16):
            r[b + j, b + 16 + j] = -1
            r[b + 16 + j, b + j] = 1
    c[:, C_ROT:C_ROT + P] = r.T
    c[:, C_IOTA:C_IOTA + 32] = np.arange(32)
    c[[2, 3, 8, 9], C_ONE] = 1
    c[:, C_EX:C_EX + 16] = np.arange(16)
    c[:, C_GW:C_GW + 4] = [4, 3, 2, 1]
    for j in range(6):
        c[j, C_REP + 2 * j:C_REP + 2 * j + 2] = 1
    for q in range(4):
        c[32 * q:32 * q + 12, C_SUM:C_SUM + 12] = np.eye(12)
    lev = []
    for b in (64, 32, 16, 8, 4, 2, 1):
        lev.append((i[:, None] // (2 * b) == i[None] // (2 * b)) & (i[:, None] // b % 2 == 0) & (i[None] // b % 2 == 1))
    allm = lev + [m.T for m in lev] + [np.eye(P, dtype=bool)]
    for n, m in enumerate(allm):
        c[:, C_LEV + n * P:C_LEV + (n + 1) * P] = m
    for q in range(2):
        ok = np.abs((q * P + i)[:, None] - t[None]) <= 128
        c[:, C_SWA + q * 512:C_SWA + q * 512 + 256] = np.where(ok, 0, -BIG)
    ll = 2 * np.pi * (np.outer(t, t) % 256) / 256
    s = 1 / math.sqrt(256 * 128)
    for q in range(2):
        c[:, C_DL + q * 512:C_DL + q * 512 + 256] = (np.cos(ll) * s)[q * P:(q + 1) * P]
        c[:, C_DL + q * 512 + 256:C_DL + (q + 1) * 512] = (np.sin(ll) * s)[q * P:(q + 1) * P]
    lw = 2 * np.pi * (np.outer(i, i) % 128) / 128
    c[:, C_DW:C_DW + P] = np.cos(lw)
    c[:, C_DW + P:C_DW + 2 * P] = -np.sin(lw)
    return c


PHASES = []


class Lane:

    def __init__(self, eng, sem, own):
        self.eng, self.sem, self.n, self.own, self.met = eng, sem, 0, own, {}

    def after(self, *marks):
        for m in marks + ((self.mark(),) if self.own and self.n else ()):
            if m is not None and self.met.get(m[0], 0) < m[2]:
                self.eng.wait_ge(m[1], m[2])
                self.met[m[0]] = m[2]
        return self.eng

    def done(self, ins):
        ins.then_inc(self.sem, 1)
        self.n += 1
        return self.mark()

    def mark(self):
        return (id(self.sem), self.sem, self.n)


class Wire:

    def __init__(self, sem):
        self.sem, self.n = sem, 0

    def sent(self, ins):
        ins.then_inc(self.sem, 16)
        self.n += 16
        return (id(self.sem), self.sem, self.n)


class Banks:

    def __init__(self, ap, lane):
        self.ap, self.lane, self.at, self.freed = ap, lane, 0, [()] * 8

    def take(self, n=1):
        at = -(-self.at // n) * n % 8
        for _ in range(8 // n):
            if all(self.freed[b] is not None for b in range(at, at + n)):
                break
            at = (at + n) % 8
        self.at = (at + n) % 8
        for b in range(at, at + n):
            assert self.freed[b] is not None, "bank in use"
            self.lane.after(*self.freed[b])
            self.freed[b] = None
        return Bank(self, at, n)


class Bank:
    def __init__(self, banks, at, n):
        self.banks, self.at, self.n = banks, at, n
        self.ap = banks.ap[:, at * 512:(at + n) * 512]

    def free(self, *marks):
        for b in range(self.at, self.at + self.n):
            self.banks.freed[b] = marks


class Ring:

    def __init__(self, ap, lane, sems, plan, ends):
        self.ap, self.lane, self.plan, self.ends = ap, lane, plan, sorted(ends)
        self.wires = [Wire(s) for s in sems]
        self.marks, self.at, self.used = {}, 0, {}
        for n in range(NS):
            self.send(n)

    def send(self, n, *marks):
        if n >= self.ends[0]:
            return
        _, src, k, cols = self.plan[n]
        dst = self.slot(n)[:, 0:k, 0:cols]
        self.lane.after(*marks)
        self.marks[n] = self.wires[n % NS].sent(self.lane.eng.dma_start(dst, src))

    def slot(self, n):
        return self.ap[:, n % NS, :].rearrange("p (c n) -> p c n", c=8)

    def take(self, key):
        n = self.at
        assert self.plan[n][0] == key, (self.plan[n][0], key)
        self.at += 1
        return self.slot(n), self.marks[n], n

    def free(self, n, mark):
        self.send(n + NS, mark)

    def resume(self, *marks):
        n = self.ends.pop(0)
        assert self.at == n
        for i in range(n, n + NS):
            self.send(i, *marks)


def program(nc, I, out, upto=3):
    ctx = ExitStack()
    sb = lambda name, shape, dt=F32: ctx.enter_context(nc.sbuf_tensor(name, shape, dt))
    sem = lambda name: ctx.enter_context(nc.semaphore(name))
    pe = Lane(nc.tensor, sem("s_pe"), False)
    dve = Lane(nc.vector, sem("s_dve"), True)
    act = Lane(nc.scalar, sem("s_act"), True)
    pool = Lane(nc.gpsimd, sem("s_pool"), True)
    sp = Lane(nc.sync, sem("s_sp"), False)

    ringt = sb("ring", [P, NS, SLOT])
    X = sb("X", [P, 4, D])
    MOD = sb("MOD", [12, D])
    KC = sb("KC", [P, C_KEEP])
    ones = sb("ones", [P, P])
    CT = sb("CT", [P, 32])
    CP = sb("CP", [P, 2, 8, 42])
    SM = sb("SM", [P, 2304])
    RT = sb("RT", [P, 8, 16])
    DST = sb("DST", [P, 8], U32)
    OE = sb("OE", [1, 16], I32)
    ar_words = 22760
    AR = sb("AR", [P, ar_words])
    PSt = ctx.enter_context(nc.psum_tensor("PS", [P, 4096], F32))
    ps = Banks(PSt[:, :], pe)
    XP = nc.dram_tensor("XP", [XROWS, D], F32).ap()
    YP = nc.dram_tensor("YP", [XROWS, D], F32).ap()

    M1 = nc.dram_tensor("M1", [12, D], F32).ap()
    M2 = nc.dram_tensor("M2", [12, D], F32).ap()
    HD = nc.dram_tensor("HD", [P, 8 * 512], F32).ap()
    ident = KC[:, C_ID:C_ID + P]
    at = [0]

    def phase(name):
        PHASES.append((name, nc.n_instructions if isinstance(nc.n_instructions, int) else nc.n_instructions()))

    def take(n):
        a = at[0]
        at[0] += n
        assert at[0] <= ar_words, at[0]
        return AR[:, a:a + n]

    smat = [0]

    def small(n):
        a = smat[0]
        smat[0] += n
        assert smat[0] <= 2304, smat[0]
        return SM[:, a:a + n]

    def fence(*more):
        marks = [x.mark() for x in (pe, dve, act, pool) if x.n] + list(more)
        for x in (pe, dve, act, pool):
            x.after(*marks)
        return marks

    def mm(o, l, r, start, stop, **kw):
        return nc.tensor.matmul(o, l, r, start=start, stop=stop, **kw)

    flip = [0]

    def evac(dst, src, *marks):
        flip[0] ^= 1
        if flip[0]:
            return dve.done(dve.after(*marks).tensor_copy(dst, src))
        return act.done(act.after(*marks).copy(dst, src))

    def cols(w, n, k0=0, k=8, width=512):
        return w[k0:k0 + k * P, n:n + width].rearrange("(c p) n -> p c n", p=P)

    plan = []

    def add(key, src, k=8, width=512):
        plan.append((key, src, k, width))

    ada, win, wo = I["ada_w"], I["even_w_in"][0], I["even_w_out"][0]
    moe = {"g": I["moe_w_gate"], "u": I["moe_w_up"], "d": I["moe_w_down"]}

    def add_ada(tag, w):
        for h in range(2):
            for j in range(6):
                add((tag, j, h), cols(w, 1024 * j + 512 * h))

    def add_moe(layer, order):
        for e in range(16):
            for m, h in order:
                add((layer, e, m, h), cols(moe[m][layer, e], 512 * h))
        ends.append(len(plan))

    ends = []
    WIDE = (("g", 0), ("u", 0), ("g", 1), ("u", 1), ("d", 0), ("d", 1))
    PAIRS = (("g", 0), ("g", 1), ("u", 0), ("u", 1), ("d", 0), ("d", 1))
    add_ada("ada0", ada[0])
    for n in range(4):
        add(("in", n), cols(win, 512 * n))
    add_ada("ada1", ada[1])
    add_ada("ada2", I["w_mod_2"][0])
    for n in range(4, 8):
        add(("in", n), cols(win, 512 * n))
    for n in range(2):
        add(("wo", n), cols(wo, 512 * n))
    add_moe(0, WIDE)
    cut = {1: len(plan)}
    for n in range(3):
        add(("qkv", n), cols(I["odd_w_qkv"][0], 512 * n))
    for n in range(2):
        add(("owo", n), cols(I["odd_w_out"][0], 512 * n))
    add_moe(1, PAIRS)
    cut[2] = len(plan)
    w2 = I["w_in_2"][0]
    for n in range(5):
        add(("xbc", n), cols(w2, 2048 + 512 * n))
    add(("dt", 0), cols(w2, 4608, width=48), width=48)
    for n in range(3):
        add(("z", n), cols(w2, 512 + 512 * n))
    for h in range(2):
        add(("sso", 0, h), cols(I["w_ssd_out_2"][0], 512 * h))
        add(("sso", 1, h), cols(I["w_ssd_out_2"][0], 512 * h, k0=1024, k=4), k=4)
    add(("uf", 0), cols(w2, 0))
    for h in range(2):
        add(("four", h), cols(I["w_fourier_2"][0], 512 * h, k=4), k=4)
    for n in (0, 2, 1, 3):
        add(("gate", n), cols(w2, 4656 + 512 * n))
    for h in range(2):
        add(("wout", h), cols(I["w_out_2"][0], 512 * h))
    for g in range(4):
        for e in range(4 * g, 4 * g + 4):
            for m, h in (("g", 0), ("u", 0), ("g", 1), ("u", 1)):
                add((2, e, m, h), cols(I["w_e_gate_2" if m == "g" else "w_e_up_2"][0, e], 512 * h))
        for h in range(2):
            for e in range(4 * g, 4 * g + 4):
                add((2, e, "d", h), cols(I["w_e_down_2"][0, e], 512 * h))

    if upto in cut:
        del plan[cut[upto]:]
    ends.append(len(plan))

    phase("start")
    w_x, w_k, w_c, w_s = Wire(sem("w_x")), Wire(sem("w_k")), Wire(sem("w_c")), Wire(sem("w_s"))
    w_x2, w_m, w_t, w_h = Wire(sem("w_x2")), Wire(sem("w_m")), Wire(sem("w_t")), Wire(sem("w_h"))
    w_v, w_vx, w_vy = [Wire(sem(f"w_v{n}")) for n in range(NS)], Wire(sem("w_vx")), Wire(sem("w_vy"))
    w_z, w_xe = Wire(sem("w_z")), [Wire(sem("w_xe0")), Wire(sem("w_xe1"))]
    w_sc, w_y, w_g, w_o = Wire(sem("w_sc")), [Wire(sem("w_y0")), Wire(sem("w_y1"))], Wire(sem("w_g")), Wire(sem("w_o"))
    crow = AR[0:32, 0:P]
    for n, name in enumerate(("c", "c_ctx", "c_2", "c_ctx_2")):
        v = I[name] if name in ("c_ctx", "c_ctx_2") else I[name][0]
        mc = w_c.sent(nc.scalar.dma_start(AR[8 * n:8 * n + 8, 0:P], v.rearrange("(a b) -> a b", b=P)))
    mk = w_k.sent(nc.scalar.dma_start(KC[:, :], I["consts"][:, 0:C_KEEP]))
    mx = w_x.sent(nc.scalar.dma_start(X[:, 0:2, :], I["x"][0].rearrange("(c p) d -> p c d", p=P)))
    mx = w_x.sent(nc.scalar.dma_start(X[:, 2:4, :], I["ctx"][0].rearrange("(c p) d -> p c d", p=P)))
    ring = Ring(ringt, sp, [sem(f"w_r{n}") for n in range(NS)], plan, ends)

    m_one = dve.done(dve.after().memset(ones[:, :], 1.0))
    m_cp = dve.done(dve.after().memset(CP[:, :, :, :], 0.0))
    b = ps.take()
    pe.after(mc, mk)
    m = pe.done(nc.tensor.transpose(b.ap[:, 0:32], crow, ident[0:32, 0:32]))
    m = act.done(act.after(m).activation(CT[:, :], b.ap[:, 0:32], ACT.Silu))
    b.free(m)
    for half in range(2):
        for r in range(2):
            m_cp = dve.done(dve.after(m, m_cp).tensor_copy(
                CP[:, half, :, 10 + r], CT[:, 16 * half + 8 * r:16 * half + 8 * r + 8]))
    fence(mx, mk)

    mod_last = [None]

    def modulation(tag, half, bias, gains, place, dst):
        sums, GB, br = place[:, 0:512], place[0:12, 512:1024], place[0:6, 1024:1536]
        m = mb = mod_last[0]
        for h in range(2):
            sl = slice(512 * h, 512 * h + 512)
            pool.after(m, mb)
            mg = pool.done(pool.eng.memset(GB, 1.0))
            pool.after(mg)
            mb = w_s.sent(nc.gpsimd.dma_start(br, bias.rearrange("(a b) -> a b", b=D)[:, sl]))
            for row, g in gains:
                for r in range(2):
                    mb = w_s.sent(nc.gpsimd.dma_start(GB[row + r:row + r + 1, :], g.rearrange("(a b) -> a b", a=1)[:, sl]))
            b = ps.take()
            for j in range(6):
                w, mw, k = ring.take((tag, j, h))
                pe.after(mw)
                for c in range(8):
                    q = c % 4
                    last = mm(b.ap[32 * q:32 * q + 32, :], CP[:, half, c, 10 - 2 * j:42 - 2 * j], w[:, c, :],
                              j == 0 and c < 4, j == 5 and c > 3, skip_group_check=True)
                m2 = pe.done(last)
                ring.free(k, m2)
                yield
            m = dve.done(dve.after(m2, m).tensor_copy(sums, b.ap))
            b.free(m)
            b = ps.take()
            pe.after(m, mb)
            mm(b.ap[0:12, :], KC[:, C_SUM:C_SUM + 12], sums, True, False)
            m = pe.done(mm(b.ap[0:12, :], KC[0:6, C_REP:C_REP + 12], br, False, True))
            o = MOD[:, sl] if dst is None else GB
            m = dve.done(dve.after(m).scalar_tensor_tensor(
                out=o, in0=b.ap[0:12, :], scalar=KC[0:12, C_ONE:C_ONE + 1], in1=GB, op0=ALU.add, op1=ALU.mult))
            b.free(m)
            if dst is not None:
                act.after(m)
                mod_last[0] = m = w_m.sent(nc.scalar.dma_start(dst[:, sl], GB))
            yield

    def fetch_modulation(src):
        fence()
        pool.after(mod_kept)
        fence(w_s.sent(nc.gpsimd.dma_start(MOD[:, :], src)))

    def in_turns(*parts):
        parts = list(parts)
        while parts:
            for g in list(parts):
                for _ in g:
                    break
                else:
                    parts.remove(g)

    def every(n, g):
        for _ in g:
            for _ in range(n):
                yield

    def spread(row):
        b = ps.take(2)
        for h in range(2):
            last = mm(b.ap[:, h * 512:h * 512 + 512], ident[0:12, row:row + 1].to_broadcast([12, P]),
                      MOD[:, h * 512:h * 512 + 512], True, True)
        return b, pe.done(last)

    def rstd_of(srcs, width, marks, rs, junk):
        for n, s in enumerate(srcs):
            m = act.done(act.after(*marks).activation(junk, s, ACT.Square, accum_out=rs[:, n:n + 1]))
        n = len(srcs)
        m = dve.done(dve.after(m).tensor_scalar(rs[:, 0:n], rs[:, 0:n], 1.0 / width, EPS, ALU.mult, ALU.add))
        m = act.done(act.after(m).activation(rs[:, 0:n], rs[:, 0:n], ACT.Sqrt))
        return dve.done(dve.after(m).reciprocal(rs[:, 0:n], rs[:, 0:n]))

    def modulated(H, chunks, shift, scale, junk, rs):
        m = rstd_of([X[:, c, :] for c in chunks], D, [dve.mark()], rs, junk)
        marks = {}
        for r in range(2):
            mine = [c for c in chunks if c // 2 == r]
            if not mine:
                continue
            a, ma = spread(scale + r)
            s, ms = spread(shift + r)
            for c in mine:
                n = chunks.index(c)
                m = dve.done(dve.after(m, ma).scalar_tensor_tensor(
                    out=H[:, c, :], in0=X[:, c, :], scalar=rs[:, n:n + 1], in1=a.ap, op0=ALU.mult, op1=ALU.mult))
                m = dve.done(dve.after(m, ms).tensor_tensor(H[:, c, :], H[:, c, :], s.ap, ALU.add))
                marks[c] = m
            a.free(m)
            s.free(m)
        return marks

    def turned(dst, src, n, mark):
        for j in range(0, n, 4):
            b = ps.take()
            pe.after(mark)
            for i in range(j, min(n, j + 4)):
                last = nc.tensor.transpose(b.ap[:, (i - j) * P:(i - j + 1) * P], src[:, i * P:(i + 1) * P], ident)
            m = pe.done(last)
            k = min(4, n - j)
            m = evac(dst[:, j:j + k, :], b.ap[:, 0:k * P].rearrange("p (a b) -> p a b", a=k), m)
            b.free(m)
            last_marks.append(m)
        return m

    last_marks = []

    def turn_all(HT, H, chunks, marks, n=8):
        last_marks.clear()
        for c in chunks:
            turned(HT[:, :, c * P:(c + 1) * P], H[:, c, :], n, marks[c])
        out_marks = list(last_marks)
        return out_marks

    def project_T(w, mw, j, HT, t0, t1, M=P, out_p=0, bank=None, wcols=None):
        b = ps.take()
        pe.after(*mw)
        for c in range(8):
            last = mm(b.ap[:, 0:t1 - t0], w[:, c, j * P:(j + 1) * P], HT[:, c, t0:t1], c == 0, c == 7)
        return b, pe.done(last)

    def project(w, mw, HT, c, width=512, K=8):
        b = ps.take()
        pe.after(*mw)
        for k in range(K):
            last = mm(b.ap[:, 0:width], HT[:, k, c * P:(c + 1) * P], w[:, k, 0:width], k == 0, k == K - 1)
        return b, pe.done(last)

    def add_branch(keys, YT, chunks, gate_row, marks, tmp):
        gates = {}
        for r in sorted({c // 2 for c in chunks}):
            g, mg = spread(gate_row + r)
            dst = tmp[r]
            m = dve.done(dve.after(mg).tensor_copy(dst, g.ap))
            g.free(m)
            gates[r] = m
        for h, key in enumerate(keys):
            w, mw, k = ring.take(key)
            for c in chunks:
                b, m = project(w, [mw] + marks, YT, c)
                last = m
                sl = slice(h * 512, h * 512 + 512)
                m = dve.done(dve.after(m, gates[c // 2]).tensor_tensor(tmp[2], b.ap, tmp[c // 2][:, sl], ALU.mult))
                b.free(m)
                m = dve.done(dve.after(m).tensor_tensor(X[:, c, sl], X[:, c, sl], tmp[2], ALU.add))
            ring.free(k, last)

    def rope(dst, raw, marks):
        b = ps.take()
        pe.after(*marks)
        m = pe.done(mm(b.ap[:, 0:256], KC[:, C_ROT:C_ROT + P], raw, True, True))
        t = rtmp
        m = dve.done(dve.after(m).tensor_tensor(t, b.ap[:, 0:256], KC[:, C_SIN:C_SIN + 256], ALU.mult))
        b.free(m)
        m = dve.done(dve.after(m).tensor_tensor(dst, raw, KC[:, C_COS:C_COS + 256], ALU.mult))
        return dve.done(dve.after(m).tensor_tensor(dst, dst, t, ALU.add))

    def softmax_tail(o, a, ):
        pass

    def broadcast_load(dst, src, n):
        return w_s.sent(nc.gpsimd.dma_start(dst, src.rearrange("(a b) -> a b", a=1).to_broadcast([P, n])))

    def routed(layer, chunks, BL):
        nover = 7
        phase("route%d" % layer)
        at[0] = 0
        smat[0] = 0
        fence()
        nch = len(chunks)
        nb = 16 + nover
        rs, rb, rw = small(8), small(16), small(8 * 16)
        w_r = w_s.sent(nc.gpsimd.dma_start(rw.rearrange("p (c e) -> p c e", c=8),
                                           I["router_w"].rearrange("(c p) e -> p c e", p=P)))
        w_r = broadcast_load(rb, I["router_b"], 16)
        H = take(4 * D).rearrange("p (c d) -> p c d", c=4)
        HT = take(8 * 512).rearrange("p (c t) -> p c t", c=8)
        junk = take(D)
        marks = modulated(H, chunks, 6, 8, junk, rs)
        tm = turn_all(HT, H, chunks, marks)
        N = nch * 16
        b = ps.take()
        pe.after(w_r, *tm)
        for i, c in enumerate(chunks):
            for k in range(8):
                last = mm(b.ap[:, i * 16:i * 16 + 16], HT[:, k, c * P:(c + 1) * P],
                          rw.rearrange("p (c e) -> p c e", c=8)[:, k, :], k == 0, k == 7)
        m = pe.done(last)
        aff, sel, o1, o2, t1, t2 = (small(N) for _ in range(6))
        m = act.done(act.after(m).activation(aff, b.ap[:, 0:N], ACT.Sigmoid))
        b.free(m)
        v3 = lambda a: a.rearrange("p (c e) -> p c e", e=16)
        g4 = lambda a: a.rearrange("p (g e) -> p g e", e=4)
        D_ = lambda ins: dve.done(ins)
        dve.after(m, w_r)
        D_(dve.after().tensor_tensor(v3(sel), v3(aff), rb.unsqueeze(1).to_broadcast([P, nch, 16]), ALU.add))
        G = nch * 4
        hi, lo, mid, gs, gt = small(2 * G), small(2 * G), small(G), small(G), small(G)
        s4 = g4(sel)
        h2, l2 = hi.rearrange("p (g e) -> p g e", e=2), lo.rearrange("p (g e) -> p g e", e=2)
        D_(dve.after().tensor_tensor(h2, s4[:, :, 0:2], s4[:, :, 2:4], ALU.max))
        D_(dve.after().tensor_tensor(l2, s4[:, :, 0:2], s4[:, :, 2:4], ALU.min))
        D_(dve.after().tensor_tensor(gs, h2[:, :, 0], h2[:, :, 1], ALU.max))
        D_(dve.after().tensor_tensor(mid, h2[:, :, 0], h2[:, :, 1], ALU.min))
        D_(dve.after().tensor_tensor(gt, l2[:, :, 0], l2[:, :, 1], ALU.max))
        D_(dve.after().tensor_tensor(mid, mid, gt, ALU.max))
        D_(dve.after().tensor_tensor(gs, gs, mid, ALU.add))
        red = small(nch)
        c4 = lambda a: a.rearrange("p (c g) -> p c g", g=4)

        def first_of_max(dst, val, weights, view, k):
            D_(dve.after().tensor_reduce(red, view(val), AX.X, ALU.max))
            D_(dve.after().tensor_tensor(view(dst), view(val), red.unsqueeze(2).to_broadcast([P, nch, k]), ALU.is_equal))
            D_(dve.after().tensor_tensor(view(dst), view(dst), weights.unsqueeze(1).to_broadcast([P, nch, k]), ALU.mult))
            D_(dve.after().tensor_reduce(red, view(dst), AX.X, ALU.max))
            return D_(dve.after().tensor_tensor(view(dst), view(dst), red.unsqueeze(2).to_broadcast([P, nch, k]), ALU.is_equal))

        first_of_max(gt, gs, KC[:, C_GW:C_GW + 4], c4, 4)
        D_(dve.after().tensor_scalar(gt, gt, 1.0, 2 * BIG, ALU.subtract, ALU.mult))
        D_(dve.after().tensor_tensor(g4(t1), g4(sel), gt.unsqueeze(2).to_broadcast([P, G, 4]), ALU.add))
        ew = small(16)
        D_(dve.after().tensor_scalar(ew, KC[:, C_EX:C_EX + 16], -1.0, 16.0, ALU.mult, ALU.add))
        first_of_max(o1, t1, ew, v3, 16)
        D_(dve.after().scalar_tensor_tensor(out=t1, in0=o1, scalar=-4 * BIG, in1=t1, op0=ALU.mult, op1=ALU.add))
        first_of_max(o2, t1, ew, v3, 16)
        wk = [small(nch), small(nch)]
        den = small(nch)
        for k, o in enumerate((o1, o2)):
            D_(dve.after().tensor_tensor(t2, o, aff, ALU.mult))
            D_(dve.after().tensor_reduce(wk[k], v3(t2), AX.X, ALU.add))
        D_(dve.after().tensor_tensor(den, wk[0], wk[1], ALU.add))
        D_(dve.after().reciprocal(den, den))
        for k in range(2):
            D_(dve.after().tensor_tensor(wk[k], wk[k], den, ALU.mult))
        M = small(N)
        m = D_(dve.after().tensor_tensor(M, o1, o2, ALU.add))
        b = ps.take()
        pe.after(m)
        for i in range(nch):
            for j in range(i):
                mm(b.ap[:, i * 16:i * 16 + 16], ones[:, :], M[:, j * 16:j * 16 + 16], j == 0, False)
            mm(b.ap[:, i * 16:i * 16 + 16], KC[:, C_LT:C_LT + P], M[:, i * 16:i * 16 + 16], i == 0, True)
        for j in range(nch):
            last = mm(b.ap[:, 64:80], ones[:, :], M[:, j * 16:j * 16 + 16], j == 0, j == nch - 1)
        m = pe.done(last)
        pos, blk, tt, cnt, inc, exc = small(N), small(N), small(N), small(16), small(16), small(16)
        D_(dve.after(m).tensor_copy(pos, b.ap[:, 0:N]))
        m = D_(dve.after().tensor_copy(cnt, b.ap[:, 64:80]))
        b.free(m)
        D_(dve.after().tensor_scalar(exc, cnt, float(BL), None, ALU.is_gt))
        for q in (2.0 * BL, 3.0 * BL):
            D_(dve.after().scalar_tensor_tensor(out=exc, in0=cnt, scalar=q, in1=exc, op0=ALU.is_gt, op1=ALU.add))
        D_(dve.after().tensor_tensor_scan(inc, ones[:, 0:16], exc, 0.0, ALU.mult, ALU.add))
        D_(dve.after().tensor_tensor(exc, inc, exc, ALU.subtract))
        D_(dve.after().tensor_scalar(blk, pos, float(BL), None, ALU.is_ge))
        for q in (2.0 * BL, 3.0 * BL):
            D_(dve.after().scalar_tensor_tensor(out=blk, in0=pos, scalar=q, in1=blk, op0=ALU.is_ge, op1=ALU.add))
        e3 = KC[:, C_EX:C_EX + 16].unsqueeze(1).to_broadcast([P, nch, 16])
        D_(dve.after().tensor_tensor(v3(tt), v3(blk), e3, ALU.subtract))
        D_(dve.after().tensor_tensor(v3(t1), v3(tt), exc.unsqueeze(1).to_broadcast([P, nch, 16]), ALU.add))
        D_(dve.after().tensor_scalar(t1, t1, 15.0, None, ALU.add))
        D_(dve.after().tensor_scalar(t2, blk, 0.0, None, ALU.is_gt))
        D_(dve.after().tensor_tensor(t1, t1, t2, ALU.mult))
        D_(dve.after().tensor_tensor(t1, t1, tt, ALU.subtract))
        D_(dve.after().scalar_tensor_tensor(out=t1, in0=t1, scalar=float(BL), in1=pos, op0=ALU.mult, op1=ALU.add))
        rowf = small(2 * nch)
        for k, o in enumerate((o1, o2)):
            D_(dve.after().tensor_tensor(t2, o, t1, ALU.mult))
            D_(dve.after().tensor_reduce(rowf[:, k * nch:(k + 1) * nch], v3(t2), AX.X, ALU.add))
        m_dst = D_(dve.after().tensor_copy(DST[:, 0:2 * nch], rowf))
        oe = small(16)
        for j in range(nover):
            D_(dve.after().tensor_scalar(t2[:, 0:16], inc, float(j), None, ALU.is_le))
            D_(dve.after().tensor_reduce(oe[:, j:j + 1], t2[:, 0:16], AX.X, ALU.add))
        D_(dve.after().tensor_scalar(oe[:, 0:nover], oe[:, 0:nover], 15.0, None, ALU.min))
        D_(dve.after().tensor_copy(OE[0:1, 0:nover], oe[0:1, 0:nover]))
        m_oe = D_(dve.after().tensor_copy(OE[0:1, 8:9], inc[0:1, 15:16]))
        pool.after(m_dst, m_z, *[marks[c] for c in chunks])
        for i, c in enumerate(chunks):
            for k in range(2):
                msc = w_sc.sent(nc.gpsimd.indirect_dma_start(
                    out=XP[:, :], out_offset=bass.IndirectOffsetOnAxis(ap=DST[:, k * nch + i:k * nch + i + 1], axis=0),
                    in_=H[:, c, :], in_offset=None))
        phase("moe%d" % layer)
        at[0] = 0
        fence(msc)
        nb = 16
        xe = [take(D) for _ in range(2)]
        xeT = [take(8 * BL).rearrange("p (c t) -> p c t", c=8) for _ in range(2)]
        hid = [take(8 * BL) for _ in range(2)]
        hidT = [take(8 * BL).rearrange("p (c t) -> p c t", c=8) for _ in range(2)]
        yo = [take(8 * BL) for _ in range(2)]
        m_in, m_st, free_xe, free_xeT, free_hid, xeT_ready = {}, {}, {}, {}, {}, {}

        def fetch(n):
            if n < nb:
                pool.after(*free_xe.get(n - 2, ()))
                m_in[n] = w_xe[n % 2].sent(nc.gpsimd.dma_start(xe[n % 2][0:BL, :], XP[n * BL:(n + 1) * BL, :]))

        def turn_in(n, ahead=True):
            if n >= nb and ahead:
                return
            last_marks.clear()
            pe.after(m_in[n], *free_xeT.get(n - 2, ()))
            k = 512 // BL
            for j in range(0, 8, k):
                b = ps.take()
                for i in range(j, j + k):
                    last = nc.tensor.transpose(b.ap[:, (i - j) * BL:(i - j + 1) * BL], xe[n % 2][0:BL, i * P:(i + 1) * P],
                                               ident[0:BL, 0:BL])
                m = pe.done(last)
                m = evac(xeT[n % 2][:, j:j + k, :], b.ap.rearrange("p (a b) -> p a b", a=k), m)
                b.free(m)
                last_marks.append(m)
            xeT_ready[n] = list(last_marks)
            free_xe[n] = (pe.mark(),)
            if ahead:
                fetch(n + 2)

        def pair(piece, n, mt, T, marks):
            (w0, m0, k0), (w1, m1, k1) = piece(n, mt, 0), piece(n, mt, 1)
            b = ps.take()
            pe.after(m0, m1, *marks)
            for c in range(8):
                for h, w in ((0, w0), (1, w1)):
                    last = mm(b.ap[64 * h:64 * h + 64, :], T(c, h), w[:, c, :], c == 0, c == 7)
            m = pe.done(last)
            return b, m, (k0, k1)

        def narrow(n, piece, spent, turn_next, store):
            i = n % 2
            b, m, ks = pair(piece, n, "g", lambda c, h: xeT[i][:, c, :], xeT_ready[n])
            spent(ks, m)
            m_g = act.done(act.after(m, *free_hid.get(n - 2, ())).activation(hid[i], b.ap, ACT.Silu))
            b.free(m_g)
            b, m, ks = pair(piece, n, "u", lambda c, h: xeT[i][:, c, :], ())
            spent(ks, m)
            free_xeT[n] = (m,)
            m = dve.done(dve.after(m, m_g).tensor_tensor(hid[i], hid[i], b.ap, ALU.mult))
            b.free(m)
            turn_next(n + 1)
            b = ps.take()
            pe.after(m)
            for j in range(4):
                last = nc.tensor.transpose(b.ap[:, j * P:(j + 1) * P], hid[i][:, j * P:(j + 1) * P], ident)
            m = pe.done(last)
            free_hid[n] = (m,)
            m = evac(hidT[i].rearrange("p (h j) t -> p j h t", h=2), b.ap.rearrange("p (j h t) -> p j h t", j=4, h=2), m)
            b.free(m)
            b, m, ks = pair(piece, n, "d", lambda c, h: hidT[i][:, c, :], (m,))
            spent(ks, m)
            m = evac(yo[i], b.ap, m, m_st.get(n - 2))
            b.free(m)
            m_st[n] = store(n, m, [(YP[n * BL:(n + 1) * BL, 512 * h:512 * h + 512], yo[i][64 * h:64 * h + 64, :]) for h in range(2)])

        def wide(n, piece, spent, turn_next, store):
            i = n % 2
            m_h = []
            for h in range(2):
                sl = slice(h * 512, h * 512 + 512)
                w, mw, k = piece(n, "g", h)
                b, m = project(w, [mw] + xeT_ready[n], xeT[i], 0)
                spent((k,), m)
                m = act.done(act.after(m, *free_hid.get(n - 2, ())).activation(hid[i][:, sl], b.ap, ACT.Silu))
                b.free(m)
                w, mw, k = piece(n, "u", h)
                b, m2 = project(w, [mw], xeT[i], 0)
                spent((k,), m2)
                m = dve.done(dve.after(m, m2).tensor_tensor(hid[i][:, sl], hid[i][:, sl], b.ap, ALU.mult))
                b.free(m)
                m_h.append(m)
            free_xeT[n] = (pe.mark(),)
            turn_next(n + 1)
            last_marks.clear()
            turned(hidT[i][:, 0:4, :], hid[i][:, 0:512], 4, m_h[0])
            turned(hidT[i][:, 4:8, :], hid[i][:, 512:D], 4, m_h[1])
            hm = list(last_marks)
            free_hid[n] = (pe.mark(),)
            ms = []
            for h in range(2):
                w, mw, k = piece(n, "d", h)
                b, m = project(w, [mw] + hm, hidT[i], 0)
                spent((k,), m)
                m = evac(yo[i][:, h * 512:h * 512 + 512], b.ap, m, m_st.get(n - 2))
                b.free(m)
                ms.append(m)
            m_st[n] = store(n, ms, [(YP[n * BL:(n + 1) * BL, :], yo[i])])

        def flat(m):
            return m if isinstance(m, list) else [m]

        def store(n, m, pairs):
            act.after(*flat(m))
            for dst, src in pairs:
                m = w_y[n % 2].sent(nc.scalar.dma_start(dst, src))
            return m

        block_of = wide if BL == P else narrow
        fetch(0)
        fetch(1)
        turn_in(0)
        for n in range(nb):
            block_of(n, lambda n, mt, h: ring.take((layer, n, mt, h)), lambda ks, m: [ring.free(k, m) for k in ks],
                     turn_in, store)
        fence(m_st[nb - 1], m_st[nb - 2], m_oe)
        sp.after(pe.mark(), m_oe)
        phase("over%d" % layer)
        many = nc.values_load(OE[0:1, 8:9], min_val=0, max_val=nover)
        order = WIDE if BL == P else PAIRS

        def further(n):
            expert = nc.sync.value_load(OE[0:1, n - 16:n - 15], min_val=0, max_val=15)
            marks = fence()
            sp.after(*marks)
            m_in[n] = w_vx.sent(nc.sync.dma_start(xe[n % 2][0:BL, :], XP[n * BL:(n + 1) * BL, :]))
            sent = {}

            def load(k, *marks):
                mt, h = order[k]
                v = moe[mt][layer].rearrange("e (c p) n -> p e c n", p=P)
                sp.after(*marks)
                sent[k] = w_v[k % NS].sent(nc.sync.dma_start(
                    ring.ap[:, k % NS, :].rearrange("p (e c n) -> p e c n", e=1, c=8),
                    v[:, bass.ds(expert, 1), :, 512 * h:512 * h + 512]))

            for k in range(NS):
                load(k)

            def piece(n, mt, h):
                k = order.index((mt, h))
                return ring.ap[:, k % NS, :].rearrange("p (c n) -> p c n", c=8), sent[k], k

            def spent(ks, m):
                for k in ks:
                    if k + NS < 6:
                        load(k + NS, m)

            def put(n, m, pairs):
                act.after(*flat(m))
                for dst, src in pairs:
                    m = w_vy.sent(nc.scalar.dma_start(dst, src))
                return m

            for d_ in (free_xe, free_xeT, free_hid, m_st, xeT_ready):
                d_.clear()
            turn_in(n, False)
            block_of(n, piece, spent, lambda n: None, put)
            marks = fence(m_st[n])
            sp.after(*marks)

        for n in range(16, 16 + nover):
            counts = [(x, x.n, dict(x.met)) for x in (pe, dve, act, pool, sp)]
            wires = [(x, x.n) for x in w_v + [w_vx, w_vy]]
            with nc.If(many > n - 16):
                further(n)
            with nc.Else():
                for x, was, _ in counts:
                    if x.n > was:
                        x.eng.sem_inc(x.sem, x.n - was)
                for x, was in wires:
                    if x.n > was:
                        (nc.scalar if x is w_vy else nc.sync).sem_inc(x.sem, x.n - was)
            for x, _, met in counts:
                x.met = met
        marks = fence()
        sp.after(*marks)
        ring.resume()
        phase("comb%d" % layer)
        at[0] = 0
        R = [take(D) for _ in range(2 * nch)]
        for i, c in enumerate(chunks):
            for k in range(2):
                mg = w_g.sent(nc.gpsimd.indirect_dma_start(
                    out=R[2 * i + k], out_offset=None, in_=YP[:, :],
                    in_offset=bass.IndirectOffsetOnAxis(ap=DST[:, k * nch + i:k * nch + i + 1], axis=0)))
        for r in sorted({c // 2 for c in chunks}):
            g, m = spread(10 + r)
            for i, c in enumerate(chunks):
                if c // 2 != r:
                    continue
                a, b2 = R[2 * i], R[2 * i + 1]
                m = dve.done(dve.after(m, mg).tensor_scalar(b2, b2, wk[1][:, i:i + 1], None, ALU.mult))
                m = dve.done(dve.after(m).scalar_tensor_tensor(
                    out=a, in0=a, scalar=wk[0][:, i:i + 1], in1=b2, op0=ALU.mult, op1=ALU.add))
                m = dve.done(dve.after(m).tensor_tensor(a, a, g.ap, ALU.mult))
                m = dve.done(dve.after(m).tensor_tensor(X[:, c, :], X[:, c, :], a, ALU.add))
            g.free(m)

    phase("mod0")
    for _ in modulation("ada0", 0, I["ada_b"][0], [(2, I["norm_mix_g"][0]), (8, I["norm_ffn_g"][0])],
                        AR[:, 0:1536], None):
        pass
    fence()
    phase("norm0")
    at[0] = 0
    allc = [0, 1, 2, 3]
    HT = take(8 * 512).rearrange("p (c t) -> p c t", c=8)
    base = at[0]
    H = take(4 * D).rearrange("p (c d) -> p c d", c=4)
    junk = take(D)
    smat[0] = 0
    rs = small(8)
    marks = modulated(H, allc, 0, 2, junk, rs)
    tm = turn_all(HT, H, allc, marks)
    at[0] = base
    fence(*tm)
    fm = lambda a: a.rearrange("p (c h t) -> p c h t", c=4, h=4)
    Q, FF, FB = (fm(take(2048)) for _ in range(3))
    V = take(2048).rearrange("p (c n) -> p c n", c=4)
    O = take(2048).rearrange("p (c n) -> p c n", c=4)
    lv = take(15 * 128)
    place = take(1536)
    zt = take(256)
    lbr = take(128)
    top = at[0]
    m_lv = w_s.sent(nc.gpsimd.dma_start(lv, I["consts"][:, C_LEV:C_LEV + 15 * P]))
    m_lv = w_s.sent(nc.gpsimd.dma_start(lbr[0:24, :], I["hgrn_lb_logits"].rearrange("a d (h k) -> (a d h) k", k=P)))
    on = small(128)
    m_lv = broadcast_load(on, I["hgrn_onorm_g"][0], P)
    phase("proj0")
    for n in range(3):
        w, mw, k = ring.take(("in", n))
        for h in range(4):
            b, m = project_T(w, [mw], h, HT, 0, 512)
            dst = (Q, FF, FB)[n][:, :, h, :]
            src = b.ap.rearrange("p (c t) -> p c t", c=4)
            m2 = act.done(act.after(m).activation(dst, src, ACT.Silu if n == 0 else ACT.Sigmoid))
            b.free(m2)
        ring.free(k, m)
    w, mw, k = ring.take(("in", 3))
    for c in allc:
        b, m = project(w, [mw], HT, c)
        m2 = dve.done(dve.after(m).tensor_copy(V[:, c, :], b.ap))
        b.free(m2)
    ring.free(k, m)
    phase("hgrn")
    b = ps.take()
    pe.after(m_lv)
    m = pe.done(nc.tensor.transpose(b.ap[:, 0:24], lbr[0:24, :], ident[0:24, 0:24]))
    lg, lb, oml, t8 = small(24), small(8), small(8), small(8)
    m = dve.done(dve.after(m).tensor_copy(lg, b.ap[:, 0:24]))
    b.free(m)
    dve.done(dve.after().tensor_tensor(t8, lg[:, 0:8], lg[:, 8:16], ALU.max))
    dve.done(dve.after().tensor_tensor(t8, t8, lg[:, 16:24], ALU.max))
    l3 = lg.rearrange("p (a b) -> p a b", a=3)
    m = dve.done(dve.after().tensor_tensor(l3, l3, t8.unsqueeze(1).to_broadcast([P, 3, 8]), ALU.subtract))
    m = act.done(act.after(m).activation(lg, lg, ACT.Exp))
    dve.done(dve.after(m).tensor_tensor(t8, lg[:, 0:8], lg[:, 8:16], ALU.add))
    dve.done(dve.after().tensor_tensor(t8, t8, lg[:, 16:24], ALU.add))
    dve.done(dve.after().reciprocal(t8, t8))
    dve.done(dve.after().tensor_tensor(lb, lg[:, 0:8], t8, ALU.mult))
    m_lb = dve.done(dve.after().tensor_scalar(oml, lb, -1.0, 1.0, ALU.mult, ALU.add))
    m_q = dve.done(dve.after().tensor_scalar(Q[:, :, :, :], Q[:, :, :, :], 128 ** -0.5, None, ALU.mult))
    fence(m_lb)
    m_hd = w_h.sent(nc.scalar.dma_start(HD, HT.rearrange("p c t -> p (c t)")))
    m_z = pool.done(pool.after().memset(zt, 0.0))
    pool.after(m_z)
    for dst, n in [(XP, n) for n in range(XROWS // P)] + [(YP, n) for n in range(16, XROWS // P)]:
        m_z = w_z.sent(nc.gpsimd.dma_start(dst[n * P:(n + 1) * P, :].rearrange("p (a b) -> p a b", a=4),
                                           zt.unsqueeze(1).to_broadcast([P, 4, 256])))
    fence(m_hd)
    at[0] = 0
    early = [take(512) for _ in range(8)]
    at[0] = top
    rest = [take(512) for _ in range(8)]
    temps = [early, rest]
    h4 = lambda a: a.rearrange("p (h t) -> p h t", h=4)
    ets = [small(4), small(4)]

    def direction(d):
        kt_, cum, ee, kk, qq, A_, tA, Sf = temps[d]
        S, et = h4(Sf), ets[d]
        lf = tA
        order = (2, 3, 0, 1) if d == 0 else (3, 2, 1, 0)
        FX = (FF, FB)[d]
        end = 127 if d == 0 else 0
        m_pe = None
        for step, c in enumerate(order):
            Qf = Q[:, c, :, :].rearrange("p h t -> p (h t)")
            for h in range(4):
                m = dve.done(dve.after().tensor_scalar(FX[:, c, h, :], FX[:, c, h, :], oml[:, 4 * d + h:4 * d + h + 1],
                                                       lb[:, 4 * d + h:4 * d + h + 1], ALU.mult, ALU.add))
            m_lf = act.done(act.after(m, m_pe).activation(h4(lf), FX[:, c, :, :], ACT.Ln))
            m_k = dve.done(dve.after(m_pe).tensor_scalar(h4(kt_), FX[:, c, :, :], -1.0, 1.0, ALU.mult, ALU.add))
            yield
            for h in range(4):
                i_, o_ = h4(lf)[:, h, :], h4(cum)[:, h, :]
                if d == 1:
                    i_, o_ = i_[:, ::-1], o_[:, ::-1]
                m = dve.done(dve.after(m_lf).tensor_tensor_scan(o_, ones[:, :], i_, 0.0, ALU.mult, ALU.add))
            m_et = act.done(act.after(m).activation(et, h4(cum)[:, :, end], ACT.Exp))
            for l in range(8):
                if l < 7:
                    hb = 64 >> l
                    v = lambda a: a.rearrange("p (n s b) -> p n s b", s=2, b=hb)
                    qs, ks, ref = (1, 0, hb - 1) if d == 0 else (0, 1, 0)
                    cv = v(cum)
                    r_ = cv[:, :, ks, ref].unsqueeze(2).to_broadcast([P, 256 // hb, hb])
                    qw, kw = ee[:, 0:256].rearrange("p (n b) -> p n b", b=hb), ee[:, 256:512].rearrange("p (n b) -> p n b", b=hb)
                    dve.done(dve.after().tensor_tensor(qw, cv[:, :, qs, :], r_, ALU.subtract))
                    m1 = dve.done(dve.after().tensor_tensor(kw, r_, cv[:, :, ks, :], ALU.subtract))
                    m1 = act.done(act.after(m1).activation(ee, ee, ACT.Exp))
                    yield
                    dve.after(m1, m_pe)
                    if l == 0:
                        dve.done(dve.after().memset(qq, 0.0))
                        dve.done(dve.after().memset(kk, 0.0))
                    dve.done(dve.after().tensor_tensor(v(qq)[:, :, qs, :], v(Qf)[:, :, qs, :], qw, ALU.mult))
                    m3 = dve.done(dve.after().tensor_tensor(v(kk)[:, :, ks, :], v(kt_)[:, :, ks, :], kw, ALU.mult))
                b = ps.take()
                pe.after(m3, m_k)
                kl, ql = (kk, qq) if l < 7 else (kt_, Qf)
                for h in range(4):
                    last = mm(b.ap[:, h * P:(h + 1) * P], h4(kl)[:, h, :], h4(ql)[:, h, :], True, True)
                m_pe = pe.done(last)
                if l < 7:
                    yield
                mask = lv[:, (7 * d + l if l < 7 else 14) * P:(7 * d + l + 1 if l < 7 else 15) * P]
                mask4 = mask.unsqueeze(1).to_broadcast([P, 4, P])
                if l == 0:
                    m = dve.done(dve.after(m_pe, m_lv).tensor_tensor(h4(A_), h4(b.ap), mask4, ALU.mult))
                else:
                    m = dve.done(dve.after(m_pe).copy_predicated(h4(A_), mask4.bitcast(U32), h4(b.ap)))
                b.free(m)
            m_A = m
            if step:
                m1 = act.done(act.after(m_A).activation(ee, cum, ACT.Exp))
                m1 = dve.done(dve.after(m1, m_pe).tensor_tensor(qq, Qf, ee, ALU.mult))
            b = ps.take()
            pe.after(m_A, m1)
            for h in range(4):
                last = mm(b.ap[:, h * P:(h + 1) * P], h4(A_)[:, h, :], V[:, c, h * P:(h + 1) * P], True, step == 0)
                if step:
                    last = mm(b.ap[:, h * P:(h + 1) * P], h4(qq)[:, h, :], S[:, h, :], False, True)
            m_pe = pe.done(last)
            yield
            if step % 2 == 0:
                m = dve.done(dve.after(m_pe).tensor_copy(O[:, c, :], b.ap))
            else:
                m = dve.done(dve.after(m_pe).tensor_tensor(O[:, c, :], O[:, c, :], b.ap, ALU.add))
            b.free(m)
            if step == 3:
                return
            m = dve.done(dve.after().tensor_tensor(h4(ee), h4(cum)[:, :, end:end + 1].to_broadcast([P, 4, P]), h4(cum), ALU.subtract))
            m = act.done(act.after(m).activation(ee, ee, ACT.Exp))
            m = dve.done(dve.after(m).tensor_tensor(kk, kt_, ee, ALU.mult))
            b = ps.take()
            pe.after(m)
            for h in range(4):
                last = nc.tensor.transpose(b.ap[:, h * P:(h + 1) * P], h4(kk)[:, h, :], ident)
            m = pe.done(last)
            yield
            m = act.done(act.after(m).copy(tA, b.ap))
            b.free(m)
            b = ps.take()
            pe.after(m)
            for h in range(4):
                last = mm(b.ap[:, h * P:(h + 1) * P], h4(tA)[:, h, :], V[:, c, h * P:(h + 1) * P], True, True)
            m_pe = pe.done(last)
            yield
            if step == 0:
                m = dve.done(dve.after(m_pe).tensor_copy(S, h4(b.ap)))
            else:
                for h in range(4):
                    m = dve.done(dve.after(m_pe, m_et).scalar_tensor_tensor(
                        out=S[:, h, :], in0=S[:, h, :], scalar=et[:, h:h + 1], in1=b.ap[:, h * P:(h + 1) * P],
                        op0=ALU.mult, op1=ALU.add))
            b.free(m)

    def both_modulations():
        for args in (("ada1", 0, I["ada_b"][1], [(2, I["norm_mix_g"][1]), (8, I["norm_ffn_g"][1])], place, M1),
                     ("ada2", 1, I["b_mod_2"][0], [(2, I["norm_mix_pre_2"][0]), (4, I["norm_mix_post_2"][0]),
                                                   (8, I["norm_ffn_pre_2"][0]), (10, I["norm_ffn_post_2"][0])], place, M2)):
            yield from modulation(*args)

    in_turns(direction(0), direction(1), every(2, both_modulations()))
    mod_kept = (id(w_m.sem), w_m.sem, w_m.n)
    marks = fence()
    act.after(*marks)
    m_ht = w_h.sent(nc.scalar.dma_start(HT.rearrange("p c t -> p (c t)"), HD))
    sq_ = rest[0]
    ss = small(16)
    for c in allc:
        m = dve.done(dve.after(pe.mark()).tensor_tensor(sq_, O[:, c, :], O[:, c, :], ALU.mult))
        m = dve.done(dve.after().tensor_reduce(ss[:, 4 * c:4 * c + 4], h4(sq_), AX.X, ALU.add))

    def finish_rstd(ss, n, width):
        m = dve.done(dve.after().tensor_scalar(ss[:, 0:n], ss[:, 0:n], 1.0 / width, EPS, ALU.mult, ALU.add))
        m = act.done(act.after(m).activation(ss[:, 0:n], ss[:, 0:n], ACT.Sqrt))
        return dve.done(dve.after(m).reciprocal(ss[:, 0:n], ss[:, 0:n]))

    m = finish_rstd(ss, 16, 128)
    for c in allc:
        for h in range(4):
            m = dve.done(dve.after(m).scalar_tensor_tensor(
                out=O[:, c, h * P:(h + 1) * P], in0=O[:, c, h * P:(h + 1) * P], scalar=ss[:, 4 * c + h:4 * c + h + 1],
                in1=on, op0=ALU.mult, op1=ALU.mult))
    phase("attn0proj")
    w, mw, k = ring.take(("in", 4))
    G = O
    for c in allc:
        b, m = project(w, [mw, m_ht], HT, c)
        last = m
        m = act.done(act.after(m).activation(rest[1 + c], b.ap, ACT.Silu))
        b.free(m)
        m = dve.done(dve.after(m).tensor_tensor(O[:, c, :], O[:, c, :], rest[1 + c], ALU.mult))
    ring.free(k, last)
    at[0] = base
    smat[0] = 0
    fence(m_ht)
    hm = lambda a: a.rearrange("p (h t) -> p h t", h=4)
    QA, KA = hm(take(2048)), hm(take(2048))
    VA = take(2048).rearrange("p (c n) -> p c n", c=4)
    take(2048)
    assert O.offset == AR[:, at[0]:at[0] + 1].offset, (O.offset, at[0])
    take(2048)
    YB = take(2048).rearrange("p (c n) -> p c n", c=4)
    P0, P1, aT = [take(512) for _ in range(3)], [take(512) for _ in range(3)], [take(512) for _ in range(2)]
    rtmp = take(256)
    rot2 = take(256)
    lam4, sub = small(256), small(128)
    m_l = broadcast_load(lam4, I["diff_lambda"][0].rearrange("a b -> (a b)"), 256)
    m_l = broadcast_load(sub, I["diff_subln_g"][0], 128)
    lt, l2 = small(128), small(2)
    for j in range(2):
        dve.done(dve.after(m_l).tensor_tensor(lt[:, j * 64:j * 64 + 64], lam4[:, 128 * j:128 * j + 64],
                                              lam4[:, 128 * j + 64:128 * j + 128], ALU.mult))
    m = dve.done(dve.after().tensor_reduce(l2, lt.rearrange("p (a b) -> p a b", a=2), AX.X, ALU.add))
    m = act.done(act.after(m).activation(l2, l2, ACT.Exp))
    lam = small(1)
    dve.done(dve.after(m).tensor_tensor(lam, l2[:, 1:2], l2[:, 0:1], ALU.subtract))
    m = dve.done(dve.after(m).tensor_scalar(lam, lam, 0.8 - 0.6 * math.exp(-0.0), None, ALU.subtract))
    for n, dst in ((5, QA), (6, KA)):
        w, mw, k = ring.take(("in", n))
        for h in range(4):
            b, m = project_T(w, [mw], h, HT, 0, 512)
            last = m
            m = evac(dst[:, h, :], b.ap, m)
            b.free(m)
            m = dve.done(dve.after(m, pe.mark()).tensor_copy(rot2, dst[:, h, 0:256]))
            rope(dst[:, h, 0:256], rot2, [m])
        ring.free(k, last)
    w, mw, k = ring.take(("in", 7))
    for c in allc:
        b, m = project(w, [mw], HT, c)
        last = m
        m = evac(VA[:, c, :], b.ap, m)
        b.free(m)
    ring.free(k, last)
    fence()
    phase("attn0")
    sts = [small(8) for _ in range(3)]
    units = [(qi, h) for qi in allc for h in range(4)]
    got, obs = {}, {}

    def scores0(u):
        qi, h = units[u]
        k0, k1 = (0, 512) if qi < 2 else (256, 512)
        nk = k1 - k0
        st = sts[u % 3]
        for mp in range(2):
            b = ps.take()
            pr = slice(64 * mp, 64 * mp + 64)
            m = pe.done(mm(b.ap[:, 0:nk], QA[pr, h, qi * P:(qi + 1) * P], KA[pr, h, k0:k1], True, True))
            Pm = (P0, P1)[mp][u % 3]
            m = dve.done(dve.after(m).tensor_reduce(st[:, mp:mp + 1], b.ap[:, 0:nk], AX.X, ALU.max))
            m = dve.done(dve.after(m).tensor_scalar(st[:, mp:mp + 1], st[:, mp:mp + 1], -0.125, None, ALU.mult))
            m = act.done(act.after(m, got.get(("t", u - 3))).activation(
                Pm[:, 0:nk], b.ap[:, 0:nk], ACT.Exp, bias=st[:, mp:mp + 1], scale=0.125, accum_out=st[:, 2 + mp:3 + mp]))
            b.free(m)
        got["e", u] = m

    def weights0(u):
        qi, h = units[u]
        nk = 512 if qi < 2 else 256
        st = sts[u % 3]
        dve.done(dve.after(got["e", u]).reciprocal(st[:, 4:6], st[:, 2:4]))
        dve.done(dve.after().tensor_tensor(st[:, 5:6], st[:, 5:6], lam, ALU.mult))
        a0, a1 = P0[u % 3][:, 0:nk], P1[u % 3][:, 0:nk]
        dve.done(dve.after().tensor_scalar(a1, a1, st[:, 5:6], None, ALU.mult))
        got["a", u] = dve.done(dve.after().scalar_tensor_tensor(out=a0, in0=a0, scalar=st[:, 4:5], in1=a1, op0=ALU.mult, op1=ALU.add))

    def turn0(u):
        qi, h = units[u]
        nk = 512 if qi < 2 else 256
        b = ps.take()
        pe.after(got["a", u])
        for j in range(nk // P):
            last = nc.tensor.transpose(b.ap[:, j * P:(j + 1) * P], P0[u % 3][:, j * P:(j + 1) * P], ident)
        got["t", u] = m = pe.done(last)
        got["c", u] = m = evac(aT[u % 2][:, 0:nk], b.ap[:, 0:nk], m, got.get(("v", u - 2)))
        b.free(m)

    def values0(u):
        qi, h = units[u]
        k0, nk = (0, 512) if qi < 2 else (256, 256)
        if h == 0:
            obs[qi] = ps.take()
        ob = obs[qi]
        pe.after(got["c", u])
        for j in range(nk // P):
            last = mm(ob.ap[:, h * P:(h + 1) * P], aT[u % 2][:, j * P:(j + 1) * P],
                      VA[:, k0 // P + j, h * P:(h + 1) * P], j == 0, j == nk // P - 1)
        got["v", u] = m = pe.done(last)
        if h == 3:
            m = dve.done(dve.after(m).tensor_copy(YB[:, qi, :], ob.ap))
            ob.free(m)

    def staggered(n, *stages):
        for i in range(n + len(stages) - 1):
            for k, stage in enumerate(stages):
                if 0 <= i - k < n:
                    stage(i - k)

    staggered(16, scores0, weights0, turn0, values0)
    ss = small(16)
    for c in allc:
        m = dve.done(dve.after().tensor_tensor(P0[0], YB[:, c, :], YB[:, c, :], ALU.mult))
        m = dve.done(dve.after().tensor_reduce(ss[:, 4 * c:4 * c + 4], h4(P0[0]), AX.X, ALU.add))
    m = finish_rstd(ss, 16, 128)
    m = dve.done(dve.after().tensor_scalar(ss, ss, 1.0 - (0.8 - 0.6 * math.exp(-0.0)), None, ALU.mult))
    for c in allc:
        for h in range(4):
            m = dve.done(dve.after(m).scalar_tensor_tensor(
                out=YB[:, c, h * P:(h + 1) * P], in0=YB[:, c, h * P:(h + 1) * P], scalar=ss[:, 4 * c + h:4 * c + h + 1],
                in1=sub, op0=ALU.mult, op1=ALU.mult))
    fence()
    last_marks.clear()
    for c in allc:
        turned(HT[:, 0:4, c * P:(c + 1) * P], G[:, c, :], 4, None)
        turned(HT[:, 4:8, c * P:(c + 1) * P], YB[:, c, :], 4, None)
    tm = list(last_marks)
    at[0] = base
    fence(*tm)
    phase("out0")
    tmp = [take(D), take(D), take(512)]
    add_branch([("wo", 0), ("wo", 1)], HT, allc, 4, tm, tmp)
    routed(0, allc, P)

    def finish(src_marks, final=None):
        mo = w_o.sent(nc.scalar.dma_start(out[0].rearrange("(c p) d -> p c d", p=P), final if final is not None else X[:, 0:2, :]))
        act.after(mo, mod_kept)
        ctx.close()

    if upto == 1:
        fence()
        return finish(None)

    phase("mod1")
    fetch_modulation(M1)
    phase("norm")
    at[0] = 0
    smat[0] = 0
    HT = take(8 * 512).rearrange("p (c t) -> p c t", c=8)
    base = at[0]
    H = take(4 * D).rearrange("p (c d) -> p c d", c=4)
    junk = take(D)
    rs = small(8)
    marks = modulated(H, allc, 0, 2, junk, rs)
    tm = turn_all(HT, H, allc, marks)
    at[0] = base
    fence(*tm)
    QC = take(8 * 256).rearrange("p (c t) -> p c t", c=8)
    KK = take(4 * 512).rearrange("p (c t) -> p c t", c=4)
    VC = take(4 * 256).rearrange("p (c n) -> p c n", c=4)
    YC = take(2 * D).rearrange("p (c n) -> p c n", c=2)
    swa = take(1024).rearrange("p (q n) -> p q n", q=2)
    Sx, aT = [take(512) for _ in range(3)], [take(512) for _ in range(2)]
    rtmp = take(256)
    rot2 = take(256)
    sink = small(16)
    w_sw = w_s.sent(nc.gpsimd.dma_start(swa, I["consts"][:, C_SWA:C_SWA + 1024].rearrange("p (q n) -> p q n", q=2)))
    w_sw = broadcast_load(sink, I["swa_sink"][0], 16)
    phase("proj1")
    for n in range(2):
        w, mw, k = ring.take(("qkv", n))
        for j in range(4):
            b, m = project_T(w, [mw], j, HT, 0, 256)
            last = m
            m = evac(rot2, b.ap[:, 0:256], m, dve.mark(), pe.mark())
            b.free(m)
            rope(QC[:, 4 * n + j, :], rot2, [m])
        ring.free(k, last)
    w, mw, k = ring.take(("qkv", 2))
    pe.after(mw)
    for j in range(4):
        b = ps.take()
        for half in range(2):
            for c in range(8):
                last = mm(b.ap[64 * half:64 * half + 64, :], w[:, c, 64 * j:64 * j + 64], HT[:, c, :], c == 0, c == 7)
        m = pe.done(last)
        m = evac(KK[:, j, :], b.ap, m)
        b.free(m)
        m = dve.done(dve.after(m, pe.mark()).tensor_copy(rot2, KK[:, j, 0:256]))
        rope(KK[:, j, 0:256], rot2, [m])
    for c in allc:
        b = ps.take()
        for k8 in range(8):
            last = mm(b.ap[:, 0:256], HT[:, k8, c * P:(c + 1) * P], w[:, k8, 256:512], k8 == 0, k8 == 7)
        m = pe.done(last)
        m2 = evac(VC[:, c, :], b.ap[:, 0:256], m)
        b.free(m2)
    ring.free(k, m)
    fence()
    phase("attn1")
    sts = [small(4) for _ in range(3)]
    rr = [small(16) for _ in range(2)]
    units = [(qi, h) for qi in range(2) for h in range(16)]
    got, obs = {}, {}

    def scores1(u):
        qi, h = units[u]
        pr = slice(64 * (h % 2), 64 * (h % 2) + 64)
        s, st = Sx[u % 3], sts[u % 3]
        b = ps.take()
        m = pe.done(mm(b.ap, QC[pr, h // 2, qi * P:(qi + 1) * P], KK[pr, h // 4, :], True, True))
        m = dve.done(dve.after(m, w_sw, got.get(("t", u - 3))).scalar_tensor_tensor(
            out=s, in0=b.ap, scalar=0.125, in1=swa[:, qi, :], op0=ALU.mult, op1=ALU.add))
        b.free(m)
        dve.done(dve.after().tensor_reduce(st[:, 0:1], s, AX.X, ALU.max))
        m = dve.done(dve.after().tensor_scalar(st[:, 0:1], st[:, 0:1], sink[:, h:h + 1], -1.0, ALU.max, ALU.mult))
        got["e", u] = act.done(act.after(m).activation(s, s, ACT.Exp, bias=st[:, 0:1], accum_out=st[:, 1:2]))
        got["s", u] = act.done(act.after(m).activation(st[:, 2:3], sink[:, h:h + 1], ACT.Exp, bias=st[:, 0:1]))

    def turn1(u):
        qi, h = units[u]
        st = sts[u % 3]
        dve.done(dve.after(got["s", u]).tensor_tensor(st[:, 1:2], st[:, 1:2], st[:, 2:3], ALU.add))
        dve.done(dve.after().reciprocal(rr[qi][:, h:h + 1], st[:, 1:2]))
        b = ps.take()
        pe.after(got["e", u])
        for j in range(4):
            last = nc.tensor.transpose(b.ap[:, j * P:(j + 1) * P], Sx[u % 3][:, j * P:(j + 1) * P], ident)
        got["t", u] = m = pe.done(last)
        got["c", u] = m = evac(aT[u % 2], b.ap, m, got.get(("v", u - 2)))
        b.free(m)

    def values1(u):
        qi, h = units[u]
        if h % 8 == 0:
            obs[u // 8] = ps.take()
        ob = obs[u // 8]
        pe.after(got["c", u])
        o8 = (h % 8) * 64
        for j in range(4):
            last = mm(ob.ap[:, o8:o8 + 64], aT[u % 2][:, j * P:(j + 1) * P], VC[:, j, 64 * (h // 4):64 * (h // 4) + 64],
                      j == 0, j == 3)
        got["v", u] = m = pe.done(last)
        if h % 8 == 7:
            h0 = h - 7
            m = dve.done(dve.after(m).tensor_tensor(
                YC[:, qi, h0 * 64:h0 * 64 + 512].rearrange("p (h d) -> p h d", h=8),
                ob.ap.rearrange("p (h d) -> p h d", h=8),
                rr[qi][:, h0:h0 + 8].unsqueeze(2).to_broadcast([P, 8, 64]), ALU.mult))
            ob.free(m)

    staggered(32, scores1, turn1, values1)
    fence()
    phase("out1")
    xc = [0, 1]
    tm = turn_all(HT, YC, xc, {0: None, 1: None})
    at[0] = base
    fence(*tm)
    tmp = [take(D), take(D), take(512)]
    add_branch([("owo", 0), ("owo", 1)], HT, xc, 4, tm, tmp)
    routed(1, xc, 64)
    phase("fnorm")
    at[0] = 0
    smat[0] = 0
    fence()
    mx = w_x2.sent(nc.gpsimd.dma_start(X[:, 2:4, :], I["ctx_2"][0].rearrange("(c p) d -> p c d", p=P)))
    fg = take(D)
    junk = take(D)
    m_f = broadcast_load(fg, I["final_norm_g"], D)
    rs = small(8)
    m = rstd_of([X[:, c, :] for c in xc], D, [], rs, junk)
    for c in xc:
        m = dve.done(dve.after(m, m_f).scalar_tensor_tensor(out=X[:, c, :], in0=X[:, c, :], scalar=rs[:, c:c + 1], in1=fg,
                                                            op0=ALU.mult, op1=ALU.mult))
    fence(mx)
    if upto == 2:
        return finish(None)

    phase("mod2")
    fetch_modulation(M2)
    phase("norm")
    at[0] = 0
    smat[0] = 0
    HT = take(8 * 512).rearrange("p (c t) -> p c t", c=8)
    base = at[0]
    H = take(4 * D).rearrange("p (c d) -> p c d", c=4)
    junk = take(D)
    rs = small(8)
    marks = modulated(H, allc, 0, 2, junk, rs)
    tm = turn_all(HT, H, allc, marks)
    at[0] = base
    fence(*tm)
    BT = take(4 * 512).rearrange("p (g t) -> p g t", g=4)
    CTt = take(4 * 256).rearrange("p (g t) -> p g t", g=4)
    XH = take(4 * 1536).rearrange("p (c n) -> p c n", c=4)
    BK = take(4 * 512).rearrange("p (c n) -> p c n", c=4)
    HS = [take(1536) for _ in range(2)]
    XW = take(1536)
    cv = [XW[:, 0:512], XW[:, 512:1024], XW[:, 1024:1536], take(512)]
    Y2 = XH[:, 2:4, :]
    cw = small(80)
    cwr = small(128)
    w_cv = w_s.sent(nc.gpsimd.dma_start(cwr[0:60, :], I["conv_w_2"][0].rearrange("k (c p) -> (k c) p", p=P)))
    w_cv = w_s.sent(nc.gpsimd.dma_start(cwr[60:80, :], I["conv_b_2"][0].rearrange("(c p) -> c p", p=P)))
    dtb, alog, dsk = small(48), small(48), small(24)
    w_cv = broadcast_load(dtb, I["dt_bias_2"][0].rearrange("a b -> (a b)"), 48)
    w_cv = broadcast_load(alog, I["a_log_2"][0].rearrange("a b -> (a b)"), 48)
    w_cv = broadcast_load(dsk, I["d_skip_2"][0], 24)
    b = ps.take()
    pe.after(w_cv)
    m = pe.done(nc.tensor.transpose(b.ap[:, 0:80], cwr[0:80, :], ident[0:80, 0:80]))
    m_cw = dve.done(dve.after(m).tensor_copy(cw, b.ap[:, 0:80]))
    b.free(m_cw)
    phase("conv")
    cvd, cvt = {}, {}

    def convolve(ch):
        T = 512 if ch < 16 else 256
        if ch % 4 == 0:
            got["w"] = ring.take(("xbc", ch // 4))
        w, mw, k = got["w"]
        b, m = project_T(w, [mw], ch % 4, HT, 0, T)
        if ch % 4 == 3:
            ring.free(k, m)
        a = cv[ch % 4]
        m = act.done(act.after(m, m_cw, cvt.get(ch - 4)).activation(
            a[:, 0:T], b.ap[:, 0:T], ACT.Identity, bias=cw[:, 60 + ch:61 + ch], scale=cw[:, 20 + ch:21 + ch]))
        rows = [(a[:, 0:256].rearrange("p (r t) -> p r t", r=4), b.ap[:, 0:256].rearrange("p (r t) -> p r t", r=4), 64)]
        if T == 512:
            rows.append((a[:, 256:512].rearrange("p (r t) -> p r t", r=1),
                         b.ap[:, 256:512].rearrange("p (r t) -> p r t", r=1), 256))
        for av, bv, L in rows:
            dve.done(dve.after(m).scalar_tensor_tensor(out=av[:, :, 1:L], in0=bv[:, :, 0:L - 1], scalar=cw[:, ch:ch + 1],
                                                       in1=av[:, :, 1:L], op0=ALU.mult, op1=ALU.add))
            m2 = dve.done(dve.after().scalar_tensor_tensor(out=av[:, :, 0:L - 1], in0=bv[:, :, 1:L],
                                                           scalar=cw[:, 40 + ch:41 + ch], in1=av[:, :, 0:L - 1],
                                                           op0=ALU.mult, op1=ALU.add))
        b.free(m2)
        cvd[ch] = m2

    def conv_act(ch):
        T = 512 if ch < 16 else 256
        a = cv[ch % 4]
        dst = a if ch < 12 else BT[:, ch - 12, :] if ch < 16 else CTt[:, ch - 16, :]
        cvt[ch] = cvd[ch] = act.done(act.after(cvd[ch]).activation(dst[:, 0:T], a[:, 0:T], ACT.Silu))

    def conv_turn(ch):
        if ch >= 16:
            return
        src = cv[ch % 4] if ch < 12 else BT[:, ch - 12, :]
        b = ps.take()
        pe.after(cvd[ch])
        for c in allc:
            last = nc.tensor.transpose(b.ap[:, c * P:(c + 1) * P], src[:, c * P:(c + 1) * P], ident)
        cvt[ch] = m = pe.done(last)
        d2 = XH[:, :, ch * P:(ch + 1) * P] if ch < 12 else BK[:, :, (ch - 12) * P:(ch - 11) * P]
        m = evac(d2, b.ap.rearrange("p (c t) -> p c t", c=4), m)
        b.free(m)

    staggered(20, convolve, conv_act, conv_turn)
    phase("ssdstate")
    w, mw, k = ring.take(("dt", 0))
    b = ps.take()
    pe.after(mw)
    for c in allc:
        for k8 in range(8):
            last = mm(b.ap[:, c * 48:c * 48 + 48], HT[:, k8, c * P:(c + 1) * P], w[:, k8, 0:48], k8 == 0, k8 == 7)
    m = pe.done(last)
    ring.free(k, m)
    DT, U, DA, AC, NA, EA, WS, ET = (small(192) for _ in range(8))
    v4 = lambda a: a.rearrange("p (c n) -> p c n", c=4)
    m = dve.done(dve.after(m).tensor_tensor(v4(DT), v4(b.ap[:, 0:192]), dtb.unsqueeze(1).to_broadcast([P, 4, 48]), ALU.add))
    b.free(m)
    dve.done(dve.after().tensor_scalar(U, DT, -1.0, None, ALU.mult))
    m = dve.done(dve.after().tensor_tensor(U, DT, U, ALU.min))
    m = act.done(act.after(m).activation(U, U, ACT.Exp))
    m = act.done(act.after(m).activation(U, U, ACT.Ln, bias=1.0))
    m = act.done(act.after(m).activation(alog, alog, ACT.Exp))
    dve.done(dve.after(m).tensor_scalar(DT, DT, 0.0, None, ALU.max))
    dve.done(dve.after().tensor_tensor(DT, DT, U, ALU.add))
    dve.done(dve.after().tensor_scalar(alog, alog, -1.0, None, ALU.mult))
    m = dve.done(dve.after().tensor_tensor(v4(DA), v4(DT), alog.unsqueeze(1).to_broadcast([P, 4, 48]), ALU.mult))
    b = ps.take()
    pe.after(m)
    for d in range(2):
        tri = KC[:, (C_LE, C_GE)[d]:(C_LE, C_GE)[d] + P]
        mm(v4(b.ap[:, 0:192])[:, :, 24 * d:24 * d + 24], tri, v4(DA)[:, :, 24 * d:24 * d + 24], True, True)
    m = pe.done(mm(b.ap[:, 192:384], ones[:, :], DA, True, True))
    m = dve.done(dve.after(m).tensor_copy(AC, b.ap[:, 0:192]))
    m = dve.done(dve.after().tensor_tensor(WS, b.ap[:, 192:384], AC, ALU.subtract))
    m = act.done(act.after(m).activation(ET, b.ap[:, 192:384], ACT.Exp))
    b.free(m)
    m = act.done(act.after(m).activation(WS, WS, ACT.Exp))
    m = act.done(act.after(m).activation(EA, AC, ACT.Exp))
    dve.done(dve.after(m).tensor_tensor(WS, WS, DT, ALU.mult))
    m_s = dve.done(dve.after().tensor_scalar(NA, AC, -1.0, None, ALU.mult))
    fence()

    def heads(a):
        return a.rearrange("p (h d) -> p h d", d=64)

    def four(b):
        return b.ap.rearrange("p (g n) -> p g n", g=4)[:, :, 0:384].rearrange("p g (h d) -> p g h d", d=64)

    def g6(a):
        return a.rearrange("p (g h d) -> p g h d", g=4, d=64)

    def s6(a, c, d):
        return a[:, c * 48 + d * 24:c * 48 + d * 24 + 24].rearrange("p (g h) -> p g h", g=4).unsqueeze(3).to_broadcast([P, 4, 6, 64])

    def advance(d, c, first):
        m = dve.done(dve.after(pe.mark()).tensor_tensor(
            heads(XW), heads(XH[:, c, :]),
            WS[:, c * 48 + d * 24:c * 48 + d * 24 + 24].unsqueeze(2).to_broadcast([P, 24, 64]), ALU.mult))
        b = ps.take(4)
        pe.after(m)
        for g in range(4):
            last = mm(b.ap[:, g * 512:g * 512 + 384], BK[:, c, g * P:(g + 1) * P], XW[:, g * 384:(g + 1) * 384], True, True)
        m = pe.done(last)
        for g in range(4):
            hs = HS[d][:, g * 384:(g + 1) * 384]
            if first:
                m = dve.done(dve.after(m).tensor_copy(hs, b.ap[:, g * 512:g * 512 + 384]))
            else:
                e6 = ET[:, c * 48 + d * 24 + 6 * g:c * 48 + d * 24 + 6 * g + 6].unsqueeze(2).to_broadcast([P, 6, 64])
                m = dve.done(dve.after(m).tensor_tensor(heads(hs), heads(hs), e6, ALU.mult))
                m = dve.done(dve.after(m).tensor_tensor(hs, hs, b.ap[:, g * 512:g * 512 + 384], ALU.add))
        b.free(m)

    advance(0, 2, True)
    advance(0, 3, False)
    advance(1, 3, True)
    advance(1, 2, False)
    fence()

    def from_state(d, c, first):
        b = ps.take(4)
        pe.after(dve.mark())
        for g in range(4):
            last = mm(b.ap[:, g * 512:g * 512 + 384], CTt[:, g, c * P:(c + 1) * P], HS[d][:, g * 384:(g + 1) * 384], True, True)
        m = pe.done(last)
        for g in range(4):
            e6 = EA[:, c * 48 + d * 24 + 6 * g:c * 48 + d * 24 + 6 * g + 6].unsqueeze(2).to_broadcast([P, 6, 64])
            y = Y2[:, c, g * 384:(g + 1) * 384]
            if first:
                m = dve.done(dve.after(m).tensor_tensor(heads(y), heads(b.ap[:, g * 512:g * 512 + 384]), e6, ALU.mult))
            else:
                m = dve.done(dve.after(m).tensor_tensor(heads(XW[:, 0:384]), heads(b.ap[:, g * 512:g * 512 + 384]), e6, ALU.mult))
                m = dve.done(dve.after(m).tensor_tensor(y, y, XW[:, 0:384], ALU.add))
        b.free(m)

    from_state(0, 0, True)
    advance(0, 0, False)
    from_state(0, 1, True)
    from_state(1, 1, False)
    advance(1, 1, False)
    from_state(1, 0, False)
    fence()
    phase("ssddiag")
    CB = XW[:, 0:512]
    Dd = [XW[:, 512:1024], XW[:, 1024:1536], HS[0][:, 512:1024]]
    WW = [HS[0][:, 0:256], HS[0][:, 256:512]]
    xd = HS[1]
    for c in range(2):
        b = ps.take()
        pe.after(dve.mark())
        for g in range(4):
            last = mm(b.ap[:, g * P:(g + 1) * P], BT[:, g, c * P:(c + 1) * P], CTt[:, g, c * P:(c + 1) * P], True, True)
        m = pe.done(last)
        m = dve.done(dve.after(m).tensor_copy(CB, b.ap))
        b.free(m)
        m = dve.done(dve.after(m).tensor_tensor(heads(xd), heads(XH[:, c, :]), dsk.unsqueeze(2).to_broadcast([P, 24, 64]), ALU.mult))
        m = dve.done(dve.after(m).tensor_tensor(Y2[:, c, :], Y2[:, c, :], xd, ALU.add))
        got, obs = {}, {}

        def decays(u):
            b = ps.take()
            for hh in range(2):
                for d in range(2):
                    o = b.ap[:, (hh * 2 + d) * P:(hh * 2 + d + 1) * P]
                    col = c * 48 + d * 24 + 2 * u + hh
                    mm(o, DA[:, col:col + 1].to_broadcast([P, P]), KC[:, (C_LE, C_GE)[d]:(C_LE, C_GE)[d] + P], True, False)
                    last = mm(o, ident, KC[:, (C_NF, C_NB)[d]:(C_NF, C_NB)[d] + P], False, True)
            m = pe.done(last)
            dd = Dd[u % 3]
            act.after(m, got.get(("w", u - 3)))
            for hh in range(2):
                for d in range(2):
                    col = c * 48 + d * 24 + 2 * u + hh
                    sl = slice((hh * 2 + d) * P, (hh * 2 + d + 1) * P)
                    m = act.done(nc.scalar.activation(dd[:, sl], b.ap[:, sl], ACT.Exp, bias=NA[:, col:col + 1]))
            b.free(m)
            got["d", u] = m

        def weigh(u):
            dd, ww = Dd[u % 3], WW[u % 2]
            dve.after(got["d", u], got.get(("y", u - 2)))
            for hh in range(2):
                cf = c * 48 + 2 * u + hh
                wv = ww[:, hh * P:(hh + 1) * P]
                dve.done(dve.after().tensor_scalar(wv, dd[:, hh * 256:hh * 256 + P], DT[:, cf:cf + 1], None, ALU.mult))
                dve.done(dve.after().scalar_tensor_tensor(out=wv, in0=dd[:, hh * 256 + P:hh * 256 + 256],
                                                          scalar=DT[:, cf + 24:cf + 25], in1=wv, op0=ALU.mult, op1=ALU.add))
            w2_ = ww.rearrange("p (a b) -> p a b", a=2)
            got["w", u] = dve.done(dve.after().tensor_tensor(
                w2_, w2_, CB[:, (u // 3) * P:(u // 3 + 1) * P].unsqueeze(1).to_broadcast([P, 2, P]), ALU.mult))

        def products(u):
            g = u // 3
            if u % 3 == 0:
                obs[g] = ps.take()
            pe.after(got["w", u])
            for hh in range(2):
                h = 2 * u + hh
                last = mm(obs[g].ap[:, (h % 6) * 64:(h % 6 + 1) * 64], WW[u % 2][:, hh * P:(hh + 1) * P],
                          XH[:, c, h * 64:(h + 1) * 64], True, True)
            got["y", u] = m = pe.done(last)
            if u % 3 == 2:
                y = Y2[:, c, g * 384:(g + 1) * 384]
                m = dve.done(dve.after(m).tensor_tensor(y, y, obs[g].ap[:, 0:384], ALU.add))
                obs[g].free(m)

        staggered(12, decays, weigh, products)
    phase("zgate")
    smat[0] = 0
    at[0] = base
    fence()
    take(2048 + 1024 + 2 * 1536)
    take(2 * 1536)
    at3 = at[0]
    at[0] = base
    YT = take(12 * 256).rearrange("p (c t) -> p c t", c=12)
    at[0] = at3
    zz = [take(512) for _ in range(2)]
    sn = take(1536)
    m_sn = broadcast_load(sn, I["ssd_norm_2"][0], 1536)
    for n in range(3):
        w, mw, k = ring.take(("z", n))
        for c in range(2):
            b, m = project(w, [mw], HT, c)
            last = m
            m = act.done(act.after(m, dve.mark()).activation(zz[c], b.ap, ACT.Silu))
            b.free(m)
            y = Y2[:, c, n * 512:n * 512 + 512]
            m = dve.done(dve.after(m).tensor_tensor(y, y, zz[c], ALU.mult))
        ring.free(k, last)
    rs = small(8)
    junk = take(1536)
    m = rstd_of([Y2[:, c, :] for c in range(2)], 1536, [m], rs, junk)
    for c in range(2):
        m = dve.done(dve.after(m, m_sn).scalar_tensor_tensor(out=Y2[:, c, :], in0=Y2[:, c, :], scalar=rs[:, c:c + 1], in1=sn,
                                                             op0=ALU.mult, op1=ALU.mult))
    tm = turn_all(YT, Y2, [0, 1], {0: m, 1: m}, n=12)
    at[0] = base + 12 * 256
    fence(*tm)
    SB = take(2 * D).rearrange("p (c n) -> p c n", c=2)
    FBR = take(2 * D).rearrange("p (c n) -> p c n", c=2)
    UF = take(2 * 512).rearrange("p (c n) -> p c n", c=2)
    V1 = take(4 * 512).rearrange("p (g n) -> p g n", g=4)
    FT = take(4 * 256).rearrange("p (g t) -> p g t", g=4)
    dft = take(1280)
    bgt = take(2 * D)[0:1, :]
    m_df = w_s.sent(nc.gpsimd.dma_start(dft, I["consts"][:, C_DL:C_DL + 1280]))
    m_df = w_s.sent(nc.gpsimd.dma_start(bgt, I["b_gate_2"][0].rearrange("a b -> (a b)").rearrange("(a b) -> a b", a=1)))
    phase("branches")
    for h in range(2):
        w, mw, k = ring.take(("sso", 0, h))
        w_, mw_, k_ = ring.take(("sso", 1, h))
        for c in range(2):
            b = ps.take()
            pe.after(mw, mw_)
            for kk_ in range(12):
                last = mm(b.ap, YT[:, kk_, c * P:(c + 1) * P], w[:, kk_, :] if kk_ < 8 else w_[:, kk_ - 8, :], kk_ == 0, kk_ == 11)
            m = pe.done(last)
            last = m
            m = evac(SB[:, c, h * 512:h * 512 + 512], b.ap, m)
            b.free(m)
        ring.free(k, last)
        ring.free(k_, last)
    w, mw, k = ring.take(("uf", 0))
    um = []
    for c in range(2):
        b, m = project(w, [mw], HT, c)
        last = m
        m = evac(UF[:, c, :], b.ap, m)
        um.append(m)
        b.free(m)
    ring.free(k, last)
    vm = []
    for g in range(4):
        b = ps.take()
        pe.after(m_df, *um)
        for c in range(2):
            last = mm(b.ap, UF[:, c, g * P:(g + 1) * P], dft[:, c * 512:c * 512 + 512], c == 0, c == 1)
        m = pe.done(last)
        m = evac(V1[:, g, :], b.ap, m)
        vm.append(m)
        b.free(m)
    fmk = []
    for g in range(4):
        b = ps.take()
        pe.after(*vm)
        for c in range(2):
            last = mm(b.ap[:, 0:256], dft[:, 1024 + c * P:1024 + (c + 1) * P], V1[:, g, c * 256:c * 256 + 256], c == 0, c == 1)
        m = pe.done(last)
        m = evac(FT[:, g, :], b.ap[:, 0:256], m)
        fmk.append(m)
        b.free(m)
    for h in range(2):
        w, mw, k = ring.take(("four", h))
        for c in range(2):
            b, m = project(w, [mw] + fmk, FT, c, K=4)
            last = m
            m = evac(FBR[:, c, h * 512:h * 512 + 512], b.ap, m)
            b.free(m)
        ring.free(k, last)
    fence()
    gt2 = [V1[:, 0, :], V1[:, 1, :]]
    MG = FBR
    for n in (0, 2, 1, 3):
        w, mw, k = ring.take(("gate", n))
        for c in range(2):
            b = ps.take()
            pe.after(mw)
            mm(b.ap, ones[0:1, :], bgt[:, n * 512:n * 512 + 512], True, False)
            for k8 in range(8):
                last = mm(b.ap, HT[:, k8, c * P:(c + 1) * P], w[:, k8, :], False, k8 == 7)
            m = pe.done(last)
            last = m
            m = act.done(act.after(m, dve.mark()).activation(gt2[c], b.ap, ACT.Sigmoid))
            b.free(m)
            sl = slice((n % 2) * 512, (n % 2) * 512 + 512)
            src = (FBR, SB)[n // 2][:, c, sl]
            m = dve.done(dve.after(m).tensor_tensor(src, src, gt2[c], ALU.mult))
            if n >= 2:
                m = dve.done(dve.after(m).tensor_tensor(FBR[:, c, sl], FBR[:, c, sl], src, ALU.add))
        ring.free(k, last)
    MT = YT[:, 0:8, :]
    tm = turn_all(MT, MG, [0, 1], {0: m, 1: m})
    mixed = []
    for h in range(2):
        w, mw, k = ring.take(("wout", h))
        for c in range(2):
            b, m = project(w, [mw] + tm, MT, c)
            last = m
            m = evac(SB[:, c, h * 512:h * 512 + 512], b.ap, m)
            mixed.append(m)
            b.free(m)
        ring.free(k, last)

    def add_normed(src, row, marks, junk, rs):
        m = rstd_of([src[:, c, :] for c in range(2)], D, marks, rs, junk)
        g, mg = spread(row)
        for c in range(2):
            m = dve.done(dve.after(m, mg).scalar_tensor_tensor(out=src[:, c, :], in0=src[:, c, :], scalar=rs[:, c:c + 1],
                                                               in1=g.ap, op0=ALU.mult, op1=ALU.mult))
            m = dve.done(dve.after(m).tensor_tensor(X[:, c, :], X[:, c, :], src[:, c, :], ALU.add))
        g.free(m)

    fence()
    add_normed(SB, 4, mixed, V1.rearrange("p g n -> p (g n)")[:, 0:D], rs)
    phase("ecroute")
    at[0] = 0
    smat[0] = 0
    fence()
    rs, rw = small(8), small(8 * 16)
    w_r = w_s.sent(nc.gpsimd.dma_start(rw.rearrange("p (c e) -> p c e", c=8),
                                       I["w_router_2"][0].rearrange("(c p) e -> p c e", p=P)))
    XE = take(8 * 512).rearrange("p (c s) -> p c s", c=8)
    SWT = take(4 * 256).rearrange("p (g t) -> p g t", g=4)
    YE = take(4 * D).rearrange("p (g n) -> p g n", g=4)
    base2 = at[0]
    H = take(2 * D).rearrange("p (c d) -> p c d", c=2)
    HT2 = take(8 * 256).rearrange("p (c t) -> p c t", c=8)
    junk = take(D)
    SS = take(2 * 512).rearrange("p (c e s) -> p c e s", c=2, e=16)
    SW = take(2 * 512).rearrange("p (c e s) -> p c e s", c=2, e=16)
    m16 = take(1024)
    marks = modulated(H, xc, 6, 8, junk, rs)
    tm = turn_all(HT2, H, xc, marks)
    b = ps.take()
    pe.after(w_r, *tm)
    for c in xc:
        for k in range(8):
            last = mm(b.ap[:, c * 16:c * 16 + 16], HT2[:, k, c * P:(c + 1) * P],
                      rw.rearrange("p (c e) -> p c e", c=8)[:, k, :], k == 0, k == 7)
    m = pe.done(last)
    af, rm = small(32), small(2)
    a3 = af.rearrange("p (c e) -> p c e", c=2)
    m = dve.done(dve.after(m).tensor_copy(af, b.ap[:, 0:32]))
    b.free(m)
    dve.done(dve.after().tensor_reduce(rm, a3, AX.X, ALU.max))
    m = dve.done(dve.after().tensor_tensor(a3, a3, rm.unsqueeze(2).to_broadcast([P, 2, 16]), ALU.subtract))
    m = act.done(act.after(m).activation(af, af, ACT.Exp))
    dve.done(dve.after(m).tensor_reduce(rm, a3, AX.X, ALU.add))
    dve.done(dve.after().reciprocal(rm, rm))
    m = dve.done(dve.after().tensor_tensor(a3, a3, rm.unsqueeze(2).to_broadcast([P, 2, 16]), ALU.mult))
    b = ps.take()
    pe.after(m)
    for c in xc:
        last = nc.tensor.transpose(b.ap[0:16, c * P:(c + 1) * P], af[:, c * 16:c * 16 + 16], ident)
    m = pe.done(last)
    wk_, pz, mv = m16[0:16, 0:256], m16[0:16, 256:512], m16[0:16, 512:520]
    m = dve.done(dve.after(m).tensor_copy(wk_, b.ap[0:16, 0:256]))
    b.free(m)
    for r in range(4):
        dve.done(dve.after().max(mv, wk_))
        m = dve.done(dve.after().match_replace(wk_, mv, wk_, -1.0))
    dve.done(dve.after().tensor_scalar(wk_, wk_, 0.0, None, ALU.is_lt))
    dve.done(dve.after().tensor_tensor_scan(pz[:, 0:P], ones[0:16, :], wk_[:, 0:P], 0.0, ALU.mult, ALU.add))
    dve.done(dve.after().tensor_tensor_scan(pz[:, P:256], ones[0:16, :], wk_[:, P:256], pz[:, P - 1:P], ALU.mult, ALU.add))
    dve.done(dve.after().tensor_tensor(pz, pz, wk_, ALU.mult))
    m = dve.done(dve.after().tensor_scalar(pz, pz, 1.0, None, ALU.subtract))
    b = ps.take()
    pe.after(m)
    for c in xc:
        last = nc.tensor.transpose(b.ap[:, c * 16:c * 16 + 16], pz[:, c * P:(c + 1) * P], ident[0:16, 0:16])
    m = pe.done(last)
    pt = small(32)
    m = dve.done(dve.after(m).tensor_copy(pt, b.ap[:, 0:32]))
    b.free(m)
    for c in xc:
        m = dve.done(dve.after(m).tensor_tensor(
            SS[:, c, :, :], KC[:, C_IOTA:C_IOTA + 32].unsqueeze(1).to_broadcast([P, 16, 32]),
            pt[:, c * 16:c * 16 + 16].unsqueeze(2).to_broadcast([P, 16, 32]), ALU.is_equal))
        m = dve.done(dve.after(m).tensor_tensor(
            SW[:, c, :, :], SS[:, c, :, :], a3[:, c, :].unsqueeze(2).to_broadcast([P, 16, 32]), ALU.mult))
    fence()
    for k in range(8):
        b = ps.take()
        for c in xc:
            last = mm(b.ap, H[:, c, k * P:(k + 1) * P], SS[:, c, :, :].rearrange("p e s -> p (e s)"), c == 0, c == 1)
        m = pe.done(last)
        m = evac(XE[:, k, :], b.ap, m)
        b.free(m)
    for c in xc:
        turned(SWT[:, :, c * P:(c + 1) * P], SW[:, c, :, :].rearrange("p e s -> p (e s)"), 4, None)
    at[0] = base2
    phase("ecmoe")
    fence()
    hid = [take(D) for _ in range(2)]
    hidT = [take(D).rearrange("p (c s) -> p c s", c=8) for _ in range(2)]
    for g in range(4):
        i = g % 2
        bg, bu = ps.take(2), ps.take(2)
        for j in range(4):
            e = 4 * g + j
            pr = slice(32 * j, 32 * j + 32)
            for h in range(2):
                sl = slice(h * 512, h * 512 + 512)
                for mt, bb in (("g", bg), ("u", bu)):
                    w, mw, k = ring.take((2, e, mt, h))
                    pe.after(mw)
                    for c in range(8):
                        last = mm(bb.ap[pr, sl], XE[:, c, e * 32:e * 32 + 32], w[:, c, :], c == 0, c == 7)
                    m = pe.done(last)
                    ring.free(k, m)
        m_u = m
        m = act.done(act.after(m).activation(hid[i], bg.ap, ACT.Silu))
        bg.free(m)
        m = dve.done(dve.after(m, m_u).tensor_tensor(hid[i], hid[i], bu.ap, ALU.mult))
        bu.free(m)
        last_marks.clear()
        turned(hidT[i], hid[i], 8, m)
        hm_ = list(last_marks)
        for h in range(2):
            sl = slice(h * 512, h * 512 + 512)
            b = ps.take()
            pe.after(*hm_)
            for j in range(4):
                w, mw, k = ring.take((2, 4 * g + j, "d", h))
                pe.after(mw)
                for c in range(8):
                    last = mm(b.ap[32 * j:32 * j + 32, :], hidT[i][:, c, 32 * j:32 * j + 32], w[:, c, :], c == 0, c == 7)
                m = pe.done(last)
                ring.free(k, m)
            m = evac(YE[:, g, sl], b.ap, m)
            b.free(m)
    fence()
    phase("final")
    F2 = XE.rearrange("p c s -> p (c s)")[:, 0:2 * D].rearrange("p (c n) -> p c n", c=2)
    fm_ = []
    for c in xc:
        for h in range(2):
            b = ps.take()
            for g in range(4):
                last = mm(b.ap, SWT[:, g, c * P:(c + 1) * P], YE[:, g, h * 512:h * 512 + 512], g == 0, g == 3)
            m = pe.done(last)
            m = evac(F2[:, c, h * 512:h * 512 + 512], b.ap, m)
            fm_.append(m)
            b.free(m)
    add_normed(F2, 10, fm_, hid[0], rs)
    fence()
    finish(None)


_INS = ['x', 'c', 'ctx', 'c_ctx', 'ada_w', 'ada_b', 'norm_mix_g', 'norm_ffn_g', 'even_w_in', 'even_w_out',
        'hgrn_lb_logits', 'hgrn_onorm_g', 'diff_lambda', 'diff_subln_g', 'odd_w_qkv', 'odd_w_out', 'swa_sink',
        'router_w', 'router_b', 'moe_w_gate', 'moe_w_up', 'moe_w_down', 'final_norm_g', 'c_2', 'ctx_2', 'c_ctx_2',
        'w_mod_2', 'b_mod_2', 'norm_mix_pre_2', 'norm_mix_post_2', 'norm_ffn_pre_2', 'norm_ffn_post_2', 'w_in_2',
        'conv_w_2', 'conv_b_2', 'dt_bias_2', 'a_log_2', 'd_skip_2', 'ssd_norm_2', 'w_fourier_2', 'w_ssd_out_2',
        'b_gate_2', 'w_out_2', 'w_router_2', 'w_e_gate_2', 'w_e_up_2', 'w_e_down_2']


def kernel(**inputs):
    import concourse.bacc as _bacc
    from concourse.bass_utils import run_bass_kernel_spmd as _run

    nc = _bacc.Bacc("TRN2", target_bir_lowering=False, num_devices=1)
    arrays, ins = {}, {}
    for name in _INS + ["consts"]:
        a = constants() if name == "consts" else np.ascontiguousarray(inputs[name])
        arrays[f"in_{name}"] = a
        ins[name] = nc.dram_tensor(f"in_{name}", a.shape, F32, kind="ExternalInput").ap()
    out = nc.dram_tensor("out_0", (1, 256, 1024), F32, kind="ExternalOutput").ap()
    program(nc, ins, out)
    r = _run(nc, [arrays], core_ids=[0])
    return r.results[0]["out_0"]
```

```python
import math
from contextlib import ExitStack

import numpy as np
import concourse.bass as bass
from concourse import mybir

P = 128
D = 1024
NS = 5
SLOT = 8 * 512
F32 = mybir.dt.float32
U32 = mybir.dt.uint32
I32 = mybir.dt.int32
F32R = mybir.dt.float32r
ALU = mybir.AluOpType
ACT = mybir.ActivationFunctionType
AX = mybir.AxisListType
EPS = 1e-6
BIG = 1e30
XROWS = 23 * P

C_ID, C_LE, C_LT, C_GE, C_COS, C_SIN, C_ROT, C_NF, C_NB = 0, 128, 256, 384, 512, 768, 1024, 1152, 1280
C_IOTA, C_ONE, C_EX, C_GW, C_REP, C_SUM = 1408, 1440, 1441, 1457, 1461, 1473
C_KEEP = 1485
C_LEV = 1488
C_SWA = C_LEV + 15 * 128
C_DL = C_SWA + 1024
C_DW = C_DL + 1024
C_END = C_DW + 256


def constants():
    c = np.zeros((P, C_END), np.float32)
    i = np.arange(P)
    c[:, C_ID:C_ID + P] = np.eye(P)
    c[:, C_LE:C_LE + P] = i[:, None] <= i[None]
    c[:, C_LT:C_LT + P] = i[:, None] < i[None]
    c[:, C_GE:C_GE + P] = i[:, None] >= i[None]
    c[:, C_NF:C_NF + P] = np.where(i[:, None] <= i[None], 0, -BIG)
    c[:, C_NB:C_NB + P] = np.where(i[:, None] >= i[None], 0, -BIG)
    t = np.arange(256)
    inv = (1.0 / (np.float32(10000.0) ** (np.arange(0, 32, 2, dtype=np.float32) / np.float32(32)))).astype(np.float32)
    ar = (t // 64).astype(np.float32)[:, None] * inv
    ac = (t % 64).astype(np.float32)[:, None] * inv
    ang = np.concatenate([ar, ar, ac, ac], axis=-1).astype(np.float32)
    c[:, C_COS:C_COS + 256] = np.tile(np.cos(ang).T, (2, 1))
    c[:, C_SIN:C_SIN + 256] = np.tile(np.sin(ang).T, (2, 1))
    r = np.zeros((P, P), np.float32)
    for b in range(0, P, 32):
        for j in range(16):
            r[b + j, b + 16 + j] = -1
            r[b + 16 + j, b + j] = 1
    c[:, C_ROT:C_ROT + P] = r.T
    c[:, C_IOTA:C_IOTA + 32] = np.arange(32)
    c[[2, 3, 8, 9], C_ONE] = 1
    c[:, C_EX:C_EX + 16] = np.arange(16)
    c[:, C_GW:C_GW + 4] = [4, 3, 2, 1]
    for j in range(6):
        c[j, C_REP + 2 * j:C_REP + 2 * j + 2] = 1
    for q in range(4):
        c[32 * q:32 * q + 12, C_SUM:C_SUM + 12] = np.eye(12)
    lev = []
    for b in (64, 32, 16, 8, 4, 2, 1):
        lev.append((i[:, None] // (2 * b) == i[None] // (2 * b)) & (i[:, None] // b % 2 == 0) & (i[None] // b % 2 == 1))
    allm = lev + [m.T for m in lev] + [np.eye(P, dtype=bool)]
    for n, m in enumerate(allm):
        c[:, C_LEV + n * P:C_LEV + (n + 1) * P] = m
    for q in range(2):
        ok = np.abs((q * P + i)[:, None] - t[None]) <= 128
        c[:, C_SWA + q * 512:C_SWA + q * 512 + 256] = np.where(ok, 0, -BIG)
    ll = 2 * np.pi * (np.outer(t, t) % 256) / 256
    s = 1 / math.sqrt(256 * 128)
    for q in range(2):
        c[:, C_DL + q * 512:C_DL + q * 512 + 256] = (np.cos(ll) * s)[q * P:(q + 1) * P]
        c[:, C_DL + q * 512 + 256:C_DL + (q + 1) * 512] = (np.sin(ll) * s)[q * P:(q + 1) * P]
    lw = 2 * np.pi * (np.outer(i, i) % 128) / 128
    c[:, C_DW:C_DW + P] = np.cos(lw)
    c[:, C_DW + P:C_DW + 2 * P] = -np.sin(lw)
    return c


class Lane:

    def __init__(self, eng, sem, own):
        self.eng, self.sem, self.n, self.own, self.met = eng, sem, 0, own, {}

    def after(self, *marks):
        for m in marks + ((self.mark(),) if self.own and self.n else ()):
            if m is not None and self.met.get(m[0], 0) < m[2]:
                self.eng.wait_ge(m[1], m[2])
                self.met[m[0]] = m[2]
        return self.eng

    def apart(self, *marks):
        own, self.own = self.own, False
        eng = self.after(*marks)
        self.own = own
        return eng

    def done(self, ins):
        ins.then_inc(self.sem, 1)
        self.n += 1
        return self.mark()

    def mark(self):
        return (id(self.sem), self.sem, self.n)


class Wire:

    def __init__(self, sem):
        self.sem, self.n = sem, 0

    def sent(self, ins):
        ins.then_inc(self.sem, 16)
        self.n += 16
        return (id(self.sem), self.sem, self.n)


class Banks:

    def __init__(self, ap, lane):
        self.ap, self.lane, self.at, self.freed = ap, lane, 0, [()] * 8

    def take(self, n=1):
        at = -(-self.at // n) * n % 8
        for _ in range(8 // n):
            if all(self.freed[b] is not None for b in range(at, at + n)):
                break
            at = (at + n) % 8
        self.at = (at + n) % 8
        for b in range(at, at + n):
            assert self.freed[b] is not None, "bank in use"
            self.lane.after(*self.freed[b])
            self.freed[b] = None
        return Bank(self, at, n)


class Bank:
    def __init__(self, banks, at, n):
        self.banks, self.at, self.n = banks, at, n
        self.ap = banks.ap[:, at * 512:(at + n) * 512]

    def free(self, *marks):
        for b in range(self.at, self.at + self.n):
            self.banks.freed[b] = marks


class Ring:

    def __init__(self, ap, lane, sems, plan, ends):
        self.lane, self.plan, self.ends = lane, plan, sorted(ends)
        self.ap = ap
        self.slots = [ap[:, n, :] for n in range(NS)]
        self.wires = [Wire(s) for s in sems]
        self.marks, self.at, self.next, self.place, self.once = {}, 0, 0, {}, set()
        for n in range(NS):
            self.send(n)

    def send(self, slot, *marks):
        n = self.next
        if n >= self.ends[0]:
            return
        self.next += 1
        self.place[n] = slot
        _, src, k, cols = self.plan[n]
        dst = self.view(n)[:, 0:k, 0:cols]
        self.lane.after(*marks)
        self.marks[n] = self.wires[slot].sent(self.lane.eng.dma_start(dst, src))

    def view(self, n):
        return self.slots[self.place[n]].rearrange("p (c n) -> p c n", c=8)

    def take(self, key):
        n = self.at
        assert self.plan[n][0] == key, (self.plan[n][0], key)
        self.at += 1
        return self.view(n), self.marks[n], n

    def free(self, n, mark):
        slot = self.place[n]
        if slot not in self.once:
            self.send(slot, mark)

    def widen(self, tiles, once, *marks):
        assert len(self.slots) == NS
        for tile in tiles + once:
            self.slots.append(tile)
            if tile is not None and any(tile is t for t in once):
                self.once.add(len(self.slots) - 1)
            self.send(len(self.slots) - 1, *marks)

    def resume(self, *marks):
        n = self.ends.pop(0)
        assert self.at == n == self.next
        del self.slots[NS:]
        self.once.clear()
        for i in range(NS):
            self.send(i, *marks)


def program(nc, I, out):
    ctx = ExitStack()
    sb = lambda name, shape, dt=F32: ctx.enter_context(nc.sbuf_tensor(name, shape, dt))
    sem = lambda name: ctx.enter_context(nc.semaphore(name))
    pe = Lane(nc.tensor, sem("s_pe"), False)
    dve = Lane(nc.vector, sem("s_dve"), True)
    act = Lane(nc.scalar, sem("s_act"), True)
    pool = Lane(nc.gpsimd, sem("s_pool"), True)
    sp = Lane(nc.sync, sem("s_sp"), False)

    ringt = sb("ring", [P, NS, SLOT])
    X = sb("X", [P, 4, D])
    MOD = sb("MOD", [12, D])
    KC = sb("KC", [P, C_KEEP])
    ones = sb("ones", [P, P])
    CT = sb("CT", [P, 32])
    CP = sb("CP", [P, 2, 8, 42])
    SM = sb("SM", [P, 2304])
    XS = sb("XS", [P, 4])
    SQ = sb("SQ", [P, D], mybir.dt.bfloat16)
    DST = sb("DST", [P, 8], U32)
    OE = sb("OE", [1, 16], I32)
    ar_words = 22360
    arena = {}
    PSt = ctx.enter_context(nc.psum_tensor("PS", [P, 4096], F32))
    ps = Banks(PSt[:, :], pe)
    XP = nc.dram_tensor("XP", [XROWS, D], F32).ap()
    YP = nc.dram_tensor("YP", [XROWS, D], F32).ap()

    M0 = nc.dram_tensor("M0", [12, D], F32).ap()
    M1 = nc.dram_tensor("M1", [12, D], F32).ap()
    M2 = nc.dram_tensor("M2", [12, D], F32).ap()
    HD = nc.dram_tensor("HD", [P, 8 * 512], F32).ap()
    ident = KC[:, C_ID:C_ID + P]
    at, rat = [0], [0]

    def lay_out(parts=0, keep=0):
        if arena:
            arena["stack"].close()
            if arena["keep"] != keep:
                arena["base"].close()
        n = arena["n"] = arena.get("n", 0) + 1
        if arena.get("keep", -1) != keep:
            arena["keep"], arena["base"] = keep, ExitStack()
            if keep:
                arena["k"] = arena["base"].enter_context(nc.sbuf_tensor(f"AK{n}", [P, keep], F32))
        stack = arena["stack"] = ExitStack()
        arena["words"], arena["parts"] = ar_words - parts, parts
        if parts:
            arena["r"] = stack.enter_context(nc.sbuf_tensor(f"AP{n}", [P, parts], F32R))
        arena["f"] = stack.enter_context(nc.sbuf_tensor(f"AR{n}", [P, ar_words - parts - keep], F32))
        at[0] = rat[0] = 0

    KEEP, PARTS = 9984, 8192 + 4096
    lay_out(PARTS, KEEP)

    def take(n):
        a = at[0]
        at[0] += n
        assert at[0] <= arena["words"], at[0]
        keep = arena["keep"]
        if a < keep:
            assert at[0] <= keep, (a, n)
            return arena["k"][:, a:a + n]
        return arena["f"][:, a - keep:a - keep + n]

    def take_parts(n):
        a = rat[0]
        rat[0] += 2 * n
        assert rat[0] <= arena["parts"], rat[0]
        return arena["r"][:, a:a + n], arena["r"][:, a + n:a + 2 * n]

    smat, sm_top = [0], [2304]

    def small(n):
        a = smat[0]
        smat[0] += n
        assert smat[0] <= sm_top[0], smat[0]
        return SM[:, a:a + n]

    def fence(*more):
        marks = [x.mark() for x in (pe, dve, act, pool) if x.n] + list(more)
        for x in (pe, dve, act, pool):
            x.after(*marks)
        return marks

    def mm(o, l, r, start, stop, **kw):
        return nc.tensor.matmul(o, l, r, start=start, stop=stop, **kw)

    flip = [0]

    def evac(dst, src, *marks):
        flip[0] ^= 1
        if flip[0]:
            return dve.done(dve.apart(*marks).tensor_copy(dst, src))
        return act.done(act.apart(*marks).copy(dst, src))

    def halve(high, low, src, *marks):
        m = act.done(act.apart(*marks).copy(high, src))
        return dve.done(dve.apart(m).tensor_tensor(low, src, high.bitcast(F32), ALU.subtract))

    class Cutter:

        def __init__(self, units, bufs, take, spent):
            self.units, self.bufs, self.take, self.spent = units, bufs, take, spent
            self.got, self.ready, self.freed, self.left = {}, [], [], {}
            for key, _ in units:
                self.left[key] = self.left.get(key, 0) + 1
            self.advance()

        def advance(self):
            nb = len(self.bufs)
            while len(self.ready) < min(len(self.units), len(self.freed) + nb):
                i = len(self.ready)
                key, q = self.units[i]
                if key not in self.got:
                    self.got[key] = self.take(key)
                w, mw, k = self.got[key]
                h, l = self.bufs[i % nb]
                m = halve(h, l, w[:, 2 * q:2 * q + 2, :], mw, self.freed[i - nb] if i >= nb else None)
                self.left[key] -= 1
                if not self.left[key]:
                    self.spent(k, m)
                self.ready.append((h, l, m))

        def product_T(self, outs, parts, *marks):
            i = len(self.freed)
            q = self.units[i][1]
            h, l, m = self.ready[i]
            xh, xl = parts
            pe.after(m, *marks)
            for j, o in enumerate(outs):
                sl = slice(j * P, (j + 1) * P)
                for c in range(2):
                    k = 2 * q + c
                    mm(o, h[:, c, sl], xh[:, k, :], k == 0, False)
                    mm(o, h[:, c, sl], xl[:, k, :], False, False)
                    ins = mm(o, l[:, c, sl], xh[:, k, :], False, k == 7)
            m = pe.done(ins)
            self.freed.append(m)
            self.advance()
            return m

        def product(self, outs, parts, first, last, *marks):
            i = len(self.freed)
            q = self.units[i][1]
            h, l, m = self.ready[i]
            pe.after(m, *marks)
            for o, (th, tl) in zip(outs, parts):
                for c in range(2):
                    s_, e_ = first and c == 0, last and c == 1
                    mm(o, th(2 * q + c), h[:, c, :], s_, False)
                    mm(o, th(2 * q + c), l[:, c, :], False, False)
                    ins = mm(o, tl(2 * q + c), h[:, c, :], False, e_)
            m = pe.done(ins)
            self.freed.append(m)
            self.advance()
            return m

    def cols(w, n, k0=0, k=8, width=512):
        return w[k0:k0 + k * P, n:n + width].rearrange("(c p) n -> p c n", p=P)

    plan = []

    def add(key, src, k=8, width=512):
        plan.append((key, src, k, width))

    ada, win, wo = I["ada_w"], I["even_w_in"][0], I["even_w_out"][0]
    moe = {"g": I["moe_w_gate"], "u": I["moe_w_up"], "d": I["moe_w_down"]}

    def add_ada(tag, w, js):
        for h in range(2):
            for j in js:
                add((tag, j, h), cols(w, 1024 * j + 512 * h))

    def add_moe(layer, order):
        for e in range(16):
            for m, h in order:
                add((layer, e, m, h), cols(moe[m][layer, e], 512 * h))
        ends.append(len(plan))

    ends = []
    WIDE = (("g", 0), ("u", 0), ("g", 1), ("u", 1), ("d", 0), ("d", 1))
    PAIRS = (("g", 0), ("g", 1), ("u", 0), ("u", 1), ("d", 0), ("d", 1))
    add_ada("ada0", ada[0], range(2))
    for n in range(4):
        add(("in", n), cols(win, 512 * n))
    add_ada("ada0", ada[0], range(2, 6))
    add_ada("ada1", ada[1], range(6))
    add_ada("ada2", I["w_mod_2"][0], range(6))
    for n in range(4, 8):
        add(("in", n), cols(win, 512 * n))
    for n in range(2):
        add(("wo", n), cols(wo, 512 * n))
    add_moe(0, WIDE)
    for n in range(3):
        add(("qkv", n), cols(I["odd_w_qkv"][0], 512 * n))
    for n in range(2):
        add(("owo", n), cols(I["odd_w_out"][0], 512 * n))
    add_moe(1, PAIRS)
    w2 = I["w_in_2"][0]
    add(("dt", 0), cols(w2, 4608, width=48), width=48)
    for n in range(5):
        add(("xbc", n), cols(w2, 2048 + 512 * n))
    for n in range(3):
        add(("z", n), cols(w2, 512 + 512 * n))
    for h in range(2):
        add(("sso", 0, h), cols(I["w_ssd_out_2"][0], 512 * h))
        add(("sso", 1, h), cols(I["w_ssd_out_2"][0], 512 * h, k0=1024, k=4), k=4)
    add(("uf", 0), cols(w2, 0))
    for h in range(2):
        add(("four", h), cols(I["w_fourier_2"][0], 512 * h, k=4), k=4)
    for n in (0, 2, 1, 3):
        add(("gate", n), cols(w2, 4656 + 512 * n))
    for h in range(2):
        add(("wout", h), cols(I["w_out_2"][0], 512 * h))
    for g in range(4):
        for h in range(2):
            for e in range(4 * g, 4 * g + 4):
                for m in "gu":
                    add((2, e, m, h), cols(I["w_e_gate_2" if m == "g" else "w_e_up_2"][0, e], 512 * h))
        for h in range(2):
            for e in range(4 * g, 4 * g + 4):
                add((2, e, "d", h), cols(I["w_e_down_2"][0, e], 512 * h))

    ends.append(len(plan))

    w_x, w_k, w_c, w_s = Wire(sem("w_x")), Wire(sem("w_k")), Wire(sem("w_c")), Wire(sem("w_s"))
    w_x2, w_m, w_t, w_h = Wire(sem("w_x2")), Wire(sem("w_m")), Wire(sem("w_t")), Wire(sem("w_h"))
    w_v, w_vx, w_vy = [Wire(sem(f"w_v{n}")) for n in range(NS)], Wire(sem("w_vx")), Wire(sem("w_vy"))
    w_z, w_xe = Wire(sem("w_z")), [Wire(sem("w_xe0")), Wire(sem("w_xe1"))]
    w_sc, w_y, w_g, w_o = Wire(sem("w_sc")), [Wire(sem("w_y0")), Wire(sem("w_y1"))], [Wire(sem(f"w_g{n}")) for n in range(4)], Wire(sem("w_o"))
    AR = arena["k"]
    crow = AR[0:32, 0:P]
    for n, name in enumerate(("c", "c_ctx", "c_2", "c_ctx_2")):
        v = I[name] if name in ("c_ctx", "c_ctx_2") else I[name][0]
        mc = w_c.sent(nc.sync.dma_start(AR[8 * n:8 * n + 8, 0:P], v.rearrange("(a b) -> a b", b=P)))
    mk = w_k.sent(nc.sync.dma_start(KC[:, :], I["consts"][:, 0:C_KEEP]))
    mx = w_x.sent(nc.sync.dma_start(X[:, 0:2, :], I["x"][0].rearrange("(c p) d -> p c d", p=P)))
    mx = w_x.sent(nc.sync.dma_start(X[:, 2:4, :], I["ctx"][0].rearrange("(c p) d -> p c d", p=P)))
    ring = Ring(ringt, sp, [sem(f"w_r{n}") for n in range(NS + 3)], plan, ends)

    m_one = dve.done(dve.after().memset(ones[:, :], 1.0))
    m_cp = dve.done(dve.after().memset(CP[:, :, :, :], 0.0))
    b = ps.take()
    pe.after(mc, mk)
    m = pe.done(nc.tensor.transpose(b.ap[:, 0:32], crow, ident[0:32, 0:32]))
    m = act.done(act.after(m).activation(CT[:, :], b.ap[:, 0:32], ACT.Silu))
    b.free(m)
    for half in range(2):
        for r in range(2):
            m_cp = dve.done(dve.after(m, m_cp).tensor_copy(
                CP[:, half, :, 10 + r], CT[:, 16 * half + 8 * r:16 * half + 8 * r + 8]))
    fence(mk)

    mod_last = [None]

    def modulation(tag, half, bias, gains, place, dst, js):
        sums, GB, br = place[:, 0:512], place[0:12, 512:1024], place[0:6, 1024:1536]
        m = mb = mod_last[0]
        for h in range(2):
            sl = slice(512 * h, 512 * h + 512)
            pool.after(m, mb)
            mg = pool.done(pool.eng.memset(GB, 1.0))
            pool.after(mg)
            mb = w_s.sent(nc.gpsimd.dma_start(br, bias.rearrange("(a b) -> a b", b=D)[:, sl]))
            for row, g in gains:
                for r in range(2):
                    mb = w_s.sent(nc.gpsimd.dma_start(GB[row + r:row + r + 1, :], g.rearrange("(a b) -> a b", a=1)[:, sl]))
            b = ps.take()
            for j in js:
                w, mw, k = ring.take((tag, j, h))
                pe.after(mw)
                for c in range(8):
                    q = c % 4
                    last = mm(b.ap[32 * q:32 * q + 32, :], CP[:, half, c, 10 - 2 * j:42 - 2 * j], w[:, c, :],
                              j == js[0] and c < 4, j == js[-1] and c > 3, skip_group_check=True)
                m2 = pe.done(last)
                ring.free(k, m2)
                yield
            m = dve.done(dve.after(m2, m).tensor_copy(sums, b.ap))
            b.free(m)
            b = ps.take()
            pe.after(m, mb)
            mm(b.ap[0:12, :], KC[:, C_SUM:C_SUM + 12], sums, True, False)
            m = pe.done(mm(b.ap[0:12, :], KC[0:6, C_REP:C_REP + 12], br, False, True))
            o = MOD[:, sl] if dst is None else GB
            m = dve.done(dve.after(m).scalar_tensor_tensor(
                out=o, in0=b.ap[0:12, :], scalar=KC[0:12, C_ONE:C_ONE + 1], in1=GB, op0=ALU.add, op1=ALU.mult))
            b.free(m)
            if dst is not None:
                act.after(m)
                mod_last[0] = m = w_m.sent(nc.scalar.dma_start(dst[:, sl], GB))
            yield

    def in_turns(*parts):
        parts = list(parts)
        while parts:
            for g in list(parts):
                for _ in g:
                    break
                else:
                    parts.remove(g)

    def every(n, g):
        for _ in g:
            for _ in range(n):
                yield

    def spread(row):
        b = ps.take(2)
        for h in range(2):
            last = mm(b.ap[:, h * 512:h * 512 + 512], ident[0:12, row:row + 1].to_broadcast([12, P]),
                      MOD[:, h * 512:h * 512 + 512], True, True)
        return b, pe.done(last)

    def rstd_of(srcs, width, marks, rs, junk):
        m = None
        for n, s in enumerate(srcs):
            if junk is not None:
                m = act.done(act.after(*marks).activation(junk, s, ACT.Square, accum_out=rs[:, n:n + 1]))
            else:
                m = act.mark()
        n = len(srcs)
        m = dve.done(dve.after(m).tensor_scalar(rs[:, 0:n], rs[:, 0:n], 1.0 / width, EPS, ALU.mult, ALU.add))
        m = act.done(act.after(m).activation(rs[:, 0:n], rs[:, 0:n], ACT.Sqrt))
        return dve.done(dve.after(m).reciprocal(rs[:, 0:n], rs[:, 0:n]))

    def modulated(H, chunks, shift, scale, junk, rs):
        m = rstd_of([X[:, c, :] for c in chunks], D, [dve.mark()], rs, junk)
        marks = {}
        for r in range(2):
            mine = [c for c in chunks if c // 2 == r]
            if not mine:
                continue
            a, ma = spread(scale + r)
            s, ms = spread(shift + r)
            for c in mine:
                n = chunks.index(c)
                m = dve.done(dve.after(m, ma).scalar_tensor_tensor(
                    out=H[:, c, :], in0=X[:, c, :], scalar=rs[:, n:n + 1], in1=a.ap, op0=ALU.mult, op1=ALU.mult))
                m = dve.done(dve.after(m, ms).tensor_tensor(H[:, c, :], H[:, c, :], s.ap, ALU.add))
                marks[c] = m
            a.free(m)
            s.free(m)
        return marks

    def turned(dst, src, n, mark):
        for j in range(0, n, 4):
            b = ps.take()
            pe.after(mark)
            for i in range(j, min(n, j + 4)):
                last = nc.tensor.transpose(b.ap[:, (i - j) * P:(i - j + 1) * P], src[:, i * P:(i + 1) * P], ident)
            m = pe.done(last)
            k = min(4, n - j)
            m = evac(dst[:, j:j + k, :], b.ap[:, 0:k * P].rearrange("p (a b) -> p a b", a=k), m)
            b.free(m)
            last_marks.append(m)
        return m

    last_marks = []

    def turn_all(HT, H, chunks, marks, n=8):
        last_marks.clear()
        for c in chunks:
            turned(HT[:, :, c * P:(c + 1) * P], H[:, c, :], n, marks[c])
        out_marks = list(last_marks)
        return out_marks

    def project_T(w, mw, j, HT, t0, t1, M=P, out_p=0, bank=None, wcols=None):
        b = ps.take()
        pe.after(*mw)
        for c in range(8):
            last = mm(b.ap[:, 0:t1 - t0], w[:, c, j * P:(j + 1) * P], HT[:, c, t0:t1], c == 0, c == 7)
        return b, pe.done(last)

    def project(w, mw, HT, c, width=512, K=8):
        b = ps.take()
        pe.after(*mw)
        for k in range(K):
            last = mm(b.ap[:, 0:width], HT[:, k, c * P:(c + 1) * P], w[:, k, 0:width], k == 0, k == K - 1)
        return b, pe.done(last)

    def cutter_for(keys):
        bufs = [[a.rearrange("p (c t) -> p c t", c=2) for a in take_parts(1024)] for _ in range(2)]
        return Cutter([(key, q) for key in keys for q in range(4)], bufs, ring.take, ring.free)

    def of_chunk(parts, c):
        return tuple((lambda k, a=a: a[:, k, c * P:(c + 1) * P]) for a in parts)

    def project_all(cutter, parts, chunks, marks=None):
        bs = [ps.take() for _ in chunks]
        for q in range(4):
            m = cutter.product([b.ap for b in bs], [of_chunk(parts, c) for c in chunks], q == 0, q == 3,
                               marks[q] if marks else None)
        return bs, m

    def project_all_T(cutter, parts, marks=None):
        bs = [ps.take() for _ in range(4)]
        for q in range(4):
            m = cutter.product_T([b.ap for b in bs], parts, marks[q] if marks else None)
        return bs, m

    def square(c, mark):
        act.done(act.after(mark).activation(SQ[:, :], X[:, c, :], ACT.Square, accum_out=XS[:, c:c + 1]))

    def add_branch(keys, YT, chunks, gate_row, marks, tmp):
        gates = {}
        for r in sorted({c // 2 for c in chunks}):
            g, mg = spread(gate_row + r)
            dst = tmp[r]
            m = dve.done(dve.after(mg).tensor_copy(dst, g.ap))
            g.free(m)
            gates[r] = m
        for h, key in enumerate(keys):
            w, mw, k = ring.take(key)
            for c in chunks:
                b, m = project(w, [mw] + marks, YT, c)
                last = m
                sl = slice(h * 512, h * 512 + 512)
                m = dve.done(dve.after(m, gates[c // 2]).tensor_tensor(tmp[2], b.ap, tmp[c // 2][:, sl], ALU.mult))
                b.free(m)
                m = dve.done(dve.after(m).tensor_tensor(X[:, c, sl], X[:, c, sl], tmp[2], ALU.add))
                if h == 1:
                    square(c, m)
            ring.free(k, last)

    def rope(dst, raw, marks):
        b = ps.take()
        pe.after(*marks)
        m = pe.done(mm(b.ap[:, 0:256], KC[:, C_ROT:C_ROT + P], raw, True, True))
        t = rtmp
        m = dve.done(dve.after(m).tensor_tensor(t, b.ap[:, 0:256], KC[:, C_SIN:C_SIN + 256], ALU.mult))
        b.free(m)
        m = dve.done(dve.after(m).tensor_tensor(dst, raw, KC[:, C_COS:C_COS + 256], ALU.mult))
        return dve.done(dve.after(m).tensor_tensor(dst, dst, t, ALU.add))

    later = []

    def turn_later(n=0):
        while len(later) > n:
            a, m = later.pop(0)
            rope(a, a, [m])

    def broadcast_load(dst, src, n):
        return w_s.sent(nc.gpsimd.dma_start(dst, src.rearrange("(a b) -> a b", a=1).to_broadcast([P, n])))

    def routed(layer, chunks, BL):
        nover = 7
        smat[0] = 0
        marks = fence()
        lay_out()
        if layer:
            arena["words"] -= 3 * SLOT
            top = arena["words"]
            ring.widen([arena["f"][:, top + i * SLOT:top + (i + 1) * SLOT] for i in range(3)], [], *marks)
        nch = len(chunks)
        nb = 16 + nover
        rs, rb, rw = XS, small(16), small(8 * 16)
        w_r = w_s.sent(nc.gpsimd.dma_start(rw.rearrange("p (c e) -> p c e", c=8),
                                           I["router_w"].rearrange("(c p) e -> p c e", p=P)))
        w_r = broadcast_load(rb, I["router_b"], 16)
        H = take(4 * D).rearrange("p (c d) -> p c d", c=4)
        HT = take(8 * 512).rearrange("p (c t) -> p c t", c=8)
        junk = take(D)
        marks = modulated(H, chunks, 6, 8, None, rs)
        tm = turn_all(HT, H, chunks, marks)
        N = nch * 16
        b = ps.take()
        pe.after(w_r, *tm)
        for i, c in enumerate(chunks):
            for k in range(8):
                last = mm(b.ap[:, i * 16:i * 16 + 16], HT[:, k, c * P:(c + 1) * P],
                          rw.rearrange("p (c e) -> p c e", c=8)[:, k, :], k == 0, k == 7)
        m = pe.done(last)
        aff, sel, o1, o2, t1, t2 = (small(N) for _ in range(6))
        m = act.done(act.after(m).activation(aff, b.ap[:, 0:N], ACT.Sigmoid))
        b.free(m)
        v3 = lambda a: a.rearrange("p (c e) -> p c e", e=16)
        g4 = lambda a: a.rearrange("p (g e) -> p g e", e=4)
        D_ = lambda ins: dve.done(ins)
        dve.after(m, w_r)
        D_(dve.after().tensor_tensor(v3(sel), v3(aff), rb.unsqueeze(1).to_broadcast([P, nch, 16]), ALU.add))
        G = nch * 4
        hi, lo, mid, gs, gt = small(2 * G), small(2 * G), small(G), small(G), small(G)
        s4 = g4(sel)
        h2, l2 = hi.rearrange("p (g e) -> p g e", e=2), lo.rearrange("p (g e) -> p g e", e=2)
        D_(dve.after().tensor_tensor(h2, s4[:, :, 0:2], s4[:, :, 2:4], ALU.max))
        D_(dve.after().tensor_tensor(l2, s4[:, :, 0:2], s4[:, :, 2:4], ALU.min))
        D_(dve.after().tensor_tensor(gs, h2[:, :, 0], h2[:, :, 1], ALU.max))
        D_(dve.after().tensor_tensor(mid, h2[:, :, 0], h2[:, :, 1], ALU.min))
        D_(dve.after().tensor_tensor(gt, l2[:, :, 0], l2[:, :, 1], ALU.max))
        D_(dve.after().tensor_tensor(mid, mid, gt, ALU.max))
        D_(dve.after().tensor_tensor(gs, gs, mid, ALU.add))
        red = small(nch)
        c4 = lambda a: a.rearrange("p (c g) -> p c g", g=4)

        def first_of_max(dst, val, weights, view, k):
            D_(dve.after().tensor_reduce(red, view(val), AX.X, ALU.max))
            D_(dve.after().tensor_tensor(view(dst), view(val), red.unsqueeze(2).to_broadcast([P, nch, k]), ALU.is_equal))
            D_(dve.after().tensor_tensor(view(dst), view(dst), weights.unsqueeze(1).to_broadcast([P, nch, k]), ALU.mult))
            D_(dve.after().tensor_reduce(red, view(dst), AX.X, ALU.max))
            return D_(dve.after().tensor_tensor(view(dst), view(dst), red.unsqueeze(2).to_broadcast([P, nch, k]), ALU.is_equal))

        first_of_max(gt, gs, KC[:, C_GW:C_GW + 4], c4, 4)
        D_(dve.after().tensor_scalar(gt, gt, 1.0, 2 * BIG, ALU.subtract, ALU.mult))
        D_(dve.after().tensor_tensor(g4(t1), g4(sel), gt.unsqueeze(2).to_broadcast([P, G, 4]), ALU.add))
        ew = small(16)
        D_(dve.after().tensor_scalar(ew, KC[:, C_EX:C_EX + 16], -1.0, 16.0, ALU.mult, ALU.add))
        first_of_max(o1, t1, ew, v3, 16)
        D_(dve.after().scalar_tensor_tensor(out=t1, in0=o1, scalar=-4 * BIG, in1=t1, op0=ALU.mult, op1=ALU.add))
        first_of_max(o2, t1, ew, v3, 16)
        wk = [small(nch), small(nch)]
        den = small(nch)
        for k, o in enumerate((o1, o2)):
            D_(dve.after().tensor_tensor(t2, o, aff, ALU.mult))
            D_(dve.after().tensor_reduce(wk[k], v3(t2), AX.X, ALU.add))
        D_(dve.after().tensor_tensor(den, wk[0], wk[1], ALU.add))
        D_(dve.after().reciprocal(den, den))
        for k in range(2):
            D_(dve.after().tensor_tensor(wk[k], wk[k], den, ALU.mult))
        M = small(N)
        m = D_(dve.after().tensor_tensor(M, o1, o2, ALU.add))
        b = ps.take()
        pe.after(m)
        for i in range(nch):
            for j in range(i):
                mm(b.ap[:, i * 16:i * 16 + 16], ones[:, :], M[:, j * 16:j * 16 + 16], j == 0, False)
            mm(b.ap[:, i * 16:i * 16 + 16], KC[:, C_LT:C_LT + P], M[:, i * 16:i * 16 + 16], i == 0, True)
        for j in range(nch):
            last = mm(b.ap[:, 64:80], ones[:, :], M[:, j * 16:j * 16 + 16], j == 0, j == nch - 1)
        m = pe.done(last)
        pos, blk, tt, cnt, inc, exc = small(N), small(N), small(N), small(16), small(16), small(16)
        D_(dve.after(m).tensor_copy(pos, b.ap[:, 0:N]))
        m = D_(dve.after().tensor_copy(cnt, b.ap[:, 64:80]))
        b.free(m)
        D_(dve.after().tensor_scalar(exc, cnt, float(BL), None, ALU.is_gt))
        for q in (2.0 * BL, 3.0 * BL):
            D_(dve.after().scalar_tensor_tensor(out=exc, in0=cnt, scalar=q, in1=exc, op0=ALU.is_gt, op1=ALU.add))
        D_(dve.after().tensor_tensor_scan(inc, ones[:, 0:16], exc, 0.0, ALU.mult, ALU.add))
        D_(dve.after().tensor_tensor(exc, inc, exc, ALU.subtract))
        D_(dve.after().tensor_scalar(blk, pos, float(BL), None, ALU.is_ge))
        for q in (2.0 * BL, 3.0 * BL):
            D_(dve.after().scalar_tensor_tensor(out=blk, in0=pos, scalar=q, in1=blk, op0=ALU.is_ge, op1=ALU.add))
        e3 = KC[:, C_EX:C_EX + 16].unsqueeze(1).to_broadcast([P, nch, 16])
        D_(dve.after().tensor_tensor(v3(tt), v3(blk), e3, ALU.subtract))
        D_(dve.after().tensor_tensor(v3(t1), v3(tt), exc.unsqueeze(1).to_broadcast([P, nch, 16]), ALU.add))
        D_(dve.after().tensor_scalar(t1, t1, 15.0, None, ALU.add))
        D_(dve.after().tensor_scalar(t2, blk, 0.0, None, ALU.is_gt))
        D_(dve.after().tensor_tensor(t1, t1, t2, ALU.mult))
        D_(dve.after().tensor_tensor(t1, t1, tt, ALU.subtract))
        D_(dve.after().scalar_tensor_tensor(out=t1, in0=t1, scalar=float(BL), in1=pos, op0=ALU.mult, op1=ALU.add))
        rowf = small(2 * nch)
        for k, o in enumerate((o1, o2)):
            D_(dve.after().tensor_tensor(t2, o, t1, ALU.mult))
            D_(dve.after().tensor_reduce(rowf[:, k * nch:(k + 1) * nch], v3(t2), AX.X, ALU.add))
        m_dst = D_(dve.after().tensor_copy(DST[:, 0:2 * nch], rowf))
        oe = small(16)
        for j in range(nover):
            D_(dve.after().tensor_scalar(t2[:, 0:16], inc, float(j), None, ALU.is_le))
            D_(dve.after().tensor_reduce(oe[:, j:j + 1], t2[:, 0:16], AX.X, ALU.add))
        D_(dve.after().tensor_scalar(oe[:, 0:nover], oe[:, 0:nover], 15.0, None, ALU.min))
        D_(dve.after().tensor_copy(OE[0:1, 0:nover], oe[0:1, 0:nover]))
        m_oe = D_(dve.after().tensor_copy(OE[0:1, 8:9], inc[0:1, 15:16]))
        pool.after(m_dst, m_z, *[marks[c] for c in chunks])
        for i, c in enumerate(chunks):
            for k in range(2):
                msc = w_sc.sent(nc.gpsimd.indirect_dma_start(
                    out=XP[:, :], out_offset=bass.IndirectOffsetOnAxis(ap=DST[:, k * nch + i:k * nch + i + 1], axis=0),
                    in_=H[:, c, :], in_offset=None))
        fence(msc)
        nb = 16
        by8 = lambda a: a.rearrange("p (c t) -> p c t", c=8)
        if BL == P:
            lay_out(8 * 1024 + 8 * 1024)
            xeT = [[by8(a) for a in take_parts(8 * BL)] for _ in range(2)]
            hidT = [[by8(a) for a in take_parts(8 * BL)] for _ in range(2)]
            bufs = [[a.rearrange("p (c t) -> p c t", c=2) for a in take_parts(1024)] for _ in range(4)]
        else:
            at[0] = 0
            xeT = [by8(take(8 * BL)) for _ in range(2)]
            hidT = [by8(take(8 * BL)) for _ in range(2)]
        xe = [take(D) for _ in range(2)]
        hid = [take(8 * BL) for _ in range(2)]
        yo = [take(8 * BL)] * 2 if BL == P else [take(8 * BL) for _ in range(2)]
        m_in, m_st, free_xe, free_xeT, free_hid, xeT_ready = {}, {}, {}, {}, {}, {}

        def fetch(n):
            if n < nb:
                pool.after(*free_xe.get(n - 2, ()))
                m_in[n] = w_xe[n % 2].sent(nc.gpsimd.dma_start(xe[n % 2][0:BL, :], XP[n * BL:(n + 1) * BL, :]))

        def turn_in(n, ahead=True):
            if n >= nb and ahead:
                return
            last_marks.clear()
            pe.after(m_in[n], *free_xeT.get(n - 2, ()))
            k = 512 // BL
            for j in range(0, 8, k):
                b = ps.take()
                for i in range(j, j + k):
                    last = nc.tensor.transpose(b.ap[:, (i - j) * BL:(i - j + 1) * BL], xe[n % 2][0:BL, i * P:(i + 1) * P],
                                               ident[0:BL, 0:BL])
                m = pe.done(last)
                src = b.ap.rearrange("p (a b) -> p a b", a=k)
                if BL == P:
                    m = halve(xeT[n % 2][0][:, j:j + k, :], xeT[n % 2][1][:, j:j + k, :], src, m)
                else:
                    m = evac(xeT[n % 2][:, j:j + k, :], src, m)
                b.free(m)
                last_marks.append(m)
            xeT_ready[n] = list(last_marks)
            free_xe[n] = (pe.mark(),)
            if ahead:
                fetch(n + 2)

        def pair(piece, n, mt, T, marks):
            (w0, m0, k0), (w1, m1, k1) = piece(n, mt, 0), piece(n, mt, 1)
            b = ps.take()
            pe.after(m0, m1, *marks)
            for c in range(8):
                for h, w in ((0, w0), (1, w1)):
                    last = mm(b.ap[64 * h:64 * h + 64, :], T(c, h), w[:, c, :], c == 0, c == 7)
            m = pe.done(last)
            return b, m, (k0, k1)

        def narrow(n, piece, spent, turn_next, store):
            i = n % 2
            b, m, ks = pair(piece, n, "g", lambda c, h: xeT[i][:, c, :], xeT_ready[n])
            spent(ks, m)
            m_g = act.done(act.after(m, *free_hid.get(n - 2, ())).activation(hid[i], b.ap, ACT.Silu))
            b.free(m_g)
            b, m, ks = pair(piece, n, "u", lambda c, h: xeT[i][:, c, :], ())
            spent(ks, m)
            free_xeT[n] = (m,)
            m = dve.done(dve.after(m, m_g).tensor_tensor(hid[i], hid[i], b.ap, ALU.mult))
            b.free(m)
            turn_next(n + 1)
            b = ps.take()
            pe.after(m)
            for j in range(4):
                last = nc.tensor.transpose(b.ap[:, j * P:(j + 1) * P], hid[i][:, j * P:(j + 1) * P], ident)
            m = pe.done(last)
            free_hid[n] = (m,)
            m = evac(hidT[i].rearrange("p (h j) t -> p j h t", h=2), b.ap.rearrange("p (j h t) -> p j h t", j=4, h=2), m)
            b.free(m)
            b, m, ks = pair(piece, n, "d", lambda c, h: hidT[i][:, c, :], (m,))
            spent(ks, m)
            m = evac(yo[i], b.ap, m, m_st.get(n - 2))
            b.free(m)
            m_st[n] = store(n, m, [(YP[n * BL:(n + 1) * BL, 512 * h:512 * h + 512], yo[i][64 * h:64 * h + 64, :]) for h in range(2)])

        def wide_units(n):
            g = [((n, mt, h), q) for mt, h in WIDE[:4] for q in range(4)]
            return g + [((n, "d", h), q) for q2 in (0, 2) for h in range(2) for q in (q2, q2 + 1)]

        def wide(n, cutter, turn_next, store):
            i = n % 2
            x_ = [(lambda c: xeT[i][0][:, c, :], lambda c: xeT[i][1][:, c, :])]
            t_ = [(lambda c: hidT[i][0][:, c, :], lambda c: hidT[i][1][:, c, :])]

            def turn(h, m):
                b = ps.take()
                pe.after(m)
                for j in range(4):
                    last = nc.tensor.transpose(b.ap[:, j * P:(j + 1) * P], hid[i][:, h * 512 + j * P:h * 512 + (j + 1) * P], ident)
                m = pe.done(last)
                m = halve(hidT[i][0][:, 4 * h:4 * h + 4, :], hidT[i][1][:, 4 * h:4 * h + 4, :],
                        b.ap.rearrange("p (a b) -> p a b", a=4), m)
                b.free(m)
                return m

            m_h, m_t = [], []
            for h in range(2):
                sl = slice(h * 512, h * 512 + 512)
                b = ps.take()
                for q in range(4):
                    m = cutter.product([b.ap], x_, q == 0, q == 3, *xeT_ready[n])
                m = act.done(act.after(m, *free_hid.get(n - 2, ())).activation(hid[i][:, sl], b.ap, ACT.Silu))
                b.free(m)
                if h:
                    m_t.append(turn(0, m_h[0]))
                b = ps.take()
                for q in range(4):
                    m2 = cutter.product([b.ap], x_, q == 0, q == 3)
                m = dve.done(dve.after(m, m2).tensor_tensor(hid[i][:, sl], hid[i][:, sl], b.ap, ALU.mult))
                b.free(m)
                m_h.append(m)
            free_xeT[n] = (pe.mark(),)
            turn_next(n + 1)
            bs = [ps.take(), ps.take()]
            for half in range(2):
                if half:
                    m_t.append(turn(1, m_h[1]))
                for h in range(2):
                    for q in range(2):
                        m = cutter.product([bs[h].ap], t_, half + q == 0, half + q == 2, m_t[-1])
                    if half:
                        bs[h] = (bs[h], m)
            free_hid[n] = (pe.mark(),)
            ms = []
            for h in range(2):
                b, m = bs[h]
                m = evac(yo[i][:, h * 512:h * 512 + 512], b.ap, m, m_st.get(n - 1))
                b.free(m)
                ms.append(m)
            m_st[n] = store(n, ms, [(YP[n * BL:(n + 1) * BL, :], yo[i])])

        def flat(m):
            return m if isinstance(m, list) else [m]

        def store(n, m, pairs):
            act.after(*flat(m))
            for dst, src in pairs:
                m = w_y[n % 2].sent(nc.scalar.dma_start(dst, src))
            return m

        fetch(0)
        fetch(1)
        turn_in(0)
        if BL == P:
            cutter = Cutter([u for n in range(nb) for u in wide_units(n)], bufs,
                            lambda key: ring.take((layer,) + key), ring.free)
        for n in range(nb):
            if BL == P:
                wide(n, cutter, turn_in, store)
            else:
                narrow(n, lambda n, mt, h: ring.take((layer, n, mt, h)), lambda ks, m: [ring.free(k, m) for k in ks],
                       turn_in, store)
        gates = {r: spread(10 + r) for r in sorted({c // 2 for c in chunks})}
        fence(m_st[nb - 1], m_st[nb - 2], m_oe)
        sp.after(pe.mark(), m_oe)
        many = nc.values_load(OE[0:1, 8:9], min_val=0, max_val=nover)
        order = WIDE if BL == P else PAIRS

        def further(n):
            expert = nc.sync.value_load(OE[0:1, n - 16:n - 15], min_val=0, max_val=15)
            marks = fence()
            sp.after(*marks)
            m_in[n] = w_vx.sent(nc.sync.dma_start(xe[n % 2][0:BL, :], XP[n * BL:(n + 1) * BL, :]))
            sent = {}

            def load(k, *marks):
                mt, h = order[k]
                v = moe[mt][layer].rearrange("e (c p) n -> p e c n", p=P)
                sp.after(*marks)
                sent[k] = w_v[k % NS].sent(nc.sync.dma_start(
                    ring.ap[:, k % NS, :].rearrange("p (e c n) -> p e c n", e=1, c=8),
                    v[:, bass.ds(expert, 1), :, 512 * h:512 * h + 512]))

            for k in range(NS):
                load(k)

            def piece(n, mt, h):
                k = order.index((mt, h))
                return ring.ap[:, k % NS, :].rearrange("p (c n) -> p c n", c=8), sent[k], k

            def spent(ks, m):
                for k in ks:
                    if k + NS < 6:
                        load(k + NS, m)

            def put(n, m, pairs):
                act.after(*flat(m))
                for dst, src in pairs:
                    m = w_vy.sent(nc.scalar.dma_start(dst, src))
                return m

            for d_ in (free_xe, free_xeT, free_hid, m_st, xeT_ready):
                d_.clear()
            turn_in(n, False)
            if BL == P:
                wide(n, Cutter(wide_units(n), bufs, lambda key: piece(*key), lambda k, m: spent((k,), m)),
                     lambda n: None, put)
            else:
                narrow(n, piece, spent, lambda n: None, put)
            marks = fence(m_st[n])
            sp.after(*marks)

        for n in range(16, 16 + nover):
            counts = [(x, x.n, dict(x.met)) for x in (pe, dve, act, pool, sp)]
            wires = [(x, x.n) for x in w_v + [w_vx, w_vy]]
            with nc.If(many > n - 16):
                further(n)
            with nc.Else():
                for x, was, _ in counts:
                    if x.n > was:
                        x.eng.sem_inc(x.sem, x.n - was)
                for x, was in wires:
                    if x.n > was:
                        (nc.scalar if x is w_vy else nc.sync).sem_inc(x.sem, x.n - was)
            for x, _, met in counts:
                x.met = met
        marks = fence()
        sp.after(*marks)
        lay_out()
        R = [take(D) for _ in range(2 * nch)]
        mg = []
        pool.after(mod_kept)
        m_mod = w_s.sent(nc.gpsimd.dma_start(MOD[:, :], (M1, M2)[layer][:, :]))
        fg = take(D)
        if layer:
            m_mod = broadcast_load(fg, I["final_norm_g"], D)
        for i, c in enumerate(chunks):
            for k in range(2):
                m = w_g[i].sent(nc.gpsimd.indirect_dma_start(
                    out=R[2 * i + k], out_offset=None, in_=YP[:, :],
                    in_offset=bass.IndirectOffsetOnAxis(ap=DST[:, k * nch + i:k * nch + i + 1], axis=0)))
            mg.append(m)
        sp.after(mg[0] if layer else mg[-1])
        ring.resume()
        scaled = [act.done(act.apart(mg[i]).mul(R[2 * i + 1], R[2 * i + 1], wk[1][:, i:i + 1])) for i in range(nch)]
        for r, (g, m_g) in gates.items():
            for i, c in enumerate(chunks):
                if c // 2 != r:
                    continue
                a, b2 = R[2 * i], R[2 * i + 1]
                m = dve.done(dve.after(scaled[i], m_g).scalar_tensor_tensor(
                    out=a, in0=a, scalar=wk[0][:, i:i + 1], in1=b2, op0=ALU.mult, op1=ALU.add))
                m = dve.done(dve.after(m).tensor_tensor(a, a, g.ap, ALU.mult))
                m = dve.done(dve.after(m).tensor_tensor(X[:, c, :], X[:, c, :], a, ALU.add))
                square(c, m)
            g.free(m)
        return m_mod, fg

    for _ in modulation("ada0", 0, I["ada_b"][0], [(2, I["norm_mix_g"][0]), (8, I["norm_ffn_g"][0])],
                        AR[:, 0:1536], None, range(2)):
        pass
    fence()
    at[0] = 0
    allc = [0, 1, 2, 3]
    H = take(4 * D).rearrange("p (c d) -> p c d", c=4)
    HT = take(8 * 512).rearrange("p (c t) -> p c t", c=8)
    smat[0] = 0
    rs = small(8)
    marks = modulated(H, allc, 0, 2, SQ[:, :], rs)
    tm = turn_all(HT, H, allc, marks)
    fence(*tm)
    m_hd = w_h.sent(nc.scalar.dma_start(HD, HT.rearrange("p c t -> p (c t)")))

    def split_turned(HT, keys, *marks):
        parts = [a.rearrange("p (c t) -> p c t", c=8) for a in take_parts(8 * 512)]
        ms = []
        for q in range(4):
            sl = slice(2 * q, 2 * q + 2)
            ms.append(halve(parts[0][:, sl, :], parts[1][:, sl, :], HT[:, sl, :], *marks))
            if q == 0:
                cutter = cutter_for(keys)
        return parts, ms, cutter

    HP, m_hp, cutter = split_turned(HT, [("in", n) for n in range(4)])
    at[0] = 0
    fm = lambda a: a.rearrange("p (c h t) -> p c h t", c=4, h=4)
    Q, FF, FB = (fm(take(2048)) for _ in range(3))
    V = take(2048).rearrange("p (c n) -> p c n", c=4)
    lv = take(14 * 128)
    lbr = small(128)
    m_lv = w_s.sent(nc.gpsimd.dma_start(lv, I["consts"][:, C_LEV:C_LEV + 14 * P]))
    m_lv = w_s.sent(nc.gpsimd.dma_start(lbr[0:24, :], I["hgrn_lb_logits"].rearrange("a d (h k) -> (a d h) k", k=P)))
    on = small(128)
    m_lv = broadcast_load(on, I["hgrn_onorm_g"][0], P)
    for n in range(3):
        bs, m = project_all_T(cutter, HP, m_hp)
        for h, b in enumerate(bs):
            dst = (Q, FF, FB)[n][:, :, h, :]
            src = b.ap.rearrange("p (c t) -> p c t", c=4)
            m2 = act.done(act.apart(m, m_hp[-1], m_hd if n == 2 else None).activation(dst, src, ACT.Silu if n == 0 else ACT.Sigmoid))
            b.free(m2)
        if n == 0:
            b = ps.take()
            pe.after(m_lv)
            m = pe.done(nc.tensor.transpose(b.ap[:, 0:24], lbr[0:24, :], ident[0:24, 0:24]))
            lg, lb, oml, t8 = small(24), small(8), small(8), small(8)
            m = dve.done(dve.after(m).tensor_copy(lg, b.ap[:, 0:24]))
            b.free(m)
            dve.done(dve.after().tensor_tensor(t8, lg[:, 0:8], lg[:, 8:16], ALU.max))
            dve.done(dve.after().tensor_tensor(t8, t8, lg[:, 16:24], ALU.max))
            l3 = lg.rearrange("p (a b) -> p a b", a=3)
            m = dve.done(dve.after().tensor_tensor(l3, l3, t8.unsqueeze(1).to_broadcast([P, 3, 8]), ALU.subtract))
            m = act.done(act.after(m).activation(lg, lg, ACT.Exp))
            dve.done(dve.after(m).tensor_tensor(t8, lg[:, 0:8], lg[:, 8:16], ALU.add))
            dve.done(dve.after().tensor_tensor(t8, t8, lg[:, 16:24], ALU.add))
            dve.done(dve.after().reciprocal(t8, t8))
            dve.done(dve.after().tensor_tensor(lb, lg[:, 0:8], t8, ALU.mult))
            m_lb = dve.done(dve.after().tensor_scalar(oml, lb, -1.0, 1.0, ALU.mult, ALU.add))
            m_q = dve.done(dve.after(m2).tensor_scalar(Q[:, :, :, :], Q[:, :, :, :], 128 ** -0.5, None, ALU.mult))
    bs, m = project_all(cutter, HP, allc)
    for c, b in enumerate(bs):
        m2 = dve.done(dve.after(m, m_hd).tensor_copy(V[:, c, :], b.ap))
        b.free(m2)
    fence(m_lb)
    lay_out(0, KEEP)
    at[0] = KEEP
    O = take(2048).rearrange("p (c n) -> p c n", c=4)
    place = take(1536)
    early = [take(512) for _ in range(8)]
    rest = [take(512) for _ in range(8)]
    temps = [early, rest]
    h4 = lambda a: a.rearrange("p (h t) -> p h t", h=4)
    ets = [small(4), small(4)]

    def direction(d):
        kt_, cum, ee, kk, qq, A_, tA, Sf = temps[d]
        S, et = h4(Sf), ets[d]
        lf = tA
        order = (2, 3, 0, 1) if d == 0 else (3, 2, 1, 0)
        FX = (FF, FB)[d]
        end = 127 if d == 0 else 0
        m_pe = None
        for step, c in enumerate(order):
            Qf = Q[:, c, :, :].rearrange("p h t -> p (h t)")
            for h in range(4):
                m = dve.done(dve.apart().tensor_scalar(FX[:, c, h, :], FX[:, c, h, :], oml[:, 4 * d + h:4 * d + h + 1],
                                                       lb[:, 4 * d + h:4 * d + h + 1], ALU.mult, ALU.add))
            m_lf = act.done(act.after(m, m_pe).activation(h4(lf), FX[:, c, :, :], ACT.Ln))
            m_k = dve.done(dve.after(m_pe).tensor_scalar(h4(kt_), FX[:, c, :, :], -1.0, 1.0, ALU.mult, ALU.add))
            yield
            for h in range(4):
                i_, o_ = h4(lf)[:, h, :], h4(cum)[:, h, :]
                if d == 1:
                    i_, o_ = i_[:, ::-1], o_[:, ::-1]
                m_cum = m = dve.done(dve.apart(m_lf, m_k).tensor_tensor_scan(o_, ones[:, :], i_, 0.0, ALU.mult, ALU.add))
            m_et = act.done(act.after(m).activation(et, h4(cum)[:, :, end], ACT.Exp))
            qs, ks = (1, 0) if d == 0 else (0, 1)
            es, ws = [ee, FX[:, c, :, :].rearrange("p h t -> p (h t)")], [qq, kk]
            m_e, m_s, m_b, m_w = {}, {}, {}, {}
            free_w = [m_pe, m_pe]

            def exps(l):
                if l == 7:
                    return
                hb = 64 >> l
                e = es[l % 2]
                cv, ev = (a.rearrange("p (n s b) -> p n s b", s=2, b=hb) for a in (cum, e))
                r_ = cv[:, :, ks, hb - 1 if d == 0 else 0].unsqueeze(2).to_broadcast([P, 256 // hb, 2 * hb])
                n2 = lambda a: a.rearrange("p (n b) -> p n b", b=2 * hb)
                m = dve.done(dve.apart(m_cum, m_w.get(l - 2)).tensor_tensor(n2(e), n2(cum), r_, ALU.subtract))
                for s, sign in ((qs, 1.0), (ks, -1.0)):
                    m_e[l] = act.done(act.apart(m).activation(ev[:, :, s, :], ev[:, :, s, :], ACT.Exp, scale=sign))

            def scores(l):
                b = ps.take()
                if l < 7:
                    hb = 64 >> l
                    v = lambda a: a.rearrange("p (n s b) -> p n s b", s=2, b=hb)
                    e, w = es[l % 2], ws[l % 2]
                    dve.apart(m_e[l], free_w[l % 2], m_k)
                    for s, of in ((qs, Qf), (ks, kt_)):
                        m_w[l] = m = dve.done(dve.eng.tensor_tensor(v(w)[:, :, s, :], v(of)[:, :, s, :], v(e)[:, :, s, :], ALU.mult))
                    pe.after(m)
                    kl, ql = w, w
                else:
                    pe.after(m_k)
                    kl, ql = kt_, Qf
                for h in range(4):
                    last = mm(b.ap[:, h * P:(h + 1) * P], h4(kl)[:, h, :], h4(ql)[:, h, :], True, True)
                free_w[l % 2] = m_s[l] = pe.done(last)
                m_b[l] = b

            def gather(l):
                b = m_b[l]
                mask = lv[:, (7 * d + l) * P:(7 * d + l + 1) * P] if l < 7 else ident
                mask4 = mask.unsqueeze(1).to_broadcast([P, 4, P])
                if l == 0:
                    m = dve.done(dve.after(m_s[l], m_lv).tensor_tensor(h4(A_), h4(b.ap), mask4, ALU.mult))
                else:
                    m = dve.done(dve.apart(m_s[l], m_s[l - 1]).copy_predicated(h4(A_), mask4.bitcast(U32), h4(b.ap)))
                b.free(m)
                m_s[l] = m

            for i in range(10):
                for k, stage in enumerate((exps, scores, gather)):
                    if 0 <= i - k < 8:
                        stage(i - k)
                yield
            m = m_s[7]
            m_pe = free_w[1]
            m1 = None
            m_A = m
            if step:
                m1 = act.done(act.after(m_A).activation(ee, cum, ACT.Exp))
                m1 = dve.done(dve.after(m1, m_pe).tensor_tensor(qq, Qf, ee, ALU.mult))
            b = ps.take()
            pe.after(m_A, m1)
            for h in range(4):
                last = mm(b.ap[:, h * P:(h + 1) * P], h4(A_)[:, h, :], V[:, c, h * P:(h + 1) * P], True, step == 0)
                if step:
                    last = mm(b.ap[:, h * P:(h + 1) * P], h4(qq)[:, h, :], S[:, h, :], False, True)
            m_pe = pe.done(last)
            yield
            if step % 2 == 0:
                m = dve.done(dve.after(m_pe).tensor_copy(O[:, c, :], b.ap))
            else:
                m = dve.done(dve.after(m_pe).tensor_tensor(O[:, c, :], O[:, c, :], b.ap, ALU.add))
            b.free(m)
            if step == 3:
                return
            m = dve.done(dve.after().tensor_tensor(h4(ee), h4(cum)[:, :, end:end + 1].to_broadcast([P, 4, P]), h4(cum), ALU.subtract))
            m = act.done(act.after(m).activation(ee, ee, ACT.Exp))
            m = dve.done(dve.after(m).tensor_tensor(kk, kt_, ee, ALU.mult))
            b = ps.take()
            pe.after(m)
            for h in range(4):
                last = nc.tensor.transpose(b.ap[:, h * P:(h + 1) * P], h4(kk)[:, h, :], ident)
            m = pe.done(last)
            yield
            m = act.done(act.after(m).copy(tA, b.ap))
            b.free(m)
            b = ps.take()
            pe.after(m)
            for h in range(4):
                last = mm(b.ap[:, h * P:(h + 1) * P], h4(tA)[:, h, :], V[:, c, h * P:(h + 1) * P], True, True)
            m_pe = pe.done(last)
            yield
            if step == 0:
                m = dve.done(dve.after(m_pe).tensor_copy(S, h4(b.ap)))
            else:
                for h in range(4):
                    m = dve.done(dve.after(m_pe, m_et).scalar_tensor_tensor(
                        out=S[:, h, :], in0=S[:, h, :], scalar=et[:, h:h + 1], in1=b.ap[:, h * P:(h + 1) * P],
                        op0=ALU.mult, op1=ALU.add))
            b.free(m)

    def all_modulations():
        for args in (("ada0", 0, I["ada_b"][0], [(2, I["norm_mix_g"][0]), (8, I["norm_ffn_g"][0])], place, M0, range(2, 6)),
                     ("ada1", 0, I["ada_b"][1], [(2, I["norm_mix_g"][1]), (8, I["norm_ffn_g"][1])], place, M1, range(6)),
                     ("ada2", 1, I["b_mod_2"][0], [(2, I["norm_mix_pre_2"][0]), (4, I["norm_mix_post_2"][0]),
                                                   (8, I["norm_ffn_pre_2"][0]), (10, I["norm_ffn_post_2"][0])], place, M2, range(6))):
            yield from modulation(*args)

    in_turns(direction(0), direction(1), every(1, all_modulations()))
    mod_kept = (id(w_m.sem), w_m.sem, w_m.n)
    marks = fence()
    at[0] = 0
    G = take(2048).rearrange("p (c n) -> p c n", c=4)
    HT = take(8 * 512).rearrange("p (c t) -> p c t", c=8)
    m_ht = w_h.sent(nc.scalar.dma_start(HT.rearrange("p c t -> p (c t)"), HD))
    pool.after(mod_kept)
    m_mod = w_s.sent(nc.gpsimd.dma_start(MOD[4:12, :], M0[4:12, :]))
    ss = small(16)
    m_sq = []
    for c in allc:
        m_sq.append(dve.done(dve.apart(pe.mark()).tensor_tensor(rest[c], O[:, c, :], O[:, c, :], ALU.mult)))
    for c in allc:
        m = dve.done(dve.apart(m_sq[c]).tensor_reduce(ss[:, 4 * c:4 * c + 4], h4(rest[c]), AX.X, ALU.add))

    def finish_rstd(ss, n, width):
        m = dve.done(dve.after().tensor_scalar(ss[:, 0:n], ss[:, 0:n], 1.0 / width, EPS, ALU.mult, ALU.add))
        m = act.done(act.after(m).activation(ss[:, 0:n], ss[:, 0:n], ACT.Sqrt))
        return dve.done(dve.after(m).reciprocal(ss[:, 0:n], ss[:, 0:n]))

    m = finish_rstd(ss, 16, 128)
    for c in allc:
        for h in range(4):
            dve.done(dve.apart(m).scalar_tensor_tensor(
                out=G[:, c, h * P:(h + 1) * P], in0=O[:, c, h * P:(h + 1) * P], scalar=ss[:, 4 * c + h:4 * c + h + 1],
                in1=on, op0=ALU.mult, op1=ALU.mult))
    smat[0] = 0
    fence(m_ht, m_mod)
    lay_out(PARTS, KEEP)
    HP, m_hp, cutter = split_turned(HT, [("in", n) for n in range(4, 8)])
    hm = lambda a: a.rearrange("p (h t) -> p h t", h=4)
    at[0] = 2048
    QA, KA = hm(take(2048)), hm(take(2048))
    VA = take(2048).rearrange("p (c n) -> p c n", c=4)
    gs_ = [take(512) for _ in range(2)]
    rtmp = take(256)
    bs, m = project_all(cutter, HP, allc, m_hp)
    for c, b in enumerate(bs):
        m2 = act.done(act.after(m, dve.mark()).activation(gs_[c % 2], b.ap, ACT.Silu))
        b.free(m2)
        dve.done(dve.after(m2).tensor_tensor(G[:, c, :], G[:, c, :], gs_[c % 2], ALU.mult))
    lam4, sub = small(256), small(128)
    m_l = broadcast_load(lam4, I["diff_lambda"][0].rearrange("a b -> (a b)"), 256)
    m_l = broadcast_load(sub, I["diff_subln_g"][0], 128)
    zt = take(256)
    m_z = pool.done(pool.after().memset(zt, 0.0))
    pool.after(m_z)
    for dst, n in [(XP, n) for n in range(XROWS // P)] + [(YP, n) for n in range(16, XROWS // P)]:
        m_z = w_z.sent(nc.gpsimd.dma_start(dst[n * P:(n + 1) * P, :].rearrange("p (a b) -> p a b", a=4),
                                           zt.unsqueeze(1).to_broadcast([P, 4, 256])))
    lt, l2 = small(128), small(2)
    for j in range(2):
        dve.done(dve.after(m_l).tensor_tensor(lt[:, j * 64:j * 64 + 64], lam4[:, 128 * j:128 * j + 64],
                                              lam4[:, 128 * j + 64:128 * j + 128], ALU.mult))
    m = dve.done(dve.after().tensor_reduce(l2, lt.rearrange("p (a b) -> p a b", a=2), AX.X, ALU.add))
    m = act.done(act.after(m).activation(l2, l2, ACT.Exp))
    lam = small(1)
    dve.done(dve.after(m).tensor_tensor(lam, l2[:, 1:2], l2[:, 0:1], ALU.subtract))
    m = dve.done(dve.after(m).tensor_scalar(lam, lam, 0.8 - 0.6 * math.exp(-0.0), None, ALU.subtract))
    for n, dst in ((5, QA), (6, KA)):
        bs, last = project_all_T(cutter, HP)
        turn_later()
        for h, b in enumerate(bs):
            m = evac(dst[:, h, :], b.ap, last, m_hp[-1])
            later.append((dst[:, h, 0:256], m))
            b.free(m)
    bs, last = project_all(cutter, HP, allc)
    turn_later()
    for c, b in enumerate(bs):
        b.free(evac(VA[:, c, :], b.ap, last))
    fence(m_z)
    lay_out(0, KEEP)
    at[0] = KEEP
    YB = take(2048).rearrange("p (c n) -> p c n", c=4)
    P0, P1, aT = [take(512) for _ in range(4)], [take(512) for _ in range(4)], [take(512) for _ in range(2)]
    sts = [small(8) for _ in range(4)]
    units = [(qi, h) for qi in allc for h in range(4)]
    got, obs = {}, {}

    def scores0(u):
        qi, h = units[u]
        k0, k1 = (0, 512) if qi < 2 else (256, 512)
        nk = k1 - k0
        st = sts[u % 4]
        bs, ms = [ps.take(), ps.take()], []
        for mp, b in enumerate(bs):
            pr = slice(64 * mp, 64 * mp + 64)
            m = pe.done(mm(b.ap[:, 0:nk], QA[pr, h, qi * P:(qi + 1) * P], KA[pr, h, k0:k1], True, True))
            m = dve.done(dve.apart(m, got.get(("t", u - 4))).tensor_reduce(st[:, mp:mp + 1], b.ap[:, 0:nk], AX.X, ALU.max))
        m = dve.done(dve.apart(m).tensor_scalar(st[:, 0:2], st[:, 0:2], -0.125, None, ALU.mult))
        for mp, b in enumerate(bs):
            Pm = (P0, P1)[mp][u % 4]
            m2 = act.done(act.apart(m, got.get(("t", u - 4))).activation(
                Pm[:, 0:nk], b.ap[:, 0:nk], ACT.Exp, bias=st[:, mp:mp + 1], scale=0.125, accum_out=st[:, 2 + mp:3 + mp]))
            b.free(m2)
        got["e", u] = m2

    def weights0(u):
        qi, h = units[u]
        nk = 512 if qi < 2 else 256
        st = sts[u % 4]
        m = dve.done(dve.apart(got["e", u]).reciprocal(st[:, 4:6], st[:, 2:4]))
        a0, a1 = P0[u % 4][:, 0:nk], P1[u % 4][:, 0:nk]
        m = dve.done(dve.apart(m).tensor_scalar(a1, a1, st[:, 5:6], lam, ALU.mult, ALU.mult))
        got["a", u] = dve.done(dve.apart(m).scalar_tensor_tensor(out=a0, in0=a0, scalar=st[:, 4:5], in1=a1, op0=ALU.mult, op1=ALU.add))

    def turn0(u):
        qi, h = units[u]
        nk = 512 if qi < 2 else 256
        b = ps.take()
        pe.after(got["a", u])
        for j in range(nk // P):
            last = nc.tensor.transpose(b.ap[:, j * P:(j + 1) * P], P0[u % 4][:, j * P:(j + 1) * P], ident)
        got["t", u] = m = pe.done(last)
        got["c", u] = m = evac(aT[u % 2][:, 0:nk], b.ap[:, 0:nk], m, got.get(("v", u - 2)))
        b.free(m)

    def values0(u):
        qi, h = units[u]
        k0, nk = (0, 512) if qi < 2 else (256, 256)
        if h == 0:
            obs[qi] = ps.take()
        ob = obs[qi]
        pe.after(got["c", u])
        for j in range(nk // P):
            last = mm(ob.ap[:, h * P:(h + 1) * P], aT[u % 2][:, j * P:(j + 1) * P],
                      VA[:, k0 // P + j, h * P:(h + 1) * P], j == 0, j == nk // P - 1)
        got["v", u] = m = pe.done(last)
        if h == 3:
            m = dve.done(dve.after(m).tensor_copy(YB[:, qi, :], ob.ap))
            ob.free(m)

    def staggered(n, *stages):
        for i in range(n + len(stages) - 1):
            for k, stage in enumerate(stages):
                if 0 <= i - k < n:
                    stage(i - k)

    staggered(16, scores0, lambda u: None, weights0, turn0, values0)
    ss = small(16)
    for c in allc:
        m = dve.done(dve.after().tensor_tensor(P0[0], YB[:, c, :], YB[:, c, :], ALU.mult))
        m = dve.done(dve.after().tensor_reduce(ss[:, 4 * c:4 * c + 4], h4(P0[0]), AX.X, ALU.add))
    m = finish_rstd(ss, 16, 128)
    m = dve.done(dve.after().tensor_scalar(ss, ss, 1.0 - (0.8 - 0.6 * math.exp(-0.0)), None, ALU.mult))
    at[0] = 2048
    YC = take(2048).rearrange("p (c n) -> p c n", c=4)
    for c in allc:
        for h in range(4):
            m = dve.done(dve.after(m).scalar_tensor_tensor(
                out=YC[:, c, h * P:(h + 1) * P], in0=YB[:, c, h * P:(h + 1) * P], scalar=ss[:, 4 * c + h:4 * c + h + 1],
                in1=sub, op0=ALU.mult, op1=ALU.mult))
    fence()
    lay_out(PARTS, KEEP)
    YP_ = [a.rearrange("p (c t) -> p c t", c=8) for a in take_parts(8 * 512)]
    for c in allc:
        for j, src in ((0, G), (4, YC)):
            b = ps.take()
            for i in range(4):
                last = nc.tensor.transpose(b.ap[:, i * P:(i + 1) * P], src[:, c, i * P:(i + 1) * P], ident)
            m = pe.done(last)
            m = halve(*(a[:, j:j + 4, c * P:(c + 1) * P] for a in YP_), b.ap.rearrange("p (a b) -> p a b", a=4), m)
            b.free(m)
    cutter = cutter_for([("wo", 0), ("wo", 1)])
    at[0] = 4096
    tmp = [take(D), take(D), take(512), take(512)]
    for r in range(2):
        g, mg = spread(4 + r)
        g.free(dve.done(dve.after(mg).tensor_copy(tmp[r], g.ap)))
    for h in range(2):
        bs, last = project_all(cutter, YP_, allc, [m] * 4)
        sl = slice(h * 512, h * 512 + 512)
        for c, b in enumerate(bs):
            t = tmp[2 + c % 2]
            m2 = dve.done(dve.after(last).tensor_tensor(t, b.ap, tmp[c // 2][:, sl], ALU.mult))
            b.free(m2)
            m2 = dve.done(dve.after(m2).tensor_tensor(X[:, c, sl], X[:, c, sl], t, ALU.add))
            if h == 1:
                square(c, m2)
    m_mod, _ = routed(0, allc, P)

    fence(m_mod)
    at[0] = 0
    smat[0] = 0
    HT = take(8 * 512).rearrange("p (c t) -> p c t", c=8)
    base = at[0]
    H = take(4 * D).rearrange("p (c d) -> p c d", c=4)
    junk = take(D)
    rs = small(8)
    marks = modulated(H, allc, 0, 2, None, XS)
    tm = turn_all(HT, H, allc, marks)
    at[0] = base
    fence(*tm)
    QC = take(8 * 256).rearrange("p (c t) -> p c t", c=8)
    KK = take(4 * 512).rearrange("p (c t) -> p c t", c=4)
    VC = take(4 * 256).rearrange("p (c n) -> p c n", c=4)
    YC = take(2 * D).rearrange("p (c n) -> p c n", c=2)
    swa = take(1024).rearrange("p (q n) -> p q n", q=2)
    Sx, aT = [take(512) for _ in range(4)], [take(512) for _ in range(2)]
    rtmp = take(256)
    sink = small(16)
    w_sw = w_s.sent(nc.gpsimd.dma_start(swa, I["consts"][:, C_SWA:C_SWA + 1024].rearrange("p (q n) -> p q n", q=2)))
    w_sw = broadcast_load(sink, I["swa_sink"][0], 16)
    for n in range(2):
        w, mw, k = ring.take(("qkv", n))
        for j in range(4):
            b, m = project_T(w, [mw], j, HT, 0, 256)
            last = m
            m = evac(QC[:, 4 * n + j, :], b.ap[:, 0:256], m)
            b.free(m)
            later.append((QC[:, 4 * n + j, :], m))
            turn_later(1)
        ring.free(k, last)
    w, mw, k = ring.take(("qkv", 2))
    pe.after(mw)
    for j in range(4):
        b = ps.take()
        for half in range(2):
            for c in range(8):
                last = mm(b.ap[64 * half:64 * half + 64, :], w[:, c, 64 * j:64 * j + 64], HT[:, c, :], c == 0, c == 7)
        m = pe.done(last)
        m = evac(KK[:, j, :], b.ap, m)
        b.free(m)
        later.append((KK[:, j, 0:256], m))
        turn_later(1)
    for c in allc:
        b = ps.take()
        for k8 in range(8):
            last = mm(b.ap[:, 0:256], HT[:, k8, c * P:(c + 1) * P], w[:, k8, 256:512], k8 == 0, k8 == 7)
        m = pe.done(last)
        m2 = evac(VC[:, c, :], b.ap[:, 0:256], m)
        b.free(m2)
        turn_later()
    ring.free(k, m)
    fence()
    sts = [small(4) for _ in range(4)]
    rr = [small(16) for _ in range(2)]
    units = [(qi, h) for qi in range(2) for h in range(16)]
    got, obs = {}, {}

    def scores1(u):
        qi, h = units[u]
        pr = slice(64 * (h % 2), 64 * (h % 2) + 64)
        s, st = Sx[u % 4], sts[u % 4]
        b = ps.take()
        m = pe.done(mm(b.ap, QC[pr, h // 2, qi * P:(qi + 1) * P], KK[pr, h // 4, :], True, True))
        m = dve.done(dve.after(m, w_sw, got.get(("t", u - 4))).scalar_tensor_tensor(
            out=s, in0=b.ap, scalar=0.125, in1=swa[:, qi, :], op0=ALU.mult, op1=ALU.add))
        b.free(m)
        dve.done(dve.after().tensor_reduce(st[:, 0:1], s, AX.X, ALU.max))
        m = dve.done(dve.after().tensor_scalar(st[:, 0:1], st[:, 0:1], sink[:, h:h + 1], -1.0, ALU.max, ALU.mult))
        got["e", u] = act.done(act.after(m).activation(s, s, ACT.Exp, bias=st[:, 0:1], accum_out=st[:, 1:2]))
        got["s", u] = act.done(act.after(m).activation(st[:, 2:3], sink[:, h:h + 1], ACT.Exp, bias=st[:, 0:1]))

    def turn1(u):
        qi, h = units[u]
        st = sts[u % 4]
        dve.done(dve.after(got["s", u]).tensor_tensor(st[:, 1:2], st[:, 1:2], st[:, 2:3], ALU.add))
        dve.done(dve.after().reciprocal(rr[qi][:, h:h + 1], st[:, 1:2]))
        b = ps.take()
        pe.after(got["e", u])
        for j in range(4):
            last = nc.tensor.transpose(b.ap[:, j * P:(j + 1) * P], Sx[u % 4][:, j * P:(j + 1) * P], ident)
        got["t", u] = m = pe.done(last)
        got["c", u] = m = evac(aT[u % 2], b.ap, m, got.get(("v", u - 2)))
        b.free(m)

    def values1(u):
        qi, h = units[u]
        if h % 8 == 0:
            obs[u // 8] = ps.take()
        ob = obs[u // 8]
        pe.after(got["c", u])
        o8 = (h % 8) * 64
        for j in range(4):
            last = mm(ob.ap[:, o8:o8 + 64], aT[u % 2][:, j * P:(j + 1) * P], VC[:, j, 64 * (h // 4):64 * (h // 4) + 64],
                      j == 0, j == 3)
        got["v", u] = m = pe.done(last)
        if h % 8 == 7:
            h0 = h - 7
            m = dve.done(dve.after(m).tensor_tensor(
                YC[:, qi, h0 * 64:h0 * 64 + 512].rearrange("p (h d) -> p h d", h=8),
                ob.ap.rearrange("p (h d) -> p h d", h=8),
                rr[qi][:, h0:h0 + 8].unsqueeze(2).to_broadcast([P, 8, 64]), ALU.mult))
            ob.free(m)

    staggered(32, scores1, lambda u: None, turn1, values1)
    fence()
    xc = [0, 1]
    tm = turn_all(HT, YC, xc, {0: None, 1: None})
    at[0] = base
    fence(*tm)
    tmp = [take(D), take(D), take(512)]
    add_branch([("owo", 0), ("owo", 1)], HT, xc, 4, tm, tmp)
    mx = w_x2.sent(nc.gpsimd.dma_start(X[:, 2:4, :], I["ctx_2"][0].rearrange("(c p) d -> p c d", p=P)))
    sm_top[0] = smat[0] = 2304
    smat[0] -= 80 + 128 + 48 + 48 + 24
    fence()
    cw = small(80)
    cwr = small(128)
    w_cv = w_s.sent(nc.gpsimd.dma_start(cwr[0:60, :], I["conv_w_2"][0].rearrange("k (c p) -> (k c) p", p=P)))
    w_cv = w_s.sent(nc.gpsimd.dma_start(cwr[60:80, :], I["conv_b_2"][0].rearrange("(c p) -> c p", p=P)))
    dtb, alog, dsk = small(48), small(48), small(24)
    w_cv = broadcast_load(dtb, I["dt_bias_2"][0].rearrange("a b -> (a b)"), 48)
    w_cv = broadcast_load(alog, I["a_log_2"][0].rearrange("a b -> (a b)"), 48)
    w_cv = broadcast_load(dsk, I["d_skip_2"][0], 24)
    sm_top[0] -= 80 + 128 + 48 + 48 + 24
    smat[0] = 0
    m_mod, fg = routed(1, xc, 64)
    at[0] = 0
    smat[0] = 0
    m_f = m_mod
    rs = small(8)
    m = rstd_of([X[:, c, :] for c in xc], D, [], XS, None)
    for c in xc:
        m = dve.done(dve.after(m, m_f).scalar_tensor_tensor(out=X[:, c, :], in0=X[:, c, :], scalar=XS[:, c:c + 1], in1=fg,
                                                            op0=ALU.mult, op1=ALU.mult))
    fence(mx)

    fence(m_mod)
    at[0] = 0
    smat[0] = 0
    HT = take(8 * 512).rearrange("p (c t) -> p c t", c=8)
    base = at[0]
    H = take(4 * D).rearrange("p (c d) -> p c d", c=4)
    junk = take(D)
    rs = small(8)
    marks = modulated(H, allc, 0, 2, junk, rs)
    tm = turn_all(HT, H, allc, marks)
    at[0] = base
    fence(*tm)
    BT = take(4 * 512).rearrange("p (g t) -> p g t", g=4)
    CTt = take(4 * 256).rearrange("p (g t) -> p g t", g=4)
    XH = take(4 * 1536).rearrange("p (c n) -> p c n", c=4)
    BK = take(4 * 512).rearrange("p (c n) -> p c n", c=4)
    HS = [take(1536) for _ in range(2)]
    XW = take(1536)
    XW2 = take(1536)
    cv = [XW[:, 0:512], XW[:, 512:1024], XW[:, 1024:1536], take(512)]
    Y2 = XH[:, 2:4, :]
    b = ps.take()
    pe.after(w_cv)
    m = pe.done(nc.tensor.transpose(b.ap[:, 0:80], cwr[0:80, :], ident[0:80, 0:80]))
    m_cw = dve.done(dve.after(m).tensor_copy(cw, b.ap[:, 0:80]))
    b.free(m_cw)
    w, mw, k = ring.take(("dt", 0))
    b = ps.take()
    pe.after(mw)
    for c in allc:
        for k8 in range(8):
            last = mm(b.ap[:, c * 48:c * 48 + 48], HT[:, k8, c * P:(c + 1) * P], w[:, k8, 0:48], k8 == 0, k8 == 7)
    m = pe.done(last)
    ring.free(k, m)
    DT, U, DA, AC, NA, EA, WS, ET = (small(192) for _ in range(8))
    v4 = lambda a: a.rearrange("p (c n) -> p c n", c=4)
    m = dve.done(dve.after(m).tensor_tensor(v4(DT), v4(b.ap[:, 0:192]), dtb.unsqueeze(1).to_broadcast([P, 4, 48]), ALU.add))
    b.free(m)
    dve.done(dve.after().tensor_scalar(U, DT, -1.0, None, ALU.mult))
    m = dve.done(dve.after().tensor_tensor(U, DT, U, ALU.min))
    m = act.done(act.after(m).activation(U, U, ACT.Exp))
    m = act.done(act.after(m).activation(U, U, ACT.Ln, bias=1.0))
    m = act.done(act.after(m).activation(alog, alog, ACT.Exp))
    dve.done(dve.after(m).tensor_scalar(DT, DT, 0.0, None, ALU.max))
    dve.done(dve.after().tensor_tensor(DT, DT, U, ALU.add))
    dve.done(dve.after().tensor_scalar(alog, alog, -1.0, None, ALU.mult))
    m_da = dve.done(dve.after().tensor_tensor(v4(DA), v4(DT), alog.unsqueeze(1).to_broadcast([P, 4, 48]), ALU.mult))

    def chunk_sums():
        b = ps.take()
        pe.after(m_da)
        for d in range(2):
            tri = KC[:, (C_LE, C_GE)[d]:(C_LE, C_GE)[d] + P]
            mm(v4(b.ap[:, 0:192])[:, :, 24 * d:24 * d + 24], tri, v4(DA)[:, :, 24 * d:24 * d + 24], True, True)
        m = pe.done(mm(b.ap[:, 192:384], ones[:, :], DA, True, True))
        m = dve.done(dve.after(m).tensor_copy(AC, b.ap[:, 0:192]))
        m = dve.done(dve.after().tensor_tensor(WS, b.ap[:, 192:384], AC, ALU.subtract))
        m = act.done(act.after(m).activation(ET, b.ap[:, 192:384], ACT.Exp))
        b.free(m)
        m = act.done(act.after(m).activation(WS, WS, ACT.Exp))
        m = act.done(act.after(m).activation(EA, AC, ACT.Exp))
        dve.done(dve.after(m).tensor_tensor(WS, WS, DT, ALU.mult))
        m_s = dve.done(dve.after().tensor_scalar(NA, AC, -1.0, None, ALU.mult))

    cvd, cvt = {}, {}

    def convolve(ch):
        T = 512 if ch < 16 else 256
        if ch % 4 == 0:
            got["w"] = ring.take(("xbc", ch // 4))
        w, mw, k = got["w"]
        b, m = project_T(w, [mw], ch % 4, HT, 0, T)
        if ch % 4 == 3:
            ring.free(k, m)
        a = cv[ch % 4]
        m = act.done(act.apart(m, m_cw, cvt.get(ch - 4), cvd.get(ch - 4)).activation(
            a[:, 0:T], b.ap[:, 0:T], ACT.Identity, bias=cw[:, 60 + ch:61 + ch], scale=cw[:, 20 + ch:21 + ch]))
        rows = [(a[:, 0:256].rearrange("p (r t) -> p r t", r=4), b.ap[:, 0:256].rearrange("p (r t) -> p r t", r=4), 64)]
        if T == 512:
            rows.append((a[:, 256:512].rearrange("p (r t) -> p r t", r=1),
                         b.ap[:, 256:512].rearrange("p (r t) -> p r t", r=1), 256))
        for av, bv, L in rows:
            m3 = dve.done(dve.apart(m).scalar_tensor_tensor(out=av[:, :, 1:L], in0=bv[:, :, 0:L - 1], scalar=cw[:, ch:ch + 1],
                                                       in1=av[:, :, 1:L], op0=ALU.mult, op1=ALU.add))
            m2 = dve.done(dve.apart(m3).scalar_tensor_tensor(out=av[:, :, 0:L - 1], in0=bv[:, :, 1:L],
                                                           scalar=cw[:, 40 + ch:41 + ch], in1=av[:, :, 0:L - 1],
                                                           op0=ALU.mult, op1=ALU.add))
        b.free(m2)
        cvd[ch] = m2

    def conv_act(ch):
        T = 512 if ch < 16 else 256
        a = cv[ch % 4]
        dst = a if ch < 12 else BT[:, ch - 12, :] if ch < 16 else CTt[:, ch - 16, :]
        cvt[ch] = cvd[ch] = act.done(act.apart(cvd[ch]).activation(dst[:, 0:T], a[:, 0:T], ACT.Silu))

    def conv_turn(ch):
        if ch >= 16:
            return
        src = cv[ch % 4] if ch < 12 else BT[:, ch - 12, :]
        b = ps.take()
        pe.after(cvd[ch])
        for c in allc:
            last = nc.tensor.transpose(b.ap[:, c * P:(c + 1) * P], src[:, c * P:(c + 1) * P], ident)
        cvt[ch] = m = pe.done(last)
        d2 = XH[:, :, ch * P:(ch + 1) * P] if ch < 12 else BK[:, :, (ch - 12) * P:(ch - 11) * P]
        m = evac(d2, b.ap.rearrange("p (c t) -> p c t", c=4), m)
        b.free(m)

    staggered(20, convolve, conv_act, conv_turn, lambda ch: chunk_sums() if ch == 0 else None)
    fence()

    def heads(a):
        return a.rearrange("p (h d) -> p h d", d=64)

    def four(b):
        return b.ap.rearrange("p (g n) -> p g n", g=4)[:, :, 0:384].rearrange("p g (h d) -> p g h d", d=64)

    def g6(a):
        return a.rearrange("p (g h d) -> p g h d", g=4, d=64)

    def s6(a, c, d):
        return a[:, c * 48 + d * 24:c * 48 + d * 24 + 24].rearrange("p (g h) -> p g h", g=4).unsqueeze(3).to_broadcast([P, 4, 6, 64])

    turn_of, xw_free, hs_m, y_m = [0], [None, None], {}, {}

    def advance(d, c, first):
        i = turn_of[0]
        turn_of[0] = 1 - i
        xw = (XW, XW2)[i]
        m = dve.done(dve.apart(xw_free[i]).tensor_tensor(
            heads(xw), heads(XH[:, c, :]),
            WS[:, c * 48 + d * 24:c * 48 + d * 24 + 24].unsqueeze(2).to_broadcast([P, 24, 64]), ALU.mult))
        b = ps.take(4)
        pe.after(m)
        for g in range(4):
            last = mm(b.ap[:, g * 512:g * 512 + 384], BK[:, c, g * P:(g + 1) * P], xw[:, g * 384:(g + 1) * 384], True, True)
        m_p = xw_free[i] = pe.done(last)
        ms = []
        for g in range(4):
            hs = HS[d][:, g * 384:(g + 1) * 384]
            if first:
                m = dve.done(dve.apart(m_p).tensor_copy(hs, b.ap[:, g * 512:g * 512 + 384]))
            else:
                e6 = ET[:, c * 48 + d * 24 + 6 * g:c * 48 + d * 24 + 6 * g + 6].unsqueeze(2).to_broadcast([P, 6, 64])
                ms.append(dve.done(dve.apart(m_p, hs_m[d]).tensor_tensor(heads(hs), heads(hs), e6, ALU.mult)))
        for g in range(0 if first else 4):
            hs = HS[d][:, g * 384:(g + 1) * 384]
            m = dve.done(dve.apart(ms[g]).tensor_tensor(hs, hs, b.ap[:, g * 512:g * 512 + 384], ALU.add))
        hs_m[d] = m
        b.free(m)

    def from_state(d, c, first):
        b = ps.take(4)
        pe.after(hs_m[d])
        for g in range(4):
            last = mm(b.ap[:, g * 512:g * 512 + 384], CTt[:, g, c * P:(c + 1) * P], HS[d][:, g * 384:(g + 1) * 384], True, True)
        m_p = pe.done(last)
        for g in range(4):
            e6 = EA[:, c * 48 + d * 24 + 6 * g:c * 48 + d * 24 + 6 * g + 6].unsqueeze(2).to_broadcast([P, 6, 64])
            y = Y2[:, c, g * 384:(g + 1) * 384]
            if first:
                m = dve.done(dve.apart(m_p).tensor_tensor(heads(y), heads(b.ap[:, g * 512:g * 512 + 384]), e6, ALU.mult))
            else:
                t = cv[3][:, 0:384]
                m = dve.done(dve.after(m_p).tensor_tensor(heads(t), heads(b.ap[:, g * 512:g * 512 + 384]), e6, ALU.mult))
                m = dve.done(dve.after(m).tensor_tensor(y, y, t, ALU.add))
        b.free(m)

    advance(0, 2, True)
    advance(1, 3, True)
    advance(0, 3, False)
    advance(1, 2, False)
    fence()
    from_state(0, 0, True)
    from_state(1, 1, True)
    advance(0, 0, False)
    advance(1, 1, False)
    from_state(0, 1, False)
    from_state(1, 0, False)
    fence()
    CB = XW[:, 0:512]
    Dd = [XW[:, 512:1024], XW[:, 1024:1536], HS[0][:, 512:1024]]
    WW = [HS[0][:, 0:256], HS[0][:, 256:512], HS[0][:, 1024:1280]]
    xd = HS[1]
    for c in range(2):
        b = ps.take()
        pe.after(dve.mark())
        for g in range(4):
            last = mm(b.ap[:, g * P:(g + 1) * P], BT[:, g, c * P:(c + 1) * P], CTt[:, g, c * P:(c + 1) * P], True, True)
        m = pe.done(last)
        m = dve.done(dve.after(m).tensor_copy(CB, b.ap))
        b.free(m)
        m = dve.done(dve.after(m).tensor_tensor(heads(xd), heads(XH[:, c, :]), dsk.unsqueeze(2).to_broadcast([P, 24, 64]), ALU.mult))
        m = dve.done(dve.after(m).tensor_tensor(Y2[:, c, :], Y2[:, c, :], xd, ALU.add))
        got, obs = {}, {}

        def decays(u):
            b = ps.take()
            for hh in range(2):
                for d in range(2):
                    o = b.ap[:, (hh * 2 + d) * P:(hh * 2 + d + 1) * P]
                    col = c * 48 + d * 24 + 2 * u + hh
                    mm(o, DA[:, col:col + 1].to_broadcast([P, P]), KC[:, (C_LE, C_GE)[d]:(C_LE, C_GE)[d] + P], True, False)
                    last = mm(o, ident, KC[:, (C_NF, C_NB)[d]:(C_NF, C_NB)[d] + P], False, True)
            m = pe.done(last)
            dd = Dd[u % 3]
            act.after(m, got.get(("w", u - 3)))
            for hh in range(2):
                for d in range(2):
                    col = c * 48 + d * 24 + 2 * u + hh
                    sl = slice((hh * 2 + d) * P, (hh * 2 + d + 1) * P)
                    m = act.done(nc.scalar.activation(dd[:, sl], b.ap[:, sl], ACT.Exp, bias=NA[:, col:col + 1]))
            b.free(m)
            got["d", u] = m

        def weigh(u):
            dd, ww = Dd[u % 3], WW[u % 3]
            dve.apart(got["d", u], got.get(("y", u - 3)))
            m_ww = []
            for hh in range(2):
                cf = c * 48 + 2 * u + hh
                wv = ww[:, hh * P:(hh + 1) * P]
                m_ww.append(dve.done(dve.eng.tensor_scalar(wv, dd[:, hh * 256:hh * 256 + P], DT[:, cf:cf + 1], None, ALU.mult)))
            for hh in range(2):
                cf = c * 48 + 2 * u + hh
                wv = ww[:, hh * P:(hh + 1) * P]
                dve.done(dve.apart(m_ww[hh]).scalar_tensor_tensor(out=wv, in0=dd[:, hh * 256 + P:hh * 256 + 256],
                                                          scalar=DT[:, cf + 24:cf + 25], in1=wv, op0=ALU.mult, op1=ALU.add))
            w2_ = ww.rearrange("p (a b) -> p a b", a=2)
            got["w", u] = dve.done(dve.after().tensor_tensor(
                w2_, w2_, CB[:, (u // 3) * P:(u // 3 + 1) * P].unsqueeze(1).to_broadcast([P, 2, P]), ALU.mult))

        def products(u):
            g = u // 3
            if u % 3 == 0:
                obs[g] = ps.take()
            pe.after(got["w", u])
            for hh in range(2):
                h = 2 * u + hh
                last = mm(obs[g].ap[:, (h % 6) * 64:(h % 6 + 1) * 64], WW[u % 3][:, hh * P:(hh + 1) * P],
                          XH[:, c, h * 64:(h + 1) * 64], True, True)
            got["y", u] = m = pe.done(last)
            if u % 3 == 2:
                y = Y2[:, c, g * 384:(g + 1) * 384]
                m = dve.done(dve.after(m).tensor_tensor(y, y, obs[g].ap[:, 0:384], ALU.add))
                obs[g].free(m)

        staggered(12, decays, weigh, lambda u: None, products)
    smat[0] = 0
    at[0] = base
    fence()
    take(2048 + 1024 + 2 * 1536)
    take(2 * 1536)
    at3 = at[0]
    at[0] = base
    YT = take(12 * 256).rearrange("p (c t) -> p c t", c=12)
    at[0] = at3
    zz = [take(512) for _ in range(2)]
    sn = take(1536)
    m_sn = broadcast_load(sn, I["ssd_norm_2"][0], 1536)
    for n in range(3):
        w, mw, k = ring.take(("z", n))
        for c in range(2):
            b, m = project(w, [mw], HT, c)
            last = m
            m = act.done(act.after(m, dve.mark()).activation(zz[c], b.ap, ACT.Silu))
            b.free(m)
            y = Y2[:, c, n * 512:n * 512 + 512]
            m = dve.done(dve.after(m).tensor_tensor(y, y, zz[c], ALU.mult))
        ring.free(k, last)
    rs = small(8)
    junk = take(1536)
    m = rstd_of([Y2[:, c, :] for c in range(2)], 1536, [m], rs, junk)
    for c in range(2):
        m = dve.done(dve.after(m, m_sn).scalar_tensor_tensor(out=Y2[:, c, :], in0=Y2[:, c, :], scalar=rs[:, c:c + 1], in1=sn,
                                                             op0=ALU.mult, op1=ALU.mult))
    tm = turn_all(YT, Y2, [0, 1], {0: m, 1: m}, n=12)
    at[0] = base + 12 * 256
    fence(*tm)
    SB = take(2 * D).rearrange("p (c n) -> p c n", c=2)
    FBR = take(2 * D).rearrange("p (c n) -> p c n", c=2)
    UF = take(2 * 512).rearrange("p (c n) -> p c n", c=2)
    V1 = take(4 * 512).rearrange("p (g n) -> p g n", g=4)
    FT = take(4 * 256).rearrange("p (g t) -> p g t", g=4)
    dft = take(1280)
    bgt = take(2 * D)[0:1, :]
    m_df = w_s.sent(nc.gpsimd.dma_start(dft, I["consts"][:, C_DL:C_DL + 1280]))
    m_df = w_s.sent(nc.gpsimd.dma_start(bgt, I["b_gate_2"][0].rearrange("a b -> (a b)").rearrange("(a b) -> a b", a=1)))
    for h in range(2):
        w, mw, k = ring.take(("sso", 0, h))
        w_, mw_, k_ = ring.take(("sso", 1, h))
        for c in range(2):
            b = ps.take()
            pe.after(mw, mw_)
            for kk_ in range(12):
                last = mm(b.ap, YT[:, kk_, c * P:(c + 1) * P], w[:, kk_, :] if kk_ < 8 else w_[:, kk_ - 8, :], kk_ == 0, kk_ == 11)
            m = pe.done(last)
            last = m
            m = evac(SB[:, c, h * 512:h * 512 + 512], b.ap, m)
            b.free(m)
        ring.free(k, last)
        ring.free(k_, last)
    w, mw, k = ring.take(("uf", 0))
    um = []
    for c in range(2):
        b, m = project(w, [mw], HT, c)
        last = m
        m = evac(UF[:, c, :], b.ap, m)
        um.append(m)
        b.free(m)
    ring.free(k, last)
    vm = []
    for g in range(4):
        b = ps.take()
        pe.after(m_df, *um)
        for c in range(2):
            last = mm(b.ap, UF[:, c, g * P:(g + 1) * P], dft[:, c * 512:c * 512 + 512], c == 0, c == 1)
        m = pe.done(last)
        m = evac(V1[:, g, :], b.ap, m)
        vm.append(m)
        b.free(m)
    fmk = []
    for g in range(4):
        b = ps.take()
        pe.after(*vm)
        for c in range(2):
            last = mm(b.ap[:, 0:256], dft[:, 1024 + c * P:1024 + (c + 1) * P], V1[:, g, c * 256:c * 256 + 256], c == 0, c == 1)
        m = pe.done(last)
        m = evac(FT[:, g, :], b.ap[:, 0:256], m)
        fmk.append(m)
        b.free(m)
    for h in range(2):
        w, mw, k = ring.take(("four", h))
        for c in range(2):
            b, m = project(w, [mw] + fmk, FT, c, K=4)
            last = m
            m = evac(FBR[:, c, h * 512:h * 512 + 512], b.ap, m)
            b.free(m)
        ring.free(k, last)
    fence()
    gt2 = [V1[:, 0, :], V1[:, 1, :]]
    MG = FBR
    for n in (0, 2, 1, 3):
        w, mw, k = ring.take(("gate", n))
        for c in range(2):
            b = ps.take()
            pe.after(mw)
            mm(b.ap, ones[0:1, :], bgt[:, n * 512:n * 512 + 512], True, False)
            for k8 in range(8):
                last = mm(b.ap, HT[:, k8, c * P:(c + 1) * P], w[:, k8, :], False, k8 == 7)
            m = pe.done(last)
            last = m
            m = act.done(act.after(m, dve.mark()).activation(gt2[c], b.ap, ACT.Sigmoid))
            b.free(m)
            sl = slice((n % 2) * 512, (n % 2) * 512 + 512)
            src = (FBR, SB)[n // 2][:, c, sl]
            m = dve.done(dve.after(m).tensor_tensor(src, src, gt2[c], ALU.mult))
            if n >= 2:
                m = dve.done(dve.after(m).tensor_tensor(FBR[:, c, sl], FBR[:, c, sl], src, ALU.add))
        ring.free(k, last)
    MT = YT[:, 0:8, :]
    tm = turn_all(MT, MG, [0, 1], {0: m, 1: m})
    mixed = []
    for h in range(2):
        w, mw, k = ring.take(("wout", h))
        for c in range(2):
            b, m = project(w, [mw] + tm, MT, c)
            last = m
            m = evac(SB[:, c, h * 512:h * 512 + 512], b.ap, m)
            mixed.append(m)
            b.free(m)
        ring.free(k, last)

    def add_normed(src, row, marks, junk, rs):
        m = rstd_of([src[:, c, :] for c in range(2)], D, marks, rs, junk)
        g, mg = spread(row)
        for c in range(2):
            m = dve.done(dve.after(m, mg).scalar_tensor_tensor(out=src[:, c, :], in0=src[:, c, :], scalar=rs[:, c:c + 1],
                                                               in1=g.ap, op0=ALU.mult, op1=ALU.mult))
            m = dve.done(dve.after(m).tensor_tensor(X[:, c, :], X[:, c, :], src[:, c, :], ALU.add))
            if row == 4:
                square(c, m)
            else:
                act.after(m)
                mo = w_o.sent(nc.scalar.dma_start(out[0, c * P:(c + 1) * P, :], X[:, c, :]))
        g.free(m)
        return mo if row == 10 else None

    fence()
    add_normed(SB, 4, mixed, V1.rearrange("p g n -> p (g n)")[:, 0:D], rs)
    at[0] = 0
    smat[0] = 0
    marks = fence()
    rs, rw = small(8), small(8 * 16)
    w_r = w_s.sent(nc.gpsimd.dma_start(rw.rearrange("p (c e) -> p c e", c=8),
                                       I["w_router_2"][0].rearrange("(c p) e -> p c e", p=P)))
    XE = take(8 * 512).rearrange("p (c s) -> p c s", c=8)
    SWT = take(4 * 256).rearrange("p (g t) -> p g t", g=4)
    YEf = take(4 * D)
    YE = YEf.rearrange("p (g n) -> p g n", g=4)
    arena["words"] -= SLOT
    top = arena["words"]
    ring.widen([arena["f"][:, top:top + SLOT]], [YEf], *marks)
    base2 = at[0]
    H = take(2 * D).rearrange("p (c d) -> p c d", c=2)
    HT2 = take(8 * 256).rearrange("p (c t) -> p c t", c=8)
    junk = take(D)
    SS = take(2 * 512).rearrange("p (c e s) -> p c e s", c=2, e=16)
    SW = take(2 * 512).rearrange("p (c e s) -> p c e s", c=2, e=16)
    m16 = take(1024)
    marks = modulated(H, xc, 6, 8, None, XS)
    tm = turn_all(HT2, H, xc, marks)
    b = ps.take()
    pe.after(w_r, *tm)
    for c in xc:
        for k in range(8):
            last = mm(b.ap[:, c * 16:c * 16 + 16], HT2[:, k, c * P:(c + 1) * P],
                      rw.rearrange("p (c e) -> p c e", c=8)[:, k, :], k == 0, k == 7)
    m = pe.done(last)
    af, rm = small(32), small(2)
    a3 = af.rearrange("p (c e) -> p c e", c=2)
    m = dve.done(dve.after(m).tensor_copy(af, b.ap[:, 0:32]))
    b.free(m)
    dve.done(dve.after().tensor_reduce(rm, a3, AX.X, ALU.max))
    m = dve.done(dve.after().tensor_tensor(a3, a3, rm.unsqueeze(2).to_broadcast([P, 2, 16]), ALU.subtract))
    m = act.done(act.after(m).activation(af, af, ACT.Exp))
    dve.done(dve.after(m).tensor_reduce(rm, a3, AX.X, ALU.add))
    dve.done(dve.after().reciprocal(rm, rm))
    m = dve.done(dve.after().tensor_tensor(a3, a3, rm.unsqueeze(2).to_broadcast([P, 2, 16]), ALU.mult))
    b = ps.take()
    pe.after(m)
    for c in xc:
        last = nc.tensor.transpose(b.ap[0:16, c * P:(c + 1) * P], af[:, c * 16:c * 16 + 16], ident)
    m = pe.done(last)
    wk_, pz, mv = m16[0:16, 0:256], m16[0:16, 256:512], m16[0:16, 512:520]
    m = dve.done(dve.after(m).tensor_copy(wk_, b.ap[0:16, 0:256]))
    b.free(m)
    for r in range(4):
        dve.done(dve.after().max(mv, wk_))
        m = dve.done(dve.after().match_replace(wk_, mv, wk_, -1.0))
    dve.done(dve.after().tensor_scalar(wk_, wk_, 0.0, None, ALU.is_lt))
    dve.done(dve.after().tensor_tensor_scan(pz[:, 0:P], ones[0:16, :], wk_[:, 0:P], 0.0, ALU.mult, ALU.add))
    dve.done(dve.after().tensor_tensor_scan(pz[:, P:256], ones[0:16, :], wk_[:, P:256], pz[:, P - 1:P], ALU.mult, ALU.add))
    dve.done(dve.after().tensor_tensor(pz, pz, wk_, ALU.mult))
    m = dve.done(dve.after().tensor_scalar(pz, pz, 1.0, None, ALU.subtract))
    b = ps.take()
    pe.after(m)
    for c in xc:
        last = nc.tensor.transpose(b.ap[:, c * 16:c * 16 + 16], pz[:, c * P:(c + 1) * P], ident[0:16, 0:16])
    m = pe.done(last)
    pt = small(32)
    m = dve.done(dve.after(m).tensor_copy(pt, b.ap[:, 0:32]))
    b.free(m)
    for c in xc:
        m = dve.done(dve.after(m).tensor_tensor(
            SS[:, c, :, :], KC[:, C_IOTA:C_IOTA + 32].unsqueeze(1).to_broadcast([P, 16, 32]),
            pt[:, c * 16:c * 16 + 16].unsqueeze(2).to_broadcast([P, 16, 32]), ALU.is_equal))
        m = dve.done(dve.after(m).tensor_tensor(
            SW[:, c, :, :], SS[:, c, :, :], a3[:, c, :].unsqueeze(2).to_broadcast([P, 16, 32]), ALU.mult))
    fence()
    for k in range(8):
        b = ps.take()
        for c in xc:
            last = mm(b.ap, H[:, c, k * P:(k + 1) * P], SS[:, c, :, :].rearrange("p e s -> p (e s)"), c == 0, c == 1)
        m = pe.done(last)
        m = evac(XE[:, k, :], b.ap, m)
        b.free(m)
    for c in xc:
        turned(SWT[:, :, c * P:(c + 1) * P], SW[:, c, :, :].rearrange("p e s -> p (e s)"), 4, None)
    at[0] = base2
    fence()
    hid = [take(D) for _ in range(2)]
    hidT = [take(D).rearrange("p (c s) -> p c s", c=8) for _ in range(2)]
    F2 = take(2 * D).rearrange("p (c n) -> p c n", c=2)
    fb = [ps.take(), ps.take(), ps.take(), ps.take()]
    for g in range(4):
        i = g % 2
        hm_ = []
        for h in range(2):
            sl = slice(h * 512, h * 512 + 512)
            bg, bu = ps.take(), ps.take()
            for j in range(4):
                e = 4 * g + j
                for mt, bb in (("g", bg), ("u", bu)):
                    w, mw, k = ring.take((2, e, mt, h))
                    pe.after(mw)
                    for c in range(8):
                        last = mm(bb.ap[32 * j:32 * j + 32, :], XE[:, c, e * 32:e * 32 + 32], w[:, c, :], c == 0, c == 7)
                    m = pe.done(last)
                    ring.free(k, m)
            m_u = m
            m = act.done(act.after(m).activation(hid[i][:, sl], bg.ap, ACT.Silu))
            bg.free(m)
            m = dve.done(dve.after(m, m_u).tensor_tensor(hid[i][:, sl], hid[i][:, sl], bu.ap, ALU.mult))
            bu.free(m)
            last_marks.clear()
            turned(hidT[i][:, 4 * h:4 * h + 4, :], hid[i][:, sl], 4, m)
            hm_ += last_marks
        for h in range(2):
            sl = slice(h * 512, h * 512 + 512)
            b = ps.take()
            pe.after(*hm_)
            for j in range(4):
                w, mw, k = ring.take((2, 4 * g + j, "d", h))
                pe.after(mw)
                for c in range(8):
                    last = mm(b.ap[32 * j:32 * j + 32, :], hidT[i][:, c, 32 * j:32 * j + 32], w[:, c, :], c == 0, c == 7)
                m = pe.done(last)
                ring.free(k, m)
            m = evac(YE[:, g, sl], b.ap, m)
            b.free(m)
            pe.after(m)
            for c in xc:
                last = mm(fb[2 * h + c].ap, SWT[:, g, c * P:(c + 1) * P], YE[:, g, sl], g == 0, g == 3)
    m = pe.done(last)
    fm_ = []
    for c in xc:
        for h in range(2):
            fm_.append(evac(F2[:, c, h * 512:h * 512 + 512], fb[2 * h + c].ap, m))
            fb[2 * h + c].free(fm_[-1])
    act.after(add_normed(F2, 10, fm_, hid[0], rs))
    arena["stack"].close()
    arena["base"].close()
    ctx.close()


_INS = ['x', 'c', 'ctx', 'c_ctx', 'ada_w', 'ada_b', 'norm_mix_g', 'norm_ffn_g', 'even_w_in', 'even_w_out',
        'hgrn_lb_logits', 'hgrn_onorm_g', 'diff_lambda', 'diff_subln_g', 'odd_w_qkv', 'odd_w_out', 'swa_sink',
        'router_w', 'router_b', 'moe_w_gate', 'moe_w_up', 'moe_w_down', 'final_norm_g', 'c_2', 'ctx_2', 'c_ctx_2',
        'w_mod_2', 'b_mod_2', 'norm_mix_pre_2', 'norm_mix_post_2', 'norm_ffn_pre_2', 'norm_ffn_post_2', 'w_in_2',
        'conv_w_2', 'conv_b_2', 'dt_bias_2', 'a_log_2', 'd_skip_2', 'ssd_norm_2', 'w_fourier_2', 'w_ssd_out_2',
        'b_gate_2', 'w_out_2', 'w_router_2', 'w_e_gate_2', 'w_e_up_2', 'w_e_down_2']


def kernel(**inputs):
    import concourse.bacc as _bacc
    from concourse.bass_utils import run_bass_kernel_spmd as _run

    nc = _bacc.Bacc("TRN2", target_bir_lowering=False, num_devices=1)
    arrays, ins = {}, {}
    for name in _INS + ["consts"]:
        a = constants() if name == "consts" else np.ascontiguousarray(inputs[name])
        arrays[f"in_{name}"] = a
        ins[name] = nc.dram_tensor(f"in_{name}", a.shape, F32, kind="ExternalInput").ap()
    out = nc.dram_tensor("out_0", (1, 256, 1024), F32, kind="ExternalOutput").ap()
    program(nc, ins, out)
    r = _run(nc, [arrays], core_ids=[0])
    return r.results[0]["out_0"]
```
